# Optimizing a Trainium2 kernel written in Bass

```python
import math
import jax, jax.numpy as jnp
from jax import lax
import numpy as np

D_MODEL = 1024
BATCH = 1
SEQ = 256
DEPTH = 2

GRID_W = 64
CTX_LEN = 256
Q_BLOCK = 128
EPS = 1e-6
ROPE_BASE = 10000.0

DIFF_HEADS = 4
DIFF_DIM = 64
DIFF_VDIM = 2 * DIFF_DIM

MLSTM_HEADS = 4
MLSTM_DIM = 128
MLSTM_CHUNK = 64
MLSTM_CONV = 3

GQA_HEADS = 8
GQA_KV_HEADS = 2
GQA_DIM = 64

HYENA_CH = 512
HYENA_ORDER = 2
HYENA_CONV = 3
FILTER_BANDS = 16
FILTER_EMB = 2 * FILTER_BANDS + 1
FILTER_HIDDEN = 64
FILTER_SHIFT = 0.05
DECAY_TARGET = 1e-2
FAST_DECAY_PCT = 0.3
SLOW_DECAY_PCT = 1.5

N_BRANCH = 4
BRANCH_W = 512

MOE_GROUPS = 4
MOE_EXPERTS_PER_GROUP = 8
MOE_EXPERTS = MOE_GROUPS * MOE_EXPERTS_PER_GROUP
MOE_TOP_K = 2
EXPERT_HIDDEN = 512
MOE_BLOCK = 128

kernel_name = 'hybrid_diff_mlstm_gqa_hyena_hmoe_dit'

def in_sizes():
    return (DIFF_HEADS * 2 * DIFF_DIM,
            DIFF_HEADS * 2 * DIFF_DIM,
            DIFF_HEADS * DIFF_VDIM,
            3 * MLSTM_HEADS * MLSTM_DIM,
            MLSTM_HEADS * MLSTM_DIM,
            4 * MLSTM_HEADS,
            GQA_HEADS * GQA_DIM,
            2 * GQA_KV_HEADS * GQA_DIM,
            (HYENA_ORDER + 1) * HYENA_CH,
            N_BRANCH * D_MODEL)

def split_cols(p):
    idx = np.cumsum(in_sizes())[:-1].tolist()
    return jnp.split(p, idx, axis=-1)

def rmsnorm(x, g):
    xf = x.astype(jnp.float32)
    y = xf * lax.rsqrt(jnp.mean(xf * xf, axis=-1, keepdims=True) + EPS)
    return y.astype(x.dtype) * g

def modulate(h, shift, scale):
    return h * (1 + scale) + shift

def axial_rope_tables(n_tok, dim):
    rows = n_tok // GRID_W
    row = jnp.repeat(jnp.arange(rows, dtype=jnp.float32), GRID_W)
    col = jnp.broadcast_to(jnp.arange(GRID_W, dtype=jnp.float32), (rows, GRID_W)).reshape(-1)
    n_freq = dim // 4
    inv = ROPE_BASE ** (-jnp.arange(n_freq, dtype=jnp.float32) / n_freq)
    ar = row[:, None] * inv
    ac = col[:, None] * inv
    ang = jnp.concatenate([ar, ar, ac, ac], axis=-1)
    return jnp.cos(ang), jnp.sin(ang)

def apply_rope(x, cos, sin):
    r1, r2, c1, c2 = jnp.split(x, 4, axis=-1)
    rot = jnp.concatenate([-r2, r1, -c2, c1], axis=-1)
    shape = (x.shape[1],) + (1,) * (x.ndim - 3) + (x.shape[-1],)
    return x * cos.reshape(shape).astype(x.dtype) + rot * sin.reshape(shape).astype(x.dtype)

def sweep_blocks(fn, q):
    b, t = q.shape[:2]
    nb = t // Q_BLOCK
    qb = jnp.swapaxes(q.reshape((b, nb, Q_BLOCK) + q.shape[2:]), 0, 1)
    out = jnp.swapaxes(lax.map(fn, qb), 0, 1)
    return out.reshape((b, t) + out.shape[3:])

def short_conv(x, w, bias):
    k, ch = w.shape
    y = lax.conv_general_dilated(x, w[:, None, :].astype(x.dtype), window_strides=(1,),
                                 padding=((k // 2, k // 2),), dimension_numbers=('NWC', 'WIO', 'NWC'),
                                 feature_group_count=ch)
    return y + bias

def diff_attention(q_c, k_c, v_c, q_l, k_l, v_l, lam_p, norm_g, layer, rope, need_ctx):
    lam_init = 0.8 - 0.6 * math.exp(-0.3 * layer)
    lam_p = lam_p.astype(jnp.float32)
    lam = jnp.exp(jnp.sum(lam_p[0] * lam_p[1])) - jnp.exp(jnp.sum(lam_p[2] * lam_p[3])) + lam_init
    scale = DIFF_DIM ** -0.5

    def heads(q, k, v):
        b, t = q.shape[:2]
        return (q.reshape(b, t, DIFF_HEADS, 2, DIFF_DIM), k.reshape(b, t, DIFF_HEADS, 2, DIFF_DIM),
                v.reshape(b, t, DIFF_HEADS, DIFF_VDIM))

    def attend(q, k, v):
        def block(qb):
            s = jnp.einsum('bqhcd,bkhcd->bhcqk', qb, k).astype(jnp.float32) * scale
            p = jax.nn.softmax(s, axis=-1)
            pd = p[:, :, 0] - lam * p[:, :, 1]
            return jnp.einsum('bhqk,bkhe->bqhe', pd.astype(v.dtype), v)
        o = rmsnorm(sweep_blocks(block, q), norm_g) * (1.0 - lam_init)
        return o.reshape(o.shape[:2] + (DIFF_HEADS * DIFF_VDIM,))

    qc, kc, vc = heads(q_c, k_c, v_c)
    ql, kl, vl = heads(q_l, k_l, v_l)
    cos, sin = rope
    ql = apply_rope(ql, cos, sin)
    kl = apply_rope(kl, cos, sin)
    y_lat = attend(ql, jnp.concatenate([kc, kl], axis=1), jnp.concatenate([vc, vl], axis=1))
    y_ctx = attend(qc, kc, vc) if need_ctx else None
    return y_ctx, y_lat

def gqa_attention(q_c, kv_c, q_l, kv_l, q_g, k_g, rope, need_ctx):
    rep = GQA_HEADS // GQA_KV_HEADS
    scale = GQA_DIM ** -0.5

    def heads(q, kv):
        b, t = q.shape[:2]
        q = rmsnorm(q.reshape(b, t, GQA_KV_HEADS, rep, GQA_DIM), q_g)
        kv = kv.reshape(b, t, 2, GQA_KV_HEADS, GQA_DIM)
        return q, rmsnorm(kv[:, :, 0], k_g), kv[:, :, 1]

    def attend(q, k, v):
        def block(qb):
            s = jnp.einsum('bqgrd,bkgd->bgrqk', qb, k).astype(jnp.float32) * scale
            p = jax.nn.softmax(s, axis=-1)
            return jnp.einsum('bgrqk,bkgd->bqgrd', p.astype(v.dtype), v)
        o = sweep_blocks(block, q)
        return o.reshape(o.shape[:2] + (GQA_HEADS * GQA_DIM,))

    qc, kc, vc = heads(q_c, kv_c)
    ql, kl, vl = heads(q_l, kv_l)
    cos, sin = rope
    ql = apply_rope(ql, cos, sin)
    kl = apply_rope(kl, cos, sin)
    y_lat = attend(ql, jnp.concatenate([kc, kl], axis=1), jnp.concatenate([vc, vl], axis=1))
    y_ctx = attend(qc, kc, vc) if need_ctx else None
    return y_ctx, y_lat

def mlstm_scan(q, k, v, log_i, log_f, state):
    b, t, h, d = q.shape
    nc = t // MLSTM_CHUNK

    def chunks(a):
        a = a.astype(jnp.float32).reshape((b, nc, MLSTM_CHUNK) + a.shape[2:])
        return jnp.swapaxes(jnp.moveaxis(a, 1, 0), 2, 3)

    causal = jnp.tril(jnp.ones((MLSTM_CHUNK, MLSTM_CHUNK), dtype=bool))

    def step(carry, inp):
        c_mat, n_vec, m = carry
        qc, kc, vc, li, lf = inp
        bcum = jnp.cumsum(lf, axis=-1)
        dmat = jnp.where(causal, bcum[..., :, None] - bcum[..., None, :] + li[..., None, :], -jnp.inf)
        inter = bcum + m[..., None]
        m_t = jnp.maximum(inter, jnp.max(dmat, axis=-1))
        w_intra = jnp.exp(dmat - m_t[..., None])
        w_inter = jnp.exp(inter - m_t)
        s = jnp.einsum('bhtd,bhsd->bhts', qc, kc) * w_intra
        num = jnp.einsum('bhts,bhse->bhte', s, vc) + w_inter[..., None] * jnp.einsum('bhtd,bhde->bhte', qc, c_mat)
        den = jnp.sum(s, axis=-1) + w_inter * jnp.einsum('bhtd,bhd->bht', qc, n_vec)
        h_out = num / jnp.maximum(jnp.abs(den), jnp.exp(-m_t))[..., None]
        b_last = bcum[..., -1]
        g = b_last[..., None] - bcum + li
        m_new = jnp.maximum(b_last + m, jnp.max(g, axis=-1))
        kw = kc * jnp.exp(g - m_new[..., None])[..., None]
        wc = jnp.exp(b_last + m - m_new)
        c_new = wc[..., None, None] * c_mat + jnp.einsum('bhsd,bhse->bhde', kw, vc)
        n_new = wc[..., None] * n_vec + jnp.sum(kw, axis=2)
        return (c_new, n_new, m_new), h_out

    state, hs = lax.scan(step, state, (chunks(q), chunks(k), chunks(v), chunks(log_i), chunks(log_f)))
    hs = jnp.moveaxis(jnp.swapaxes(hs, 2, 3), 0, 1).reshape(b, t, h, d)
    return hs.astype(q.dtype), state

def mlstm_branch(qkv_c, o_c, g_c, qkv_l, o_l, g_l, conv_w, conv_b, gate_b, norm_g, need_ctx):
    w = MLSTM_HEADS * MLSTM_DIM

    def prep(qkv, g):
        b, t = qkv.shape[:2]
        qk = jax.nn.silu(short_conv(qkv[..., :2 * w], conv_w, conv_b))
        q = qk[..., :w].reshape(b, t, MLSTM_HEADS, MLSTM_DIM)
        k = qk[..., w:].reshape(b, t, MLSTM_HEADS, MLSTM_DIM) * MLSTM_DIM ** -0.5
        v = qkv[..., 2 * w:].reshape(b, t, MLSTM_HEADS, MLSTM_DIM)
        gates = g.reshape(b, t, 2, 2, MLSTM_HEADS).astype(jnp.float32) + gate_b
        return q, k, v, gates

    def flip(a):
        return a[:, ::-1]

    def run(inp, direction, state):
        q, k, v, gates = inp
        log_i = gates[:, :, direction, 0]
        log_f = jax.nn.log_sigmoid(gates[:, :, direction, 1])
        if direction == 1:
            h, st = mlstm_scan(flip(q), flip(k), flip(v), flip(log_i), flip(log_f), state)
            return flip(h), st
        return mlstm_scan(q, k, v, log_i, log_f, state)

    ctx_in = prep(qkv_c, g_c)
    lat_in = prep(qkv_l, g_l)
    b = qkv_l.shape[0]
    zero = (jnp.zeros((b, MLSTM_HEADS, MLSTM_DIM, MLSTM_DIM), jnp.float32),
            jnp.zeros((b, MLSTM_HEADS, MLSTM_DIM), jnp.float32),
            jnp.zeros((b, MLSTM_HEADS), jnp.float32))
    hc_f, st_f = run(ctx_in, 0, zero)
    hc_b, st_b = run(ctx_in, 1, zero)
    hl = run(lat_in, 0, st_f)[0] + run(lat_in, 1, st_b)[0]

    def out(h, o):
        h = rmsnorm(h, norm_g) * jax.nn.sigmoid(o).reshape(h.shape)
        return h.reshape(h.shape[:2] + (w,))

    y_lat = out(hl, o_l)
    y_ctx = out(hc_f + hc_b, o_c) if need_ctx else None
    return y_ctx, y_lat

def hyena_filters(length, w1, b1, w2, b2, w3, freq):
    t = jnp.arange(length, dtype=jnp.float32) / length
    bands = jnp.arange(1, FILTER_BANDS + 1, dtype=jnp.float32)
    ang = 2.0 * math.pi * t[:, None] * bands
    emb = jnp.concatenate([t[:, None], jnp.cos(ang), jnp.sin(ang)], axis=-1)
    a = jnp.sin(freq[0] * (emb @ w1 + b1))
    a = jnp.sin(freq[1] * (a @ w2 + b2))
    filt = (a @ w3).astype(jnp.float32).reshape(length, HYENA_ORDER, 2, HYENA_CH)
    alpha = jnp.linspace(abs(math.log(DECAY_TARGET)) / SLOW_DECAY_PCT,
                         abs(math.log(DECAY_TARGET)) / FAST_DECAY_PCT, HYENA_CH)
    window = jnp.exp(-t[:, None] * alpha) + FILTER_SHIFT
    filt = filt * window[:, None, None, :]
    k = jnp.concatenate([filt[:, :, 0], jnp.zeros((1, HYENA_ORDER, HYENA_CH), jnp.float32),
                         filt[:0:-1, :, 1]], axis=0)
    return k * lax.rsqrt(jnp.sum(k * k, axis=0, keepdims=True) + EPS)

def fft_long_conv(z, k):
    length = z.shape[1]
    zf = jnp.fft.rfft(z.astype(jnp.float32), n=2 * length, axis=1)
    kf = jnp.fft.rfft(k, axis=0)
    y = jnp.fft.irfft(zf * kf[None], n=2 * length, axis=1)[:, :length]
    return y.astype(z.dtype)

def hyena_operator(p, conv_w, conv_b, w1, b1, w2, b2, w3, freq, bias):
    length = p.shape[1]
    u = short_conv(p, conv_w, conv_b)
    parts = jnp.split(u, HYENA_ORDER + 1, axis=-1)
    k = hyena_filters(length, w1, b1, w2, b2, w3, freq)
    z = parts[0]
    for n in range(HYENA_ORDER):
        z = parts[n + 1] * (fft_long_conv(z, k[:, n]) + bias[n] * z)
    return z

def merge_branches(ys, gate_cols, w_branch, w_out):
    y = jnp.stack(ys, axis=2)
    g = jax.nn.sigmoid(gate_cols.reshape(y.shape[:3] + (D_MODEL,)))
    merged = jnp.sum(g * jnp.einsum('btnc,ncd->btnd', y, w_branch), axis=2)
    return merged @ w_out

def hier_moe(h, w_group, b_group, w_router, b_router, w_gate, w_up, w_down):
    n_tok, d = h.shape
    g_logits = (h @ w_group + b_group).astype(jnp.float32)
    grp = jnp.argmax(g_logits, axis=-1)
    p_grp = jnp.max(jax.nn.softmax(g_logits, axis=-1), axis=-1, keepdims=True)
    e_logits = (h @ w_router + b_router).astype(jnp.float32).reshape(n_tok, MOE_GROUPS, MOE_EXPERTS_PER_GROUP)
    e_in = e_logits[jnp.arange(n_tok), grp]
    top_v, top_i = lax.top_k(e_in, MOE_TOP_K)
    gates = p_grp * jax.nn.softmax(top_v, axis=-1)
    e_flat = (grp[:, None] * MOE_EXPERTS_PER_GROUP + top_i).reshape(-1)
    m_slots = n_tok * MOE_TOP_K
    order = jnp.argsort(e_flat)
    e_s = e_flat[order]
    tok_s = order // MOE_TOP_K
    gate_s = gates.reshape(-1)[order]
    counts = jnp.bincount(e_flat, length=MOE_EXPERTS)
    padded = (counts + MOE_BLOCK - 1) // MOE_BLOCK * MOE_BLOCK
    start = jnp.cumsum(counts) - counts
    p_end = jnp.cumsum(padded)
    dest = (p_end - padded)[e_s] + jnp.arange(m_slots) - start[e_s]
    n_blocks = -(-(m_slots + MOE_EXPERTS * (MOE_BLOCK - 1)) // MOE_BLOCK)
    buf_tok = jnp.zeros((n_blocks * MOE_BLOCK,), jnp.int32).at[dest].set(tok_s.astype(jnp.int32))
    blk_exp = jnp.minimum(jnp.searchsorted(p_end, jnp.arange(n_blocks) * MOE_BLOCK, side='right'), MOE_EXPERTS - 1)
    xb = h[buf_tok].reshape(n_blocks, MOE_BLOCK, d)

    def expert_block(args):
        xblk, e = args
        return (jax.nn.silu(xblk @ w_gate[e]) * (xblk @ w_up[e])) @ w_down[e]

    yb = lax.map(expert_block, (xb, blk_exp)).reshape(-1, d)
    y_s = yb[dest] * gate_s[:, None].astype(h.dtype)
    return jnp.zeros_like(h).at[tok_s].add(y_s)

def setup_inputs(seed: int = 0) -> dict:
    key = jax.random.key(seed)
    keys = iter(jax.random.split(key, 48))

    def nrm(shape, scale):
        return scale * jax.random.normal(next(keys), shape, jnp.float32)

    d, L = D_MODEL, DEPTH
    n_in = sum(in_sizes())
    w_ml = MLSTM_HEADS * MLSTM_DIM
    inp = {}
    inp['x'] = nrm((BATCH, SEQ, d), 1.0)
    inp['c'] = nrm((BATCH, d), 1.0)
    inp['ctx'] = nrm((BATCH, CTX_LEN, d), 1.0)
    inp['c_ctx'] = nrm((d,), 1.0)
    inp['w_ada'] = nrm((L, d, 6 * d), 0.5 * d ** -0.5)
    inp['b_ada'] = nrm((L, 6 * d), 0.02)
    inp['norm1_g'] = 1.0 + nrm((L, d), 0.05)
    inp['norm2_g'] = 1.0 + nrm((L, d), 0.05)
    inp['w_in'] = nrm((L, d, n_in), d ** -0.5)
    inp['diff_lam'] = nrm((L, 4, DIFF_DIM), 0.1)
    inp['diff_norm_g'] = 1.0 + nrm((L, DIFF_VDIM), 0.05)
    inp['ml_conv_w'] = nrm((L, MLSTM_CONV, 2 * w_ml), MLSTM_CONV ** -0.5)
    inp['ml_conv_b'] = nrm((L, 2 * w_ml), 0.02)
    i_bias = nrm((L, 2, MLSTM_HEADS), 0.1)
    f_bias = jnp.linspace(3.0, 6.0, MLSTM_HEADS) + nrm((L, 2, MLSTM_HEADS), 0.1)
    inp['ml_gate_b'] = jnp.stack([i_bias, f_bias], axis=2)
    inp['ml_norm_g'] = 1.0 + nrm((L, MLSTM_DIM), 0.05)
    inp['gqa_qnorm_g'] = 1.0 + nrm((L, GQA_DIM), 0.05)
    inp['gqa_knorm_g'] = 1.0 + nrm((L, GQA_DIM), 0.05)
    inp['hy_conv_w'] = nrm((L, HYENA_CONV, (HYENA_ORDER + 1) * HYENA_CH), HYENA_CONV ** -0.5)
    inp['hy_conv_b'] = nrm((L, (HYENA_ORDER + 1) * HYENA_CH), 0.02)
    inp['hy_f_w1'] = nrm((L, FILTER_EMB, FILTER_HIDDEN), FILTER_EMB ** -0.5)
    inp['hy_f_b1'] = nrm((L, FILTER_HIDDEN), 0.1)
    inp['hy_f_w2'] = nrm((L, FILTER_HIDDEN, FILTER_HIDDEN), FILTER_HIDDEN ** -0.5)
    inp['hy_f_b2'] = nrm((L, FILTER_HIDDEN), 0.1)
    inp['hy_f_w3'] = nrm((L, FILTER_HIDDEN, HYENA_ORDER * 2 * HYENA_CH), FILTER_HIDDEN ** -0.5)
    inp['hy_f_freq'] = 1.0 + nrm((L, 2, FILTER_HIDDEN), 0.1)
    inp['hy_bias'] = nrm((L, HYENA_ORDER, HYENA_CH), 0.5)
    inp['w_branch'] = nrm((L, N_BRANCH, BRANCH_W, d), BRANCH_W ** -0.5)
    inp['w_out'] = nrm((L, d, d), d ** -0.5)
    inp['moe_w_group'] = nrm((L, d, MOE_GROUPS), d ** -0.5)
    inp['moe_b_group'] = nrm((L, MOE_GROUPS), 0.01)
    inp['moe_w_router'] = nrm((L, d, MOE_EXPERTS), d ** -0.5)
    inp['moe_b_router'] = nrm((L, MOE_EXPERTS), 0.01)
    inp['moe_w_gate'] = nrm((L, MOE_EXPERTS, d, EXPERT_HIDDEN), d ** -0.5)
    inp['moe_w_up'] = nrm((L, MOE_EXPERTS, d, EXPERT_HIDDEN), d ** -0.5)
    inp['moe_w_down'] = nrm((L, MOE_EXPERTS, EXPERT_HIDDEN, d), EXPERT_HIDDEN ** -0.5)
    inp['final_norm_g'] = 1.0 + nrm((d,), 0.05)
    return inp

def reference(x, c, ctx, c_ctx, w_ada, b_ada, norm1_g, norm2_g, w_in, diff_lam, diff_norm_g,
              ml_conv_w, ml_conv_b, ml_gate_b, ml_norm_g, gqa_qnorm_g, gqa_knorm_g,
              hy_conv_w, hy_conv_b, hy_f_w1, hy_f_b1, hy_f_w2, hy_f_b2, hy_f_w3, hy_f_freq, hy_bias,
              w_branch, w_out, moe_w_group, moe_b_group, moe_w_router, moe_b_router,
              moe_w_gate, moe_w_up, moe_w_down, final_norm_g):
    b, n, d = x.shape
    n_ctx = ctx.shape[1]
    rope_d = axial_rope_tables(n, DIFF_DIM)
    rope_g = axial_rope_tables(n, GQA_DIM)
    sc = jax.nn.silu(c)[:, None, :]
    scx = jax.nn.silu(c_ctx)
    xs, cs = x, ctx
    for l in range(DEPTH):
        need_ctx = l < DEPTH - 1
        mod_l = jnp.split(sc @ w_ada[l] + b_ada[l], 6, axis=-1)
        mod_c = jnp.split(scx @ w_ada[l] + b_ada[l], 6, axis=-1)
        hl = modulate(rmsnorm(xs, norm1_g[l]), mod_l[0], mod_l[1])
        hc = modulate(rmsnorm(cs, norm1_g[l]), mod_c[0], mod_c[1])
        pl = split_cols(hl @ w_in[l])
        pc = split_cols(hc @ w_in[l])
        yc_a, yl_a = diff_attention(pc[0], pc[1], pc[2], pl[0], pl[1], pl[2], diff_lam[l], diff_norm_g[l],
                                    l, rope_d, need_ctx)
        yc_b, yl_b = mlstm_branch(pc[3], pc[4], pc[5], pl[3], pl[4], pl[5], ml_conv_w[l], ml_conv_b[l],
                                  ml_gate_b[l], ml_norm_g[l], need_ctx)
        yc_c, yl_c = gqa_attention(pc[6], pc[7], pl[6], pl[7], gqa_qnorm_g[l], gqa_knorm_g[l], rope_g, need_ctx)
        hy_args = (hy_conv_w[l], hy_conv_b[l], hy_f_w1[l], hy_f_b1[l], hy_f_w2[l], hy_f_b2[l],
                   hy_f_w3[l], hy_f_freq[l], hy_bias[l])
        yl_d = hyena_operator(pl[8], *hy_args)
        xs = xs + mod_l[2] * merge_branches((yl_a, yl_b, yl_c, yl_d), pl[9], w_branch[l], w_out[l])
        hl2 = modulate(rmsnorm(xs, norm2_g[l]), mod_l[3], mod_l[4])
        moe_args = (moe_w_group[l], moe_b_group[l], moe_w_router[l], moe_b_router[l],
                    moe_w_gate[l], moe_w_up[l], moe_w_down[l])
        if need_ctx:
            yc_d = hyena_operator(pc[8], *hy_args)
            cs = cs + mod_c[2] * merge_branches((yc_a, yc_b, yc_c, yc_d), pc[9], w_branch[l], w_out[l])
            hc2 = modulate(rmsnorm(cs, norm2_g[l]), mod_c[3], mod_c[4])
            f = hier_moe(jnp.concatenate([hc2.reshape(-1, d), hl2.reshape(-1, d)], axis=0), *moe_args)
            cs = cs + mod_c[5] * f[:b * n_ctx].reshape(b, n_ctx, d)
            f_lat = f[b * n_ctx:]
        else:
            f_lat = hier_moe(hl2.reshape(-1, d), *moe_args)
        xs = xs + mod_l[5] * f_lat.reshape(b, n, d)
    return rmsnorm(xs, final_norm_g)


_drawn_inputs = setup_inputs


def setup_inputs(seed=0):
    import zlib

    import numpy as np

    out = dict(_drawn_inputs(seed))
    spreads = {}
    factors = {'diff_lam': 5.608,
     'diff_norm_g': 4.581,
     'ml_conv_b': 8.0,
     'ml_norm_g': 7.619,
     'gqa_qnorm_g': 8.0,
     'gqa_knorm_g': 8.0,
     'moe_b_group': 43.705,
     'moe_b_router': 21.379}
    for name, (base, spread) in spreads.items():
        noise = np.random.default_rng([zlib.crc32(name.encode()), seed]).standard_normal(out[name].shape)
        drawn = base * np.exp(spread * noise) if base else spread * noise
        out[name] = __import__('jax').numpy.asarray(drawn.astype(out[name].dtype))
    for name, factor in factors.items():
        out[name] = (out[name] * factor).astype(out[name].dtype)
    return out
```

```python
import math
from contextlib import ExitStack

import numpy as np

import concourse.bass as bass
from concourse import mybir

P = 128
D = 1024
KT = D // P
T = 512
SEG = 256
TT = T // P
DEPTH = 2
EPS = 1e-6
N_IN = 10000
HY = 512
TAPS = 256
E = 32
GROUPS, PER = 4, 8
HID = 512
MAXBLK = 40
NEG = -1.0e30

DQ, DK, DV = 0, 512, 1024
MQ, MK, MV, MO, MG = 1536, 2048, 2560, 3072, 3584
GQ, GK, GV = 3600, 4112, 4240
HU = 4368
BG = 5904

F32 = mybir.dt.float32
I32 = mybir.dt.int32
ALU = mybir.AluOpType
ACT = mybir.ActivationFunctionType
AXX = mybir.AxisListType.X

V1 = {}
_at = 0
for _name, _n in (("b_ada", 48), ("norm1", 8), ("norm2", 8), ("ml_conv", 24), ("ml_convb", 8)):
    V1[_name] = _at
    _at += _n
N1 = _at
for _name, _n in (("hy_conv", 36), ("hy_convb", 12), ("hy_bias", 8), ("diff_norm", 1), ("ml_norm", 1),
                  ("gq_norm", 1), ("gk_norm", 1), ("f_b1", 1), ("f_b2", 1), ("f_freq", 2), ("final", 8)):
    V1[_name] = _at
    _at += _n
N2 = _at - N1


def shape_constants():
    f8 = np.float64
    p = np.arange(P)
    cols, at, parts = {}, 0, []

    def add(name, a):
        nonlocal at
        a = np.asarray(a, np.float32).reshape(P, -1)
        cols[name] = (at, a.shape[1])
        at += a.shape[1]
        parts.append(a)

    add("ident", np.eye(P))
    add("ones", np.ones((P, P)))
    add("ones64", (p[:, None] // 64 == p[None, :] // 64))
    rot = np.zeros((P, P))
    for h in range(2):
        for d in range(64):
            q, r = d // 16, d % 16
            src = {0: 1, 1: 0, 2: 3, 3: 2}[q] * 16 + r
            rot[h * 64 + src, h * 64 + d] = -1.0 if q in (0, 2) else 1.0
    add("rot", rot)
    inv = (np.float32(10000.0) ** (-np.arange(16, dtype=np.float32) / np.float32(16))).astype(np.float32)
    tok = np.arange(SEG)
    ar = (tok // 64).astype(np.float32)[:, None] * inv
    ac = (tok % 64).astype(np.float32)[:, None] * inv
    ang = np.concatenate([ar, ar, ac, ac], -1)
    ang = np.concatenate([ang, ang], -1).T
    add("cos", np.cos(ang.astype(f8)))
    add("sin", np.sin(ang.astype(f8)))
    s, t = p[:, None], p[None, :]
    z = np.zeros((P, P))
    tri_f = np.where(s <= t, 0.0, NEG)
    tri_b = np.where(s >= t, 0.0, NEG)
    add("mask_f", np.concatenate([tri_f, z, z, z], 1))
    add("mask_b0", np.concatenate([tri_b, z + NEG, z, z], 1))
    add("mask_b1", np.concatenate([z, tri_b, z, z], 1))
    tt = np.arange(SEG).astype(f8)
    w = 2 * np.pi * np.outer(tt, np.arange(SEG)) / (2 * SEG)
    alt = (-1.0) ** np.arange(SEG)
    C, S = np.cos(w), np.sin(w)
    S[:, 0] = alt
    Cb = C[:, :P].copy()
    Cb[:, 0] = alt
    two = lambda a: a.reshape(2, P, -1).transpose(1, 0, 2)
    add("dft_c", two(C))
    add("dft_s", two(S))
    add("dft_cb", two(Cb))
    scale = np.full((SEG, 1), 2.0 / (2 * SEG))
    scale[0] = 1.0 / (2 * SEG)
    add("inv_c", two(C.T * scale))
    add("inv_s", two(S.T * scale))
    tf = (np.arange(TAPS, dtype=np.float32) / np.float32(TAPS))
    ld = abs(math.log(1e-2))
    alpha = np.linspace(ld / 1.5, ld / 0.3, HY).astype(np.float32)
    add("window", two(np.exp((-tf[:, None] * alpha).astype(f8)) + 0.05))
    bands = np.arange(1, 17, dtype=np.float32)
    an = np.float32(2.0 * math.pi) * tf[:, None] * bands
    emb = np.concatenate([tf[:, None], np.cos(an.astype(f8)), np.sin(an.astype(f8))], -1).T
    e = np.zeros((P, TAPS))
    e[:33] = emb
    add("emb", e)
    add("not0", (p[:, None] > 0))
    add("lt4", (p[:, None] < 4))
    add("ge4", (p[:, None] >= 4))
    add("upper", (s < t))
    add("slots", np.broadcast_to(np.arange(P), (P, P)))
    add("iota32", np.broadcast_to(np.arange(32), (P, 32)))
    add("iota40", np.broadcast_to(np.arange(MAXBLK), (P, MAXBLK)))
    return np.concatenate(parts, 1), cols


def backbone(nc, a, consts, ccols, out, tap=None):
    ctx = ExitStack()
    with ctx:
        def sb(name, shape, dt=F32):
            return ctx.enter_context(nc.sbuf_tensor(name, shape, dt))

        def sem(name):
            return ctx.enter_context(nc.semaphore(name))

        ctx.enter_context(nc.allow_non_contiguous_dma("small vectors"))

        XT = sb("XT", [P, KT, T])
        hT = sb("hT", [P, KT, T])
        Y = sb("Y", [P, 16, T])
        SLOT = 2048
        NSLOT = 3
        A0, B0, W0, S0 = 0, 8192, 16384, 16384 + NSLOT * SLOT
        AR = sb("arena", [P, 24576])
        scr = sb("scr", [P, 4, T])
        C = sb("consts", [P, consts.shape[1]])
        vrow = sb("vrow", [P, DEPTH, 2, P])
        vecs = sb("vecs", [P, DEPTH, N1 + N2])
        mod = sb("mod", [P, 48, 2])
        gs = sb("gs", [P, KT, 2])
        crow = sb("crow", [16, P])
        sc = sb("sc", [P, 16])
        small = sb("small", [P, 64])
        gw = sb("gw", [P, DEPTH, KT, 2, 2, 4])
        gb = sb("gb", [8, DEPTH, 2])
        aT = sb("aT", [P, 4, 8])
        lam4 = sb("lam4", [64, DEPTH, 4])
        w12 = sb("w12", [64, DEPTH, 128])
        rw = sb("rw", [P, DEPTH, KT, 36])
        rb = sb("rb", [P, DEPTH, 36])
        rt = sb("rt", [P, 4, 36])
        oh = sb("oh", [P, 4, 2, 32])
        dest = sb("dest", [P, 4, 2])
        gate = sb("gate", [P, 4, 2])
        desti = sb("desti", [P, 4, 2], I32)
        tab = sb("tab", [P, MAXBLK + 1], I32)
        pend = sb("pend", [P, 4, 32])
        cur = sb("cur", [P, P])
        eps_col = sb("eps_col", [P, 1])
        zeros = sb("zeros", [P, D // 2])
        ps = [ctx.enter_context(nc.psum_tensor(f"ps{i}", [P, T], F32)) for i in range(8)]
        ydram = [nc.dram_tensor(f"slot_outputs_{L}", ((MAXBLK + 2) * P, D), F32, kind="Internal").ap()
                 for L in range(DEPTH)]

        def con(name, sub=None):
            o, n = ccols[name]
            return C[:, o:o + n]

        ident, ones = con("ident"), con("ones")

        def v(L, name, i=0, n=1):
            return vecs[:, L, V1[name] + i:V1[name] + i + n]

        def slot(m, k, n):
            o = W0 + (m % NSLOT) * SLOT
            return AR[:, o:o + k * n].rearrange("p (k n) -> p k n", k=k)

        regA = AR[:, A0:A0 + 8192].rearrange("p (j t) -> p j t", t=T)
        regB = AR[:, B0:B0 + 8192].rearrange("p (j t) -> p j t", t=T)

        chunks = []

        def chunk(fill):
            chunks.append(fill)
            return len(chunks) - 1

        def w_in_chunk(L, c0, n=256):
            src = a["w_in"][L, :, c0:c0 + n].rearrange("(k p) n -> p k n", p=P)
            return chunk([(lambda m: slot(m, KT, n), src)])

        tiles = []

        def feature_tiles(L, phase, c0, n, kind, out_of, extra=None):
            for c in range(n // 256):
                m = w_in_chunk(L, c0 + 256 * c)
                for half in range(2):
                    j = 2 * c + half
                    tiles.append(dict(L=L, phase=phase, m=m, half=half, kind=kind, out=out_of(j), j=j,
                                      extra=extra, last=half == 1, tok=None))

        def token_tiles(L, phase, c0, n, out_of):
            w = min(n, 256)
            for c in range(n // w):
                m = w_in_chunk(L, c0 + w * c, w)
                for t in range(TT):
                    tiles.append(dict(L=L, phase=phase, m=m, kind="copy", out=out_of(t, c), tok=t, w=w,
                                      last=t == TT - 1))

        ada_m, w3_m, merge_m, wout_m, gate_m = {}, {}, {}, {}, {}
        for L in range(DEPTH):
            ada_m[L] = [chunk([(lambda m: slot(m, KT, 256),
                                a["w_ada"][L, :, 256 * c:256 * c + 256].rearrange("(k p) n -> p k n", p=P))])
                        for c in range(24)]
            feature_tiles(L, "ml", MQ, 1024, "conv", lambda j: regA[:, j, :], ("ml_conv", "ml_convb", 8))
            token_tiles(L, "ml", MV, 512, lambda t, c: regA[:, 8 + t, 256 * c:256 * c + 256])
            feature_tiles(L, "ml", MO, 512, "copy", lambda j: regA[:, 12 + j, :])
            feature_tiles(L, "hy", HU, 1536, "conv", lambda j: regB[:, j, :], ("hy_conv", "hy_convb", 12))
            w3_m[L] = chunk([(lambda m: slot(m, 1, 2048)[0:64, 0, :], a["hy_f_w3"][L])])
            feature_tiles(L, "df", DQ, 1024, "copy", lambda j: regA[:, j, :])
            token_tiles(L, "df", DV, 512, lambda t, c: regA[:, 8 + t, 256 * c:256 * c + 256])
            feature_tiles(L, "gq", GQ, 512, "copy", lambda j: regB[:, j, :])
            fills = []
            for g in range(2):
                src = a["w_in"][L, :, GK + 64 * g:GK + 64 * g + 64].rearrange("(k p) n -> p k n", p=P)
                for r in range(2):
                    o = 128 * g + 64 * r
                    fills.append((lambda m, o=o: slot(m, KT, 256)[:, :, o:o + 64], src))
            m = chunk(fills)
            for g in range(2):
                tiles.append(dict(L=L, phase="gq", m=m, half=g, kind="copy", out=regB[:, 4 + g, :], j=g,
                                  last=g == 1, tok=None))
            token_tiles(L, "gq", GV, 128, lambda t, c: regB[:, 6, 128 * t:128 * t + 128])
            merge_m[L] = []
            for jj in range(4):
                for n in range(4):
                    g = w_in_chunk(L, BG + n * D + 256 * jj)
                    b = chunk([(lambda m: slot(m, 4, 256),
                                a["w_branch"][L, n, :, 256 * jj:256 * jj + 256].rearrange("(k p) n -> p k n", p=P))])
                    merge_m[L].append((g, b))
            wout_m[L] = [chunk([(lambda m: slot(m, KT, 256),
                                 a["w_out"][L, :, 256 * c:256 * c + 256].rearrange("(k p) n -> p k n", p=P))])
                         for c in range(4)]
        n_conv = 0
        for q, t in enumerate(tiles):
            t["q"] = q
            if t["kind"] == "conv":
                n_conv += 1
            t["convs"] = n_conv
        layer_end_chunk = [wout_m[L][-1] for L in range(DEPTH)]

        block = ctx.enter_context(nc.Block())

        S = {}

        def sig(name):
            if name not in S:
                S[name] = sem(name)
            return S[name]

        class Book:

            def __init__(self):
                self.n = {}

            def base(self, link, k):
                b = self.n.get(link, 0)
                self.n[link] = b + k
                return b

        def arrived(e, m):
            per = sum(len(chunks[i]) for i in range(m % NSLOT, m + 1, NSLOT))
            e.wait_ge(sig(f"chunk_in_slot_{m % NSLOT}"), 16 * per)

        def meet(e, me, book):
            n = book.base("stage", 1) + 1
            e.drain().then_inc(sig(f"{me}_ended_stage"), 1)
            for other in ("tensor", "vector", "scalar"):
                if other != me:
                    e.wait_ge(sig(f"{other}_ended_stage"), n)

        def segs(ap):
            return ap.rearrange("p (s t) -> p s t", s=2)

        Yf = Y[:, :, :].rearrange("p j t -> p (j t)")
        rowsY = Yf[:, 0:4096].rearrange("p (t n) -> p t n", t=4)
        rowsB = AR[:, B0:B0 + 4096].rearrange("p (t n) -> p t n", t=4)
        rowsA = AR[:, A0:A0 + 8192].rearrange("p (t c n) -> p t c n", t=4, c=2)

        def tensor_turn(pe, book, src, groups=8):
            b, h = book.base("turned", groups), book.base("turned_out", groups // 2)
            for g in range(groups):
                if g >= 4:
                    who = "scalar" if g % 2 == 0 else "vector"
                    pe.wait_ge(sig(f"{who}_took_turned"), h + (g - 4) // 2 + 1)
                for i in range(4):
                    last = pe.transpose(ps[g % 4][:, P * i:P * i + P], src(g, i), ident)
                last.then_inc(sig("turned"), 1)

        def scalar_turn(act, book, dst, groups=8):
            b, h = book.base("turned", groups), book.base("turned_out", groups // 2)
            for g in range(0, groups, 2):
                act.wait_ge(sig("turned"), b + g + 1)
                act.activation(dst(g), ps[g % 4][:, :].rearrange("p (i t) -> p i t", i=4), ACT.Copy)\
                   .then_inc(sig("scalar_took_turned"), 1)

        def vector_turn(dve, book, dst, groups=8):
            b, h = book.base("turned", groups), book.base("turned_out", groups // 2)
            for g in range(1, groups, 2):
                dve.wait_ge(sig("turned"), b + g + 1)
                dve.tensor_copy(dst(g), ps[g % 4][:, :].rearrange("p (i t) -> p i t", i=4))\
                   .then_inc(sig("vector_took_turned"), 1)

        def xt_dst(g):
            return XT[:, 4 * (g % 2):4 * (g % 2) + 4, P * (g // 2):P * (g // 2) + P]

        def rows_src(rows):
            return lambda g, i: rows[:, g // 2, P * (4 * (g % 2) + i):P * (4 * (g % 2) + i) + P]

        def rows_dst(rows):
            return lambda g: rows[:, g // 2, 512 * (g % 2):512 * (g % 2) + 512].rearrange("p (i t) -> p i t", i=4)

        def scalar_rms(act, book):
            b = book.base("square", KT)
            c = book.base("rms", 1)
            for k in range(KT):
                if k >= 2:
                    act.wait_ge(sig("square_summed"), b + k - 1)
                act.activation(scr[:, k % 2, :], XT[:, k, :], ACT.Square).then_inc(sig("square"), 1)
            act.wait_ge(sig("square_summed"), b + KT)
            act.activation(scr[:, 2, :], ps[4][:, :], ACT.Ln, scale=1.0 / D, bias=eps_col[:, :])
            act.drain()
            act.activation(scr[:, 3, :], scr[:, 2, :], ACT.Exp, scale=-0.5).then_inc(sig("rms"), 1)

        def tensor_rms(pe, book):
            b = book.base("square", KT)
            for k in range(KT):
                pe.wait_ge(sig("square"), b + k + 1)
                pe.matmul(ps[4][:, :], ones, scr[:, k % 2, :], start=(k == 0), stop=(k == KT - 1))\
                  .then_inc(sig("square_summed"), 1)

        def vector_rms(dve, book, L, which):
            c = book.base("rms", 1)
            if which < 2:
                o = 24 * which
                for s in range(2):
                    dve.scalar_tensor_tensor(gs[:, :, s], mod[:, o + 8:o + 16, s], 1.0,
                                             v(L, ("norm1", "norm2")[which], 0, KT), ALU.add, ALU.mult)
            dve.wait_ge(sig("rms"), c + 1)
            for k in range(KT):
                dve.tensor_tensor(hT[:, k, :], XT[:, k, :], scr[:, 3, :], ALU.mult)
            dve.drain()
            for k in range(KT):
                if which < 2:
                    for s in range(2):
                        h = hT[:, k, SEG * s:SEG * s + SEG]
                        dve.tensor_scalar(h, h, gs[:, k, s:s + 1], mod[:, o + k, s:s + 1], ALU.mult, ALU.add)
                else:
                    dve.tensor_scalar(hT[:, k, :], hT[:, k, :], v(L, "final", k), None, ALU.mult)

        def vector_headnorm(dve, book, todo, more=None):
            n = len(todo)
            b = book.base("headnorm", n)

            def square(i):
                t, g = todo[i]
                if i >= 2:
                    dve.wait_ge(sig("head_squares_summed"), b + i - 1)
                dve.tensor_tensor(scr[:, i % 2, :], t, t, ALU.mult).then_inc(sig("head_squares"), 1)

            square(0)
            for i in range(n):
                if i + 1 < n:
                    square(i + 1)
                t, g = todo[i]
                dve.wait_ge(sig("head_rms"), b + i + 1)
                dve.scalar_tensor_tensor(t, t, g, scr[:, 2 + i % 2, :], ALU.mult, ALU.mult)\
                   .then_inc(sig("head_normed"), 1)
                if more:
                    dve.drain()
                    more(dve, i, t)

        def tensor_headnorm(pe, book, n, kernel_ones):
            b = book.base("headnorm", n)
            for i in range(n):
                pe.wait_ge(sig("head_squares"), b + i + 1)
                if i >= 2:
                    pe.wait_ge(sig("head_rms"), b + i - 1)
                pe.matmul(ps[4 + i % 2][:, :], kernel_ones, scr[:, i % 2, :], start=True, stop=True)\
                  .then_inc(sig("head_squares_summed"), 1)

        def scalar_headnorm(act, book, n, width):
            b = book.base("headnorm", n)
            for i in range(n):
                act.wait_ge(sig("head_squares_summed"), b + i + 1)
                if i >= 2:
                    act.wait_ge(sig("head_normed"), b + i - 1)
                act.activation(scr[:, 2 + i % 2, :], ps[4 + i % 2][:, :], ACT.Ln, scale=1.0 / width,
                               bias=eps_col[:, :])
                act.drain()
                act.activation(scr[:, 2 + i % 2, :], scr[:, 2 + i % 2, :], ACT.Exp, scale=-0.5)\
                   .then_inc(sig("head_rms"), 1)

        def tensor_project(pe, L, phase):
            for t in tiles:
                if t["L"] != L or t["phase"] != phase:
                    continue
                q, m = t["q"], t["m"]
                arrived(pe, m)
                if q >= 4:
                    pe.wait_ge(sig("projection_by_scalar"), q - 3)
                    if tiles[q - 4]["kind"] == "conv":
                        pe.wait_ge(sig("projection_by_vector"), tiles[q - 4]["convs"])
                bank = ps[q % 4]
                for k in range(KT):
                    if t["tok"] is None:
                        w = slot(m, KT, 256)[:, k, P * t["half"]:P * t["half"] + P]
                        last = pe.matmul(bank[:, :], w, hT[:, k, :], start=(k == 0), stop=(k == KT - 1))
                    else:
                        last = pe.matmul(bank[:, 0:t["w"]], hT[:, k, P * t["tok"]:P * t["tok"] + P],
                                         slot(m, KT, t["w"])[:, k, :], start=(k == 0), stop=(k == KT - 1))
                last.then_inc(sig("projected"), 1)
                if t["last"]:
                    pe.drain().then_inc(sig("chunk_used"), 1)

        def scalar_project(act, L, phase):
            for t in tiles:
                if t["L"] != L or t["phase"] != phase:
                    continue
                q = t["q"]
                act.wait_ge(sig("projected"), q + 1)
                if t["kind"] == "conv":
                    cw, cb, n = t["extra"]
                    act.activation(t["out"], ps[q % 4][:, :], ACT.Identity, bias=v(L, cb, t["j"]),
                                   scale=v(L, cw, n + t["j"])).then_inc(sig("projection_by_scalar"), 1)
                else:
                    w = t["w"] if t["tok"] is not None else T
                    act.activation(t["out"], ps[q % 4][:, 0:w], ACT.Copy)\
                       .then_inc(sig("projection_by_scalar"), 1)

        def vector_project(dve, L, phase):
            for t in tiles:
                if t["L"] != L or t["phase"] != phase or t["kind"] != "conv":
                    continue
                q = t["q"]
                cw, cb, n = t["extra"]
                dve.wait_ge(sig("projection_by_scalar"), q + 1)
                u, p = segs(t["out"]), segs(ps[q % 4][:, :])
                dve.scalar_tensor_tensor(u[:, :, 1:], p[:, :, 0:SEG - 1], v(L, cw, t["j"]), u[:, :, 1:],
                                         ALU.mult, ALU.add)
                dve.drain()
                dve.scalar_tensor_tensor(u[:, :, 0:SEG - 1], p[:, :, 1:], v(L, cw, 2 * n + t["j"]),
                                         u[:, :, 0:SEG - 1], ALU.mult, ALU.add)\
                   .then_inc(sig("projection_by_vector"), 1)
                dve.drain()

        def tensor_ada(pe, L):
            for c, m in enumerate(ada_m[L]):
                arrived(pe, m)
                for half in range(2):
                    o = 2 * (2 * c + half)
                    for k in range(KT):
                        last = pe.matmul(ps[5][:, o:o + 2], slot(m, KT, 256)[:, k, P * half:P * half + P],
                                         sc[:, k::8], start=(k == 0), stop=(k == KT - 1))
                pe.drain().then_inc(sig("chunk_used"), 1)
            pe.drain().then_inc(sig("modulation_summed"), 1)

        def vector_ada(dve, L):
            dve.wait_ge(sig("modulation_summed"), L + 1)
            dve.tensor_tensor(mod[:, :, :], ps[5][:, 0:96].rearrange("p (c s) -> p c s", s=2),
                              v(L, "b_ada", 0, 48).unsqueeze(2).to_broadcast([P, 48, 2]), ALU.add)
            dve.drain()

        gt = [AR[0:8, B0 + 512 * i:B0 + 512 * i + 512] for i in range(16)]
        LI, LF, F_F, F_B, A_F, A_B, M_F, M_B, NM, NMF, ONE, TMP, TMP2 = range(13)
        Wt = lambda j: AR[:, B0 + 512 * j:B0 + 512 * (j + 1)]

        def tensor_gates(pe, L):
            for kind in range(2):
                for k in range(KT):
                    last = pe.matmul(ps[6 + kind][0:8, :], gw[:, L, k, kind, :, :].rearrange("p d h -> p (d h)"),
                                     hT[:, k, :], start=(k == 0), stop=(k == KT - 1))
            last.then_inc(sig("gates_projected"), 1)

        def vector_gates(dve, L):
            dve.wait_ge(sig("gates_projected"), L + 1)
            dve.tensor_scalar(gt[LI], ps[6][0:8, :], gb[:, L, 0:1], None, ALU.add)
            dve.tensor_scalar(gt[LF], ps[7][0:8, :], gb[:, L, 1:2], None, ALU.add)
            dve.memset(gt[ONE], 1.0)
            dve.drain()
            dve.scalar_tensor_tensor(gt[TMP], gt[LF], -1.0, gt[LF], ALU.mult, ALU.max).then_inc(sig("gate_size"), 1)
            dve.tensor_scalar(gt[LF], gt[LF], 0.0, None, ALU.min)
            dve.drain()
            dve.wait_ge(sig("gate_log"), L + 1)
            dve.tensor_tensor(gt[LF], gt[LF], gt[TMP2], ALU.subtract)
            dve.drain()
            c, l = slice(0, SEG), slice(SEG, T)
            dve.tensor_tensor_scan(gt[F_F], gt[ONE], gt[LF], 0.0, ALU.mult, ALU.add)
            dve.tensor_tensor_scan(gt[F_B][:, 0:SEG][:, ::-1], gt[ONE][:, c], gt[LF][:, 0:SEG][:, ::-1], 0.0,
                                   ALU.mult, ALU.add)
            dve.drain()
            dve.tensor_tensor_scan(gt[F_B][:, SEG:T][:, ::-1], gt[ONE][:, c], gt[LF][:, SEG:T][:, ::-1],
                                   gt[F_B][:, 0:1], ALU.mult, ALU.add)
            dve.tensor_tensor(gt[A_F], gt[LI], gt[F_F], ALU.subtract)
            dve.drain()
            dve.tensor_tensor(gt[A_B], gt[LI], gt[F_B], ALU.subtract)
            dve.tensor_tensor_scan(gt[M_F], gt[A_F], gt[A_F], 0.0, ALU.max, ALU.max)
            dve.drain()
            ab = gt[A_B][:, 0:SEG][:, ::-1]
            dve.tensor_tensor_scan(gt[M_B][:, 0:SEG][:, ::-1], ab, ab, 0.0, ALU.max, ALU.max)
            dve.drain()
            ab = gt[A_B][:, SEG:T][:, ::-1]
            dve.tensor_tensor_scan(gt[M_B][:, SEG:T][:, ::-1], ab, ab, gt[M_B][:, 0:1], ALU.max, ALU.max)
            dve.drain()
            lt, ge = con("lt4")[0:8, :], con("ge4")[0:8, :]
            for f, b in ((A_F, A_B), (M_F, M_B), (F_F, F_B)):
                dve.tensor_scalar(gt[b], gt[b], ge, None, ALU.mult)
            dve.drain()
            for f, b in ((A_F, A_B), (M_F, M_B), (F_F, F_B)):
                dve.scalar_tensor_tensor(gt[f], gt[f], lt, gt[b], ALU.mult, ALU.add)
            dve.drain()
            dve.tensor_scalar(gt[NM], gt[M_F], -1.0, None, ALU.mult)
            dve.tensor_tensor(gt[F_F], gt[F_F], gt[M_F], ALU.add)
            dve.drain()
            dve.tensor_scalar(gt[NMF], gt[F_F], -1.0, None, ALU.mult)
            dve.drain().then_inc(sig("gate_rows"), 1)
            dve.wait_ge(sig("gate_columns"), L + 1)
            dve.tensor_copy(aT[:, :, :], ps[7][:, 0:32].rearrange("p (j r) -> p j r", j=4))
            dve.drain()

        def scalar_gates(act, L):
            act.wait_ge(sig("gate_size"), L + 1)
            act.activation(gt[TMP2], gt[TMP], ACT.Exp, scale=-1.0)
            act.drain()
            act.activation(gt[TMP2], gt[TMP2], ACT.Ln, bias=1.0).then_inc(sig("gate_log"), 1)

        def tensor_gate_columns(pe, L):
            pe.wait_ge(sig("gate_rows"), L + 1)
            for j in range(4):
                last = pe.transpose(ps[7][:, 8 * j:8 * j + 8], gt[A_F][:, P * j:P * j + P], ident[0:8, 0:8])
            last.then_inc(sig("gate_columns"), 1)

        def reach(j, r):
            if r < 4:
                return [(P * j, con("mask_f")[:, 0:T - P * j], T - P * j)]
            if j == 0:
                return [(0, con("mask_b0"), T)]
            if j == 1:
                return [(0, con("mask_b1"), T)]
            if j == 2:
                return [(2 * P, con("mask_b0")[:, 0:P], P)]
            return [(2 * P, con("mask_b1")[:, 0:2 * P], 2 * P)]

        units_ml = [(h, h + 4 * d) for h in range(4) for d in range(2)]

        def tensor_mlstm(pe, L, book):
            b = book.base("mlstm", 8)
            pe.wait_ge(sig("mlstm_qk"), L + 1)
            for u, (h, r) in enumerate(units_ml):
                if u >= 1:
                    pe.wait_ge(sig("mlstm_unit_done"), b + u)
                bc = ident[0:8, r:r + 1].to_broadcast([8, P])
                pe.matmul(ps[4][:, :], bc, gt[NM], start=True, stop=True)
                pe.matmul(ps[5][:, :], bc, gt[NMF], start=True, stop=True)
                if r < 4:
                    for j in range(4):
                        pe.matmul(ps[j][:, :], regA[:, 4 + h, P * j:P * j + P], regA[:, h, :], start=True, stop=True)
                pe.drain().then_inc(sig("mlstm_scores"), 1)
                for j in range(4):
                    (o, mask, w), = reach(j, r)
                    pe.wait_ge(sig("mlstm_weighted"), 4 * (b + u) + j + 1)
                    pe.matmul(ps[6][:, o:o + w], regA[:, 8 + j, P * h:P * h + P], Wt(j)[:, o:o + w],
                              start=(j == 0), stop=(j == 3))
                    last = pe.matmul(ps[7][:, o:o + w], ones, Wt(j)[:, o:o + w], start=(j == 0), stop=(j == 3))
                last.then_inc(sig("mlstm_summed"), 1)

        def scalar_mlstm(act, L, book):
            b = book.base("mlstm", 8)
            for u, (h, r) in enumerate(units_ml):
                act.wait_ge(sig("mlstm_scores"), b + u + 1)
                if u >= 1:
                    act.wait_ge(sig("mlstm_unit_done"), b + u)
                act.activation(scr[:, 0, :], ps[5][:, :], ACT.Exp).then_inc(sig("mlstm_floor"), 1)
                for j in range(4):
                    (o, mask, w), = reach(j, r)
                    act.wait_ge(sig("mlstm_exponent"), 4 * (b + u) + j + 1)
                    act.activation(Wt(j)[:, o:o + w], Wt(j)[:, o:o + w], ACT.Exp)\
                       .then_inc(sig("mlstm_decay"), 1)

        def vector_mlstm(dve, L, book):
            b = book.base("mlstm", 8)
            for u, (h, r) in enumerate(units_ml):
                dve.wait_ge(sig("mlstm_scores"), b + u + 1)
                for j in range(4):
                    (o, mask, w), = reach(j, r)
                    dve.scalar_tensor_tensor(Wt(j)[:, o:o + w], ps[4][:, o:o + w], aT[:, j, r:r + 1], mask,
                                             ALU.add, ALU.min).then_inc(sig("mlstm_exponent"), 1)
                for j in range(4):
                    (o, mask, w), = reach(j, r)
                    dve.wait_ge(sig("mlstm_decay"), 4 * (b + u) + j + 1)
                    dve.scalar_tensor_tensor(Wt(j)[:, o:o + w], ps[j][:, o:o + w], float(P) ** -0.5,
                                             Wt(j)[:, o:o + w], ALU.mult, ALU.mult)\
                       .then_inc(sig("mlstm_weighted"), 1)
                dve.wait_ge(sig("mlstm_summed"), b + u + 1)
                dve.wait_ge(sig("mlstm_floor"), b + u + 1)
                dve.scalar_tensor_tensor(scr[:, 1, :], ps[7][:, :], -1.0, scr[:, 0, :], ALU.mult, ALU.max)
                dve.drain()
                dve.tensor_tensor(scr[:, 1, :], ps[7][:, :], scr[:, 1, :], ALU.max)
                dve.drain()
                dve.reciprocal(scr[:, 1, :], scr[:, 1, :])
                dve.drain()
                y = Y[:, 4 + h, :]
                if r < 4:
                    dve.tensor_tensor(y, ps[6][:, :], scr[:, 1, :], ALU.mult)
                else:
                    dve.tensor_tensor(scr[:, 1, :], ps[6][:, :], scr[:, 1, :], ALU.mult)
                    dve.drain()
                    dve.tensor_tensor(y, y, scr[:, 1, :], ALU.add)
                dve.drain().then_inc(sig("mlstm_unit_done"), 1)

        def scalar_activate(act, list_of, fn):
            for t in list_of:
                act.activation(t, t, fn)

        def attention(kind, L, book):
            if kind == "df":
                q = lambda j, hf: regA[64 * hf:64 * hf + 64, j, :]
                k = lambda j, hf: regA[64 * hf:64 * hf + 64, 4 + j, :]
                vv = lambda j, hf, kt: regA[:, 8 + kt, P * j:P * j + P]
            else:
                q = lambda j, hf: regB[64 * hf:64 * hf + 64, j, :]
                k = lambda j, hf: regB[64 * hf:64 * hf + 64, 4 + j // 2, :]
                vv = lambda j, hf, kt: regB[:, 6, P * kt + 64 * (j // 2):P * kt + 64 * (j // 2) + 64]
            units = [(j, t) for t in range(TT) for j in range(4)]
            base = book.base("attention", 16)
            out = lambda j, t: Y[:, (0 if kind == "df" else 8) + j, P * t:P * t + P]
            return q, k, vv, units, base, out

        PO = S0
        prob = lambda hf: AR[:, S0 + 512 * hf:S0 + 512 * hf + 512]
        turned = lambda hf: AR[:, S0 + 1024 + 512 * hf:S0 + 1536 + 512 * hf]

        def tensor_attention(pe, kind, L, book):
            q, k, vv, units, b, out = attention(kind, L, book)
            hs = 1 if kind == "df" else 2

            def scores(u):
                j, t = units[u]
                n = SEG if t < 2 else T
                if u >= 2:
                    pe.wait_ge(sig("probabilities"), b + u - 1)
                for hf in range(2):
                    last = pe.matmul(ps[2 * (u % 2) + hf][:, 0:n], q(j, hf)[:, P * t:P * t + P], k(j, hf)[:, 0:n],
                                     start=True, stop=True)
                last.then_inc(sig("scores"), 1)

            scores(0)
            for u, (j, t) in enumerate(units):
                if u + 1 < 16:
                    scores(u + 1)
                nt = 2 if t < 2 else 4
                pe.wait_ge(sig("probabilities"), b + u + 1)
                if u >= 1:
                    pe.wait_ge(sig("turned_probabilities"), b + u)
                for hf in range(hs):
                    for kt in range(nt):
                        last = pe.transpose(ps[4 + hf][:, P * kt:P * kt + P], prob(hf)[:, P * kt:P * kt + P], ident)
                last.then_inc(sig("probabilities_turned"), 1)
                pe.wait_ge(sig("turned_probabilities"), b + u + 1)
                if u >= 2:
                    pe.wait_ge(sig("attended_out"), b + u - 1)
                for hf in range(hs):
                    o = ps[6 + u % 2][:, 0:P] if hs == 1 else ps[6 + u % 2][64 * hf:64 * hf + 64, 0:P]
                    for kt in range(nt):
                        last = pe.matmul(o, vv(j, hf, kt), turned(hf)[:, P * kt:P * kt + P],
                                         start=(kt == 0), stop=(kt == nt - 1))
                last.then_inc(sig("attended"), 1)

        def scalar_attention(act, kind, L, book):
            q, k, vv, units, b, out = attention(kind, L, book)
            hs = 1 if kind == "df" else 2
            for u, (j, t) in enumerate(units):
                n = SEG if t < 2 else T
                nt = n // P
                act.wait_ge(sig("score_maxima"), b + u + 1)
                if u >= 1:
                    act.wait_ge(sig("probabilities_turned"), b + u)
                for hf in range(2):
                    last = act.activation(prob(hf)[:, 0:n], ps[2 * (u % 2) + hf][:, 0:n], ACT.Exp, scale=0.125,
                                          bias=small[:, 2 * hf + 1:2 * hf + 2],
                                          accum_out=small[:, 4 + hf:5 + hf])
                act.drain().then_inc(sig("exponentials"), 1)
                act.wait_ge(sig("probabilities_turned"), b + u + 1)
                if u >= 1:
                    act.wait_ge(sig("attended"), b + u)
                for hf in range(hs):
                    last = act.activation(turned(hf)[:, 0:n], ps[4 + hf][:, 0:n], ACT.Copy)
                act.drain().then_inc(sig("turned_probabilities"), 1)
                act.wait_ge(sig("attended"), b + u + 1)
                act.activation(out(j, t), ps[6 + u % 2][:, 0:P], ACT.Copy).then_inc(sig("attended_out"), 1)

        def vector_attention(dve, kind, L, book):
            q, k, vv, units, b, out = attention(kind, L, book)
            for u, (j, t) in enumerate(units):
                n = SEG if t < 2 else T
                dve.wait_ge(sig("scores"), b + u + 1)
                if u >= 1:
                    dve.wait_ge(sig("exponentials"), b + u)
                for hf in range(2):
                    dve.reduce_max(small[:, 2 * hf:2 * hf + 1], ps[2 * (u % 2) + hf][:, 0:n], AXX)
                dve.drain()
                for hf in range(2):
                    dve.tensor_scalar(small[:, 2 * hf + 1:2 * hf + 2], small[:, 2 * hf:2 * hf + 1], -0.125, None,
                                      ALU.mult)
                dve.drain().then_inc(sig("score_maxima"), 1)
                dve.wait_ge(sig("exponentials"), b + u + 1)
                dve.reciprocal(small[:, 6:8], small[:, 4:6])
                dve.drain()
                if kind == "df":
                    dve.tensor_scalar(small[:, 7:8], small[:, 7:8], small[:, 16:17], None, ALU.mult)
                    dve.drain()
                for hf in range(2):
                    dve.tensor_scalar(prob(hf)[:, 0:n], prob(hf)[:, 0:n], small[:, 6 + hf:7 + hf], None, ALU.mult)
                if kind == "df":
                    dve.drain()
                    dve.tensor_tensor(prob(0)[:, 0:n], prob(0)[:, 0:n], prob(1)[:, 0:n], ALU.subtract)
                dve.drain().then_inc(sig("probabilities"), 1)

        def tensor_rope(pe, book, todo):
            b = book.base("rope", len(todo))
            for i, t in enumerate(todo):
                if i >= 2:
                    pe.wait_ge(sig("roped"), b + i - 1)
                pe.matmul(ps[6 + i % 2][:, 0:SEG], con("rot"), t[:, SEG:T], start=True, stop=True)\
                  .then_inc(sig("rotated"), 1)

        def vector_rope(dve, book, todo):
            b = book.base("rope", len(todo))
            for i, t in enumerate(todo):
                dve.wait_ge(sig("rotated"), b + i + 1)
                dve.tensor_tensor(scr[:, i % 2, 0:SEG], ps[6 + i % 2][:, 0:SEG], con("sin"), ALU.mult)
                dve.tensor_tensor(t[:, SEG:T], t[:, SEG:T], con("cos"), ALU.mult)
                dve.drain()
                dve.tensor_tensor(t[:, SEG:T], t[:, SEG:T], scr[:, i % 2, 0:SEG], ALU.add)\
                   .then_inc(sig("roped"), 1)

        def vector_lambda(dve, L):
            r = lam4[:, L, :]
            dve.tensor_tensor(small[0:64, 18:20], r[:, 0:4:2], r[:, 1:4:2], ALU.mult)
            dve.drain().then_inc(sig("lambda_products"), 1)
            dve.wait_ge(sig("lambda_exps"), L + 1)
            lam0 = 0.8 - 0.6 * math.exp(-0.3 * L)
            dve.tensor_scalar(small[:, 16:17], small[:, 20:21], small[:, 21:22], None, ALU.subtract)
            dve.drain()
            dve.tensor_scalar(small[:, 16:17], small[:, 16:17], lam0, None, ALU.add)
            dve.tensor_scalar(small[:, 17:18], v(L, "diff_norm"), 1.0 - lam0, None, ALU.mult)
            dve.drain()

        def scalar_lambda(act, L):
            act.wait_ge(sig("lambda_sums"), L + 1)
            act.activation(small[:, 20:22], ps[5][:, 0:2], ACT.Exp).then_inc(sig("lambda_exps"), 1)

        def tensor_lambda(pe, L):
            pe.wait_ge(sig("lambda_products"), L + 1)
            pe.matmul(ps[5][:, 0:2], ones[0:64, :], small[0:64, 18:20], start=True, stop=True)\
              .then_inc(sig("lambda_sums"), 1)

        KRE = lambda n, f: regA[:, 5 * n + f, :]
        KS = lambda n, f: regA[:, 5 * n + 2 + f, :]
        KRB = lambda n: regA[:, 5 * n + 4, :]
        ZT = lambda i: regA[:, 10 + i, :]
        FS = lambda i: regA[:, 10 + i, :]
        YR = lambda f: Y[:, f, :]
        YS = lambda f: Y[:, 2 + f, :]
        HA = lambda i: scr[0:64, i, 0:SEG]
        dft_c = con("dft_c").rearrange("p (t f) -> p t f", t=2)
        dft_s = con("dft_s").rearrange("p (t f) -> p t f", t=2)
        dft_cb = con("dft_cb").rearrange("p (t f) -> p t f", t=2)
        inv_c = con("inv_c").rearrange("p (f t) -> p f t", f=2)
        inv_s = con("inv_s").rearrange("p (f t) -> p f t", f=2)
        window = con("window").rearrange("p (t c) -> p t c", t=2)

        def tensor_filters(pe, L, book):
            pe.matmul(ps[0][0:64, 0:SEG], w12[0:33, L, 0:64], con("emb")[0:33, :], start=True, stop=True)\
              .then_inc(sig("filter_layer"), 1)
            pe.wait_ge(sig("filter_sine"), 2 * L + 1)
            pe.matmul(ps[1][0:64, 0:SEG], w12[:, L, 64:128], HA(0), start=True, stop=True)\
              .then_inc(sig("filter_layer"), 1)
            pe.wait_ge(sig("filter_sine"), 2 * L + 2)
            m = w3_m[L]
            arrived(pe, m)
            w3 = slot(m, 1, 2048)[0:64, 0, :]
            for n in range(2):
                if n == 1:
                    pe.wait_ge(sig("filter_windowed"), 2 * L + 1)
                for t in range(2):
                    for d in range(2):
                        last = pe.matmul(ps[2 * t + d][:, :], HA(1)[:, P * t:P * t + P],
                                         w3[:, 512 * (2 * n + d):512 * (2 * n + d) + 512], start=True, stop=True)
                last.then_inc(sig("filter_taps"), 1)
                if n == 1:
                    pe.drain().then_inc(sig("chunk_used"), 1)
                pe.wait_ge(sig("filter_windowed"), 2 * L + n + 1)
                pe.wait_ge(sig("filter_squares"), 2 * L + n + 1)
                for i in range(4):
                    last = pe.matmul(ps[4][:, :], ones, SQ(i), start=(i == 0), stop=(i == 3))
                last.then_inc(sig("filter_energy"), 1)
                pe.wait_ge(sig("filter_folded"), 2 * L + n + 1)
                for f in range(2):
                    for t in range(2):
                        pe.matmul(ps[5 + f][:, :], dft_c[:, t, P * f:P * f + P], FOLD(0, t), start=(t == 0),
                                  stop=(t == 1))
                for t in range(2):
                    last = pe.matmul(ps[7][:, :], dft_cb[:, t, :], FOLD(0, t), start=(t == 0), stop=(t == 1))
                last.then_inc(sig("filter_spectrum"), 1)
                pe.wait_ge(sig("filter_spectrum_out"), 4 * L + 2 * n + 1)
                for f in range(2):
                    for t in range(2):
                        last = pe.matmul(ps[5 + f][:, :], dft_s[:, t, P * f:P * f + P], FOLD(1, t), start=(t == 0),
                                         stop=(t == 1))
                last.then_inc(sig("filter_spectrum"), 1)

        SQ = lambda i: Y[:, i, :]
        TAP = lambda d, t: regA[:, 10 + 2 * t + d, :]
        FOLD = lambda part, t: regA[:, 10 + 2 * t + part, :]

        def sine(dve, L, i, bank, bias, freq):
            h = HA(i)
            dve.tensor_scalar(h, bank, bias[0:64, :], freq[0:64, :], ALU.add, ALU.mult)
            dve.drain()
            tmp, r = scr[0:64, 2, 0:SEG], scr[0:64, 3, 0:SEG].bitcast(I32)
            dve.tensor_scalar(tmp, h, 1.0 / (2 * math.pi), None, ALU.mult)
            dve.drain()
            magic = 12582912.0
            dve.tensor_scalar(tmp, tmp, magic, None, ALU.add)
            dve.drain()
            dve.tensor_scalar(tmp, tmp, -magic, None, ALU.add)
            dve.drain()
            hi = 6.28125
            dve.scalar_tensor_tensor(h, tmp, -hi, h, ALU.mult, ALU.add)
            dve.drain()
            dve.scalar_tensor_tensor(h, tmp, -(2 * math.pi - hi), h, ALU.mult, ALU.add)
            dve.drain()
            dve.tensor_scalar(h, h, 3.1415925, -3.1415925, ALU.min, ALU.max)
            dve.drain().then_inc(sig("filter_angle"), 1)

        def vector_filters(dve, L, book):
            dve.wait_ge(sig("filter_layer"), 2 * L + 1)
            sine(dve, L, 0, ps[0][0:64, 0:SEG], v(L, "f_b1"), v(L, "f_freq", 0))
            dve.wait_ge(sig("filter_layer"), 2 * L + 2)
            sine(dve, L, 1, ps[1][0:64, 0:SEG], v(L, "f_b2"), v(L, "f_freq", 1))
            for n in range(2):
                dve.wait_ge(sig("filter_taps"), 2 * L + n + 1)
                if n == 1:
                    dve.wait_ge(sig("filter_spectrum"), 4 * L + 2)
                for t in range(2):
                    dve.tensor_tensor(TAP(0, t), ps[2 * t][:, :], window[:, t, :], ALU.mult)
                    if t == 0:
                        dve.scalar_tensor_tensor(TAP(1, t), ps[2 * t + 1][:, :], con("not0"), window[:, t, :],
                                                 ALU.mult, ALU.mult)
                    else:
                        dve.tensor_tensor(TAP(1, t), ps[2 * t + 1][:, :], window[:, t, :], ALU.mult)
                dve.drain().then_inc(sig("filter_windowed"), 1)
                dve.wait_ge(sig("filter_root"), 2 * L + n + 1)
                for t in range(2):
                    dve.tensor_tensor(scr[:, 3, :], TAP(0, t), TAP(1, t), ALU.add)
                    dve.tensor_tensor(TAP(1, t), TAP(0, t), TAP(1, t), ALU.subtract)
                    dve.drain()
                    dve.tensor_tensor(FOLD(0, t), scr[:, 3, :], scr[:, 2, :], ALU.mult)
                    dve.tensor_tensor(FOLD(1, t), TAP(1, t), scr[:, 2, :], ALU.mult)
                    dve.drain()
                dve.drain().then_inc(sig("filter_folded"), 1)
                dve.wait_ge(sig("filter_spectrum_out"), 4 * L + 2 * n + 2)
                dve.tensor_scalar(KS(n, 0), KS(n, 0), con("not0"), None, ALU.mult)
            dve.drain()

        def scalar_filters(act, L, book):
            for i in range(2):
                act.wait_ge(sig("filter_angle"), 2 * L + i + 1)
                act.activation(HA(i), HA(i), ACT.Sin).then_inc(sig("filter_sine"), 1)
            for n in range(2):
                act.wait_ge(sig("filter_windowed"), 2 * L + n + 1)
                if n == 1:
                    act.wait_ge(sig("filter_energy"), 2 * L + 1)
                for i in range(4):
                    act.activation(SQ(i), regA[:, 10 + i, :], ACT.Square)
                act.drain().then_inc(sig("filter_squares"), 1)
                act.wait_ge(sig("filter_energy"), 2 * L + n + 1)
                act.activation(scr[:, 2, :], ps[4][:, :], ACT.Ln, bias=eps_col[:, :])
                act.drain()
                act.activation(scr[:, 2, :], scr[:, 2, :], ACT.Exp, scale=-0.5)
                act.drain().then_inc(sig("filter_root"), 1)
                act.wait_ge(sig("filter_spectrum"), 4 * L + 2 * n + 1)
                act.activation(KRE(n, 0), ps[5][:, :], ACT.Copy)
                act.activation(KRE(n, 1), ps[6][:, :], ACT.Copy)
                act.activation(KRB(n), ps[7][:, :], ACT.Copy)
                act.drain().then_inc(sig("filter_spectrum_out"), 1)
                act.wait_ge(sig("filter_spectrum"), 4 * L + 2 * n + 2)
                act.activation(KS(n, 0), ps[5][:, :], ACT.Copy)
                act.activation(KS(n, 1), ps[6][:, :], ACT.Copy)
                act.drain().then_inc(sig("filter_spectrum_out"), 1)

        units_hy = [(n, s) for n in range(2) for s in range(2)]

        def tensor_hyena(pe, L, book):
            b = book.base("hyena", 4)
            for u, (n, s) in enumerate(units_hy):
                if u >= 1:
                    pe.wait_ge(sig("hyena_gated"), b + u)
                for t in range(2):
                    for j in range(4):
                        last = pe.transpose(ps[t][:, P * j:P * j + P],
                                            regB[:, j, SEG * s + P * t:SEG * s + P * t + P], ident)
                last.then_inc(sig("hyena_turned"), 1)
                pe.wait_ge(sig("hyena_turned_out"), b + u + 1)
                for f in range(2):
                    for t in range(2):
                        pe.matmul(ps[2 + f][:, :], dft_c[:, t, P * f:P * f + P], ZT(t), start=(t == 0), stop=(t == 1))
                for f in range(2):
                    for t in range(2):
                        last = pe.matmul(ps[4 + f][:, :], dft_s[:, t, P * f:P * f + P], ZT(t), start=(t == 0),
                                         stop=(t == 1))
                last.then_inc(sig("hyena_spectrum"), 1)
                pe.wait_ge(sig("hyena_product"), b + u + 1)
                for j in range(4):
                    o = ps[6 + j // 2][:, SEG * (j % 2):SEG * (j % 2) + SEG]
                    for f in range(2):
                        pe.matmul(o, YR(f)[:, P * j:P * j + P], inv_c[:, f, :], start=(f == 0), stop=False)
                    for f in range(2):
                        last = pe.matmul(o, YS(f)[:, P * j:P * j + P], inv_s[:, f, :], start=False, stop=(f == 1))
                last.then_inc(sig("hyena_conv"), 1)

        def scalar_hyena(act, L, book):
            b = book.base("hyena", 4)
            for u, (n, s) in enumerate(units_hy):
                act.wait_ge(sig("hyena_turned"), b + u + 1)
                for t in range(2):
                    act.activation(ZT(t), ps[t][:, :], ACT.Copy)
                act.drain().then_inc(sig("hyena_turned_out"), 1)

        def vector_hyena(dve, L, book):
            b = book.base("hyena", 4)
            for u, (n, s) in enumerate(units_hy):
                dve.wait_ge(sig("hyena_spectrum"), b + u + 1)
                for f in range(2):
                    kb = KRB(n) if f == 0 else KRE(n, 1)
                    dve.tensor_tensor(YR(f), ps[2 + f][:, :], KRE(n, f), ALU.mult)
                    dve.tensor_tensor(YS(f), ps[2 + f][:, :], KS(n, f), ALU.mult)
                    dve.tensor_tensor(scr[:, 2 * f, :], ps[4 + f][:, :], KS(n, f), ALU.mult)
                    dve.tensor_tensor(scr[:, 2 * f + 1, :], ps[4 + f][:, :], kb, ALU.mult)
                dve.drain()
                for f in range(2):
                    dve.tensor_tensor(YR(f), YR(f), scr[:, 2 * f, :], ALU.subtract)
                    dve.tensor_tensor(YS(f), YS(f), scr[:, 2 * f + 1, :], ALU.add)
                dve.drain().then_inc(sig("hyena_product"), 1)
                dve.wait_ge(sig("hyena_conv"), b + u + 1)
                sl = slice(SEG * s, SEG * s + SEG)
                for j in range(4):
                    z = regB[:, j, sl]
                    dve.scalar_tensor_tensor(z, z, v(L, "hy_bias", 4 * n + j),
                                             ps[6 + j // 2][:, SEG * (j % 2):SEG * (j % 2) + SEG], ALU.mult, ALU.add)
                dve.drain()
                for j in range(4):
                    z = regB[:, j, sl]
                    dst = z if n == 0 else Y[:, 12 + j, sl]
                    dve.tensor_tensor(dst, z, regB[:, 4 * (n + 1) + j, sl], ALU.mult)
                dve.drain().then_inc(sig("hyena_gated"), 1)

        merged = lambda j: AR[:, A0 + 512 * j:A0 + 512 * j + 512]
        MG_UNITS = [(jj, n, half) for jj in range(4) for n in range(4) for half in range(2)]

        def tensor_merge(pe, L, book):
            b = book.base("merge", 32)
            for i2 in range(16):
                jj, n = i2 // 4, i2 % 4
                mg, mb = merge_m[L][i2]
                for m, width in ((mg, KT), (mb, 4)):
                    arrived(pe, m)
                    for half in range(2):
                        i = 2 * i2 + half
                        if i >= 4:
                            pe.wait_ge(sig("merged"), b + i - 3)
                        bank = ps[i % 4 if m == mg else 4 + i % 4]
                        for k in range(width):
                            rhs = hT[:, k, :] if m == mg else Y[:, 4 * n + k, :]
                            last = pe.matmul(bank[:, :], slot(m, width, 256)[:, k, P * half:P * half + P], rhs,
                                             start=(k == 0), stop=(k == width - 1))
                        last.then_inc(sig("merge_gate" if m == mg else "merge_branch"), 1)
                    pe.drain().then_inc(sig("chunk_used"), 1)

        def scalar_merge(act, L, book):
            b = book.base("merge", 32)
            for i in range(32):
                act.wait_ge(sig("merge_gate"), b + i + 1)
                if i >= 4:
                    act.wait_ge(sig("merged"), b + i - 3)
                act.activation(scr[:, i % 4, :], ps[i % 4][:, :], ACT.Sigmoid).then_inc(sig("merge_sigmoid"), 1)

        def vector_merge(dve, L, book):
            b = book.base("merge", 32)
            for i, (jj, n, half) in enumerate(MG_UNITS):
                dve.wait_ge(sig("merge_sigmoid"), b + i + 1)
                dve.wait_ge(sig("merge_branch"), b + i + 1)
                m = merged(2 * jj + half)
                if n == 0:
                    dve.tensor_tensor(m, scr[:, i % 4, :], ps[4 + i % 4][:, :], ALU.mult)
                else:
                    dve.tensor_tensor(scr[:, i % 4, :], scr[:, i % 4, :], ps[4 + i % 4][:, :], ALU.mult)
                    dve.drain()
                    dve.tensor_tensor(m, m, scr[:, i % 4, :], ALU.add)
                dve.drain().then_inc(sig("merged"), 1)

        def tensor_out(pe, L, book):
            b = book.base("out", 8)
            for j in range(8):
                m = wout_m[L][j // 2]
                arrived(pe, m)
                if j >= 4:
                    pe.wait_ge(sig("residual_added"), b + j - 3)
                for k in range(KT):
                    last = pe.matmul(ps[j % 4][:, :], slot(m, KT, 256)[:, k, P * (j % 2):P * (j % 2) + P], merged(k),
                                     start=(k == 0), stop=(k == KT - 1))
                last.then_inc(sig("out_projected"), 1)
                if j % 2 == 1:
                    pe.drain().then_inc(sig("chunk_used"), 1)

        def vector_out(dve, L, book):
            b = book.base("out", 8)
            for j in range(8):
                dve.wait_ge(sig("out_projected"), b + j + 1)
                for s in range(2):
                    x = XT[:, j, SEG * s:SEG * s + SEG]
                    last = dve.scalar_tensor_tensor(x, ps[j % 4][:, SEG * s:SEG * s + SEG], mod[:, 16 + j, s:s + 1], x,
                                                    ALU.mult, ALU.add)
                dve.drain().then_inc(sig("residual_added"), 1)

        work = scr[:, :, :].rearrange("p a t -> p (a t)")
        wk = lambda o, *shape: work[:, o:o + int(np.prod(shape))]
        iota32, iota40 = con("iota32"), con("iota40")

        def tensor_router(pe, L):
            for t in range(4):
                for k in range(KT):
                    last = pe.matmul(ps[4][:, 36 * t:36 * t + 36], hT[:, k, P * t:P * t + P], rw[:, L, k, :],
                                     start=(k == 0), stop=(k == KT - 1))
            last.then_inc(sig("router_logits"), 1)
            pe.wait_ge(sig("experts_chosen"), L + 1)
            both = pend
            for t in range(4):
                pe.matmul(ps[5][:, 32 * t:32 * t + 32], con("upper"), both[:, t, :], start=True, stop=(t == 0))
                for e in range(t):
                    pe.matmul(ps[5][:, 32 * t:32 * t + 32], ones, both[:, e, :], start=False, stop=(e == t - 1))
            for t in range(4):
                last = pe.matmul(ps[6][:, 0:32], ones, both[:, t, :], start=(t == 0), stop=(t == 3))
            last.then_inc(sig("experts_counted"), 1)

        def scalar_router(act, L):
            act.wait_ge(sig("group_margins"), L + 1)
            act.activation(wk(0, 16), wk(0, 16), ACT.Exp).then_inc(sig("group_exps"), 1)
            act.wait_ge(sig("expert_margin"), L + 1)
            act.activation(wk(16, 4), wk(16, 4), ACT.Exp).then_inc(sig("expert_exp"), 1)

        def vector_router(dve, L):
            def first_hot(vals, n, m_o, hot):
                mx = wk(m_o, 4)
                dve.tensor_reduce(mx, vals, AXX, ALU.max)
                dve.drain()
                eq = wk(1900, 4 * n).rearrange("p (t n) -> p t n", t=4)
                dve.tensor_tensor(eq, vals, mx.unsqueeze(2).to_broadcast([P, 4, n]), ALU.is_equal)
                dve.drain()
                dve.scalar_tensor_tensor(eq, eq, -100.0, iota32[:, 0:n].unsqueeze(1).to_broadcast([P, 4, n]),
                                         ALU.mult, ALU.add)
                dve.drain()
                mi = wk(1990, 4)
                dve.tensor_reduce(mi, eq, AXX, ALU.min)
                dve.drain()
                dve.tensor_tensor(hot, eq, mi.unsqueeze(2).to_broadcast([P, 4, n]), ALU.is_equal)
                dve.drain()

            dve.wait_ge(sig("router_logits"), L + 1)
            dve.tensor_tensor(rt[:, :, :], ps[4][:, 0:144].rearrange("p (t n) -> p t n", t=4),
                              rb[:, L, :].unsqueeze(1).to_broadcast([P, 4, 36]), ALU.add)
            dve.drain()
            hg = wk(40, 16).rearrange("p (t n) -> p t n", t=4)
            first_hot(rt[:, :, 0:4], 4, 32, hg)
            gm = wk(0, 16).rearrange("p (t n) -> p t n", t=4)
            dve.tensor_tensor(gm, rt[:, :, 0:4], wk(32, 4).unsqueeze(2).to_broadcast([P, 4, 4]), ALU.subtract)
            dve.drain().then_inc(sig("group_margins"), 1)
            el = wk(64, 128)
            dve.tensor_tensor(el.rearrange("p (t g e) -> p t g e", t=4, g=4),
                              rt[:, :, 4:36].rearrange("p t (g e) -> p t g e", g=4),
                              hg.unsqueeze(3).to_broadcast([P, 4, 4, 8]), ALU.mult)
            dve.drain()
            ein = wk(192, 32).rearrange("p (t e) -> p t e", t=4)
            dve.tensor_reduce(ein, el.rearrange("p (t g e) -> p t e g", t=4, g=4), AXX, ALU.add)
            dve.drain()
            h1 = wk(224, 32).rearrange("p (t e) -> p t e", t=4)
            h2 = wk(256, 32).rearrange("p (t e) -> p t e", t=4)
            e2 = wk(288, 32).rearrange("p (t e) -> p t e", t=4)
            first_hot(ein, 8, 320, h1)
            dve.tensor_scalar(e2, h1, -2.0e38, 1.0e38, ALU.mult, ALU.add)
            dve.drain()
            dve.tensor_tensor(e2, e2, ein, ALU.min)
            dve.drain()
            first_hot(e2, 8, 324, h2)
            dve.tensor_tensor(wk(16, 4), wk(324, 4), wk(320, 4), ALU.subtract)
            dve.drain().then_inc(sig("expert_margin"), 1)
            for c, h in ((0, h1), (1, h2)):
                for t in range(4):
                    dve.tensor_tensor(oh[:, t, c, :].rearrange("p (g e) -> p g e", g=4),
                                      hg[:, t, :].unsqueeze(2).to_broadcast([P, 4, 8]),
                                      h[:, t, :].unsqueeze(1).to_broadcast([P, 4, 8]), ALU.mult)
            dve.drain()
            dve.tensor_tensor(pend[:, :, :], oh[:, :, 0, :], oh[:, :, 1, :], ALU.add)
            dve.drain().then_inc(sig("experts_chosen"), 1)
            dve.wait_ge(sig("group_exps"), L + 1)
            dve.wait_ge(sig("expert_exp"), L + 1)
            dve.tensor_reduce(wk(328, 4), gm, AXX, ALU.add)
            dve.tensor_scalar(wk(332, 4), wk(16, 4), 1.0, None, ALU.add)
            dve.drain()
            dve.tensor_tensor(wk(328, 4), wk(328, 4), wk(332, 4), ALU.mult)
            dve.drain()
            dve.reciprocal(gate[:, :, 0], wk(328, 4))
            dve.drain()
            dve.tensor_tensor(gate[:, :, 1], gate[:, :, 0], wk(16, 4), ALU.mult)
            dve.wait_ge(sig("experts_counted"), L + 1)
            cnt, nb, pe_, st = wk(340, 32), wk(372, 32), wk(404, 32), wk(436, 32)
            dve.tensor_scalar(nb, ps[6][:, 0:32], 0.0, None, ALU.is_gt)
            dve.drain()
            for j in range(1, 4):
                dve.scalar_tensor_tensor(nb, ps[6][:, 0:32], float(P * j), nb, ALU.is_gt, ALU.add)
                dve.drain()
            dve.tensor_tensor_scan(pe_, nb, nb, 0.0, ALU.add, ALU.bypass)
            dve.drain()
            dve.tensor_tensor(st, pe_, nb, ALU.subtract)
            dve.drain()
            dve.tensor_scalar(st, st, float(P), None, ALU.mult)
            dve.drain()
            pos = wk(500, 128).rearrange("p (t e) -> p t e", t=4)
            dve.tensor_tensor(pos, ps[5][:, 0:128].rearrange("p (t e) -> p t e", t=4),
                              st.unsqueeze(1).to_broadcast([P, 4, 32]), ALU.add)
            dve.drain()
            for c in range(2):
                dve.tensor_tensor(oh[:, :, c, :], oh[:, :, c, :], pos, ALU.mult)
            dve.drain()
            dve.tensor_reduce(dest[:, :, :].rearrange("p t c -> p (t c)"),
                              oh[:, :, :, :].rearrange("p t c e -> p (t c) e"), AXX, ALU.add)
            dve.drain()
            dve.tensor_copy(desti[:, :, :], dest[:, :, :])
            cmp_ = wk(600, MAXBLK * 32).rearrange("p (b e) -> p b e", b=MAXBLK)
            dve.tensor_tensor(cmp_, pe_.unsqueeze(1).to_broadcast([P, MAXBLK, 32]),
                              iota40.unsqueeze(2).to_broadcast([P, MAXBLK, 32]), ALU.is_le)
            dve.drain()
            tf = wk(540, MAXBLK + 1)
            dve.tensor_reduce(tf[:, 0:MAXBLK], cmp_, AXX, ALU.add)
            pr = wk(600, MAXBLK)
            dve.drain()
            dve.tensor_scalar(tf[:, 0:MAXBLK], tf[:, 0:MAXBLK], float(E - 1), None, ALU.min)
            dve.tensor_scalar(pr, iota40, 2.0, pe_[:, 31:32], ALU.mult, ALU.is_lt)
            dve.drain()
            dve.tensor_reduce(tf[:, MAXBLK:MAXBLK + 1], pr, AXX, ALU.add)
            dve.drain()
            dve.tensor_copy(tab[:, :], tf)
            dve.tensor_copy(cur[:, :], con("slots"))
            dve.drain().then_inc(sig("moe_tables"), 1)

        part = [(0, KT), (4096, KT), (8192, 4)]
        wexp = lambda h, j: AR[:, 12288 * h + part[j][0]:12288 * h + part[j][0] + 4096]\
            .rearrange("p (k n) -> p k n", k=part[j][1])
        Sel = lambda h: scr[:, h, :].rearrange("p (t s) -> p t s", t=4)
        act_t = scr[:, 2, :]
        hid_t = scr[:, 3, :]
        xe = lambda h: Yf[:, 4096 + 1024 * h:5120 + 1024 * h].rearrange("p (k s) -> p k s", k=KT)
        yb = lambda h: Yf[:, 6144 + 1024 * h:7168 + 1024 * h]
        names = ("w_gate", "w_up", "w_down")

        def pairs(e, L, who):
            e.wait_ge(sig("moe_tables"), L + 1)
            return e.value_load(tab[0:1, MAXBLK:MAXBLK + 1], min_val=1, max_val=MAXBLK // 2)

        def lk(name, L):
            return sig(f"{name}_layer{L}")

        def sync_moe(sp, L):
            n = pairs(sp, L, "sp")
            with sp.Fori(0, n) as i:
                for h in range(2):
                    e = sp.value_load(tab[0:1, bass.ds(2 * i + h, 1)], min_val=0, max_val=E - 1)
                    for j, name in enumerate(names):
                        sp.wait_ge(lk("expert_slot_free", L), 2 * i + (h + 1))
                        src = a["moe_" + name][L][bass.ds(e, 1), :, :]
                        src = src.rearrange("o (k p) n -> p (o k) n", p=P)
                        sp.dma_start(wexp(h, j), src).then_inc(lk(f"{name}_{h}_loaded", L), 16)

        def tensor_moe(pe, L):
            n = pairs(pe, L, "pe")
            pe.drain().then_inc(lk("expert_slot_free", L), 2)
            pe.wait_ge(sig("rows_ready"), L + 1)

            def gather(b, h):
                pe.wait_ge(lk("slots_selected", L), b + 1)
                for k in range(KT):
                    for t in range(4):
                        last = pe.matmul(ps[k // 4][:, P * (k % 4):P * (k % 4) + P],
                                         rowsY[:, t, P * k:P * k + P], Sel(h)[:, t, :], start=(t == 0), stop=(t == 3))
                last.then_inc(lk("gathered", L), 1)

            gather(0, 0)
            with pe.Fori(0, n) as i:
                for h in range(2):
                    b = 2 * i + h
                    pe.wait_ge(lk("gathered_out", L), b + 1)
                    for j in range(2):
                        pe.wait_ge(lk(f"{names[j]}_{h}_loaded", L), 16 * i + 16)
                        for k in range(KT):
                            last = pe.matmul(ps[2 + j][:, :], xe(h)[:, k, :], wexp(h, j)[:, k, :],
                                             start=(k == 0), stop=(k == KT - 1))
                    last.then_inc(lk("gate_up", L), 1)
                    gather(b + 1, 1 - h)
                    pe.wait_ge(lk("hidden", L), b + 1)
                    for k in range(4):
                        last = pe.transpose(ps[4][:, P * k:P * k + P], act_t[:, P * k:P * k + P], ident)
                    last.then_inc(lk("hidden_turned", L), 1)
                    pe.wait_ge(lk("hidden_out", L), b + 1)
                    pe.wait_ge(lk("w_down_%d_loaded" % h, L), 16 * i + 16)
                    pe.wait_ge(lk("output_copied", L), 2 * b + 2)
                    for c in range(2):
                        for k in range(4):
                            last = pe.matmul(ps[5 + c][:, :], hid_t[:, P * k:P * k + P],
                                             wexp(h, 2)[:, k, 512 * c:512 * c + 512], start=(k == 0), stop=(k == 3))
                    last.then_inc(lk("down", L), 1)
                    pe.drain().then_inc(lk("expert_slot_free", L), 1)

        def scalar_moe(act, L):
            n = pairs(act, L, "act")
            act.drain().then_inc(lk("output_copied", L), 1)

            def take(b, h):
                act.wait_ge(lk("gathered", L), b + 1)
                for c in range(2):
                    act.activation(xe(h)[:, 4 * c:4 * c + 4, :],
                                   ps[c][:, :].rearrange("p (k s) -> p k s", k=4), ACT.Copy)
                act.drain().then_inc(lk("gathered_out", L), 1)

            take(0, 0)
            with act.Fori(0, n) as i:
                for h in range(2):
                    b = 2 * i + h
                    act.wait_ge(lk("gate_up", L), b + 1)
                    act.activation(act_t, ps[2][:, :], ACT.Silu).then_inc(lk("silu", L), 1)
                    take(b + 1, 1 - h)
                    act.wait_ge(lk("hidden_turned", L), b + 1)
                    act.activation(hid_t, ps[4][:, :], ACT.Copy).then_inc(lk("hidden_out", L), 1)
                    act.wait_ge(lk("down", L), b + 1)
                    act.wait_ge(lk("output_row_free", L), b + 1)
                    act.activation(yb(h)[:, 0:512], ps[5][:, :], ACT.Copy).then_inc(lk("output_copied", L), 1)

        def vector_moe(dve, L):
            n = pairs(dve, L, "dve")
            dve.drain().then_inc(lk("output_copied", L), 1)

            def select(h):
                for t in range(4):
                    dve.tensor_scalar(Sel(h)[:, t, :], cur[:, :], dest[:, t, 0:1], None, ALU.is_equal)
                dve.drain()
                for t in range(4):
                    dve.scalar_tensor_tensor(Sel(h)[:, t, :], cur[:, :], dest[:, t, 1:2], Sel(h)[:, t, :],
                                             ALU.is_equal, ALU.add)
                dve.drain().then_inc(lk("slots_selected", L), 1)
                dve.tensor_scalar(cur[:, :], cur[:, :], float(P), None, ALU.add)
                dve.drain()

            select(0)
            with dve.Fori(0, n) as i:
                for h in range(2):
                    b = 2 * i + h
                    select(1 - h)
                    dve.wait_ge(lk("silu", L), b + 1)
                    dve.tensor_tensor(act_t, act_t, ps[3][:, :], ALU.mult).then_inc(lk("hidden", L), 1)
                    dve.wait_ge(lk("down", L), b + 1)
                    dve.wait_ge(lk("output_row_free", L), b + 1)
                    dve.tensor_copy(yb(h)[:, 512:1024], ps[6][:, :]).then_inc(lk("output_copied", L), 1)

        def pool_moe(pool, L):
            n = pairs(pool, L, "pool")
            with pool.Fori(n, MAXBLK // 2 + 1) as i:
                for h in range(2):
                    row = ydram[L].rearrange("(b p) n -> b p n", p=P)[bass.ds(2 * i + h, 1), :, :]
                    for c in range(2):
                        pool.dma_start(row.rearrange("o p n -> (o p) n")[:, 512 * c:512 * c + 512], zeros[:, :])\
                            .then_inc(sig("tail_cleared"), 16)
            pool.drain().then_inc(lk("output_row_free", L), 2)
            with pool.Fori(0, n) as i:
                for h in range(2):
                    b = 2 * i + h
                    pool.wait_ge(lk("output_copied", L), 2 * b + 4)
                    row = ydram[L].rearrange("(b p) n -> b p n", p=P)[bass.ds(b, 1), :, :]
                    pool.dma_start(row.rearrange("o p n -> (o p) n"), yb(h)).then_inc(lk("output_written", L), 16)
                    pool.wait_ge(lk("output_written", L), 16 * b + 16)
                    pool.sem_inc(lk("output_row_free", L), 1)
            for t in range(4):
                for c in range(2):
                    pool.indirect_dma_start(out=rowsA[:, t, c, :], out_offset=None, in_=ydram[L],
                                            in_offset=bass.IndirectOffsetOnAxis(ap=desti[:, t, c:c + 1], axis=0))\
                        .then_inc(sig("rows_gathered"), 16)

        def vector_combine(dve, L):
            dve.wait_ge(sig("rows_gathered"), 16 * 8 * (L + 1))
            for t in range(4):
                dve.tensor_scalar(rowsA[:, t, 0, :], rowsA[:, t, 0, :], gate[:, t, 0:1], None, ALU.mult)
            dve.drain()
            for t in range(4):
                dve.scalar_tensor_tensor(rowsB[:, t, :], rowsA[:, t, 1, :], gate[:, t, 1:2], rowsA[:, t, 0, :],
                                         ALU.mult, ALU.add)
            dve.drain().then_inc(sig("rows_combined"), 1)

        def tensor_combine(pe, L, book):
            pe.wait_ge(sig("rows_combined"), L + 1)
            b = book.base("combine", 8)
            for g in range(8):
                if g >= 4:
                    pe.wait_ge(sig("combined_added"), b + g - 3)
                for i in range(4):
                    last = pe.transpose(ps[g % 4][:, P * i:P * i + P], rows_src(rowsB)(g, i), ident)
                last.then_inc(sig("combined_turned"), 1)

        def vector_combine_add(dve, L, book):
            b = book.base("combine", 8)
            for g in range(8):
                dve.wait_ge(sig("combined_turned"), b + g + 1)
                t, kg = g // 2, g % 2
                for i in range(4):
                    k = 4 * kg + i
                    x = XT[:, k, P * t:P * t + P]
                    dve.scalar_tensor_tensor(x, ps[g % 4][:, P * i:P * i + P], mod[:, 40 + k, t // 2:t // 2 + 1], x,
                                             ALU.mult, ALU.add)
                dve.drain().then_inc(sig("combined_added"), 1)

        @block.sync
        def _(sp):
            sp.dma_start(C[:, :], a["constants"]).then_inc(sig("inputs"), 16)
            sp.dma_start(rowsY[:, 0:2, :], a["ctx"][0].rearrange("(t p) n -> p t n", p=P)).then_inc(sig("inputs"), 16)
            sp.dma_start(rowsY[:, 2:4, :], a["x"][0].rearrange("(t p) n -> p t n", p=P)).then_inc(sig("inputs"), 16)

            def stream(lo, hi):
                for m in range(lo, hi):
                    if m >= NSLOT:
                        sp.wait_ge(sig("chunk_used"), m - NSLOT + 1)
                    for dst, src in chunks[m]:
                        sp.dma_start(dst(m), src).then_inc(sig(f"chunk_in_slot_{m % NSLOT}"), 16)

            at = 0
            for L in range(DEPTH):
                stream(at, layer_end_chunk[L] + 1)
                at = layer_end_chunk[L] + 1
                sp.wait_ge(sig("chunk_used"), at)
                sync_moe(sp, L)
                sp.wait_ge(sig("tensor_left_experts"), L + 1)
                if L + 1 < DEPTH:
                    sp.wait_ge(sig("stream_may_go_on"), L + 1)
            sp.wait_ge(sig("final_rows"), 1)
            sp.dma_start(out[0].rearrange("(t p) n -> p t n", p=P), rowsY[:, 2:4, :]).then_inc(sig("written"), 16)
            sp.wait_ge(sig("written"), 16)

        @block.gpsimd
        def _(pool):
            pool.memset(vrow[:, :, :, :], 0.0)
            pool.memset(eps_col[:, :], EPS)
            pool.memset(zeros[:, :], 0.0)
            pool.memset(pend[:, :, :], 0.0)
            pool.drain().then_inc(sig("rows_cleared"), 1)
            pool.wait_ge(sig("rows_cleared"), 1)
            n = 0

            def load(dst, src):
                nonlocal n
                pool.dma_start(dst, src).then_inc(sig("vectors"), 16)
                n += 1

            def rows(dst, src):
                load(dst, src)

            load(crow[0:8, :], a["c_ctx"].rearrange("(k p) -> k p", p=P))
            load(crow[8:16, :], a["c"][0].rearrange("(k p) -> k p", p=P))
            for L in range(DEPTH):
                def at(name, i, k):
                    o = V1[name] + i
                    return (vrow[o:o + k, L, 0, :] if o < N1 else vrow[o - N1:o - N1 + k, L, 1, :])

                fold = lambda x: x.rearrange("(k p) -> k p", p=P)
                load(at("b_ada", 0, 48), fold(a["b_ada"][L]))
                load(at("norm1", 0, 8), fold(a["norm1_g"][L]))
                load(at("norm2", 0, 8), fold(a["norm2_g"][L]))
                load(at("ml_conv", 0, 24), a["ml_conv_w"][L].rearrange("j (k p) -> (j k) p", p=P))
                load(at("ml_convb", 0, 8), fold(a["ml_conv_b"][L]))
                load(at("hy_conv", 0, 36), a["hy_conv_w"][L].rearrange("j (k p) -> (j k) p", p=P))
                load(at("hy_convb", 0, 12), fold(a["hy_conv_b"][L]))
                load(at("hy_bias", 0, 8), a["hy_bias"][L].rearrange("j (k p) -> (j k) p", p=P))
                row = lambda x: x.rearrange("(o n) -> o n", o=1)
                load(at("diff_norm", 0, 1), row(a["diff_norm_g"][L]))
                load(at("ml_norm", 0, 1), row(a["ml_norm_g"][L]))
                for half in range(2):
                    load(at("gq_norm", 0, 1)[:, 64 * half:64 * half + 64], row(a["gqa_qnorm_g"][L]))
                    load(at("gk_norm", 0, 1)[:, 64 * half:64 * half + 64], row(a["gqa_knorm_g"][L]))
                load(at("f_b1", 0, 1)[:, 0:64], row(a["hy_f_b1"][L]))
                load(at("f_b2", 0, 1)[:, 0:64], row(a["hy_f_b2"][L]))
                load(at("f_freq", 0, 2)[:, 0:64], a["hy_f_freq"][L])
                load(at("final", 0, 8), fold(a["final_norm_g"]))
                for kind in range(2):
                    for d in range(2):
                        c0 = MG + 8 * d + 4 * kind
                        load(gw[:, L, :, kind, d, :], a["w_in"][L, :, c0:c0 + 4].rearrange("(k p) n -> p k n", p=P))
                        load(gb[4 * d:4 * d + 4, L, kind:kind + 1],
                             a["ml_gate_b"][L, d, kind, :].rearrange("(h o) -> h o", o=1))
                load(lam4[:, L, :], a["diff_lam"][L].rearrange("j n -> n j"))
                load(w12[0:33, L, 0:64], a["hy_f_w1"][L])
                load(w12[:, L, 64:128], a["hy_f_w2"][L])
                load(rw[:, L, :, 0:4], a["moe_w_group"][L].rearrange("(k p) n -> p k n", p=P))
                load(rw[:, L, :, 4:36], a["moe_w_router"][L].rearrange("(k p) n -> p k n", p=P))
                load(rb[:, L, 0:4], a["moe_b_group"][L].partition_broadcast(P))
                load(rb[:, L, 4:36], a["moe_b_router"][L].partition_broadcast(P))
            pool.wait_ge(sig("vectors"), 16 * n)
            pool.drain().then_inc(sig("vectors_in"), 1)
            for L in range(DEPTH):
                pool_moe(pool, L)

        def turn_vectors_tensor(pe):
            pe.wait_ge(sig("inputs"), 48)
            pe.wait_ge(sig("vectors_in"), 1)
            pe.transpose(ps[4][:, 0:16], crow[:, :], ident[0:16, 0:16])
            for L in range(DEPTH):
                pe.transpose(ps[5 + L][:, 0:N1], vrow[0:N1, L, 0, :], ident[0:N1, 0:N1])
                last = pe.transpose(ps[5 + L][:, 128:128 + N2], vrow[0:N2, L, 1, :], ident[0:N2, 0:N2])
            last.then_inc(sig("vectors_turned"), 1)

        hg_attn = {"df": (0, 4), "gq": (8, 4)}
        df_rope = lambda: [regA[:, j, :] for j in range(8)]
        gq_rope = lambda: [regB[:, j, :] for j in range(6)]

        @block.tensor
        def _(pe):
            book, me = Book(), "tensor"
            turn_vectors_tensor(pe)
            tensor_turn(pe, book, rows_src(rowsY))
            meet(pe, me, book)
            for L in range(DEPTH):
                tensor_ada(pe, L)
                meet(pe, me, book)
                tensor_rms(pe, book)
                meet(pe, me, book)
                tensor_project(pe, L, "ml")
                tensor_gates(pe, L)
                tensor_gate_columns(pe, L)
                meet(pe, me, book)
                tensor_mlstm(pe, L, book)
                meet(pe, me, book)
                tensor_headnorm(pe, book, 4, ones)
                meet(pe, me, book)
                tensor_project(pe, L, "hy")
                meet(pe, me, book)
                tensor_filters(pe, L, book)
                meet(pe, me, book)
                tensor_hyena(pe, L, book)
                meet(pe, me, book)
                tensor_project(pe, L, "df")
                meet(pe, me, book)
                tensor_rope(pe, book, df_rope())
                tensor_lambda(pe, L)
                meet(pe, me, book)
                tensor_attention(pe, "df", L, book)
                meet(pe, me, book)
                tensor_headnorm(pe, book, 4, ones)
                meet(pe, me, book)
                tensor_project(pe, L, "gq")
                meet(pe, me, book)
                tensor_headnorm(pe, book, 6, con("ones64"))
                meet(pe, me, book)
                tensor_rope(pe, book, gq_rope())
                meet(pe, me, book)
                tensor_attention(pe, "gq", L, book)
                meet(pe, me, book)
                tensor_merge(pe, L, book)
                meet(pe, me, book)
                tensor_out(pe, L, book)
                meet(pe, me, book)
                tensor_rms(pe, book)
                meet(pe, me, book)
                tensor_turn(pe, book, lambda g, i: hT[:, 4 * (g % 2) + i, P * (g // 2):P * (g // 2) + P])
                meet(pe, me, book)
                pe.drain().then_inc(sig("rows_ready"), 1)
                tensor_router(pe, L)
                meet(pe, me, book)
                tensor_moe(pe, L)
                pe.drain().then_inc(sig("tensor_left_experts"), 1)
                meet(pe, me, book)
                tensor_combine(pe, L, book)
                meet(pe, me, book)
            tensor_rms(pe, book)
            meet(pe, me, book)
            tensor_turn(pe, book, lambda g, i: hT[:, 4 * (g % 2) + i, P * (g // 2):P * (g // 2) + P])

        @block.scalar
        def _(act):
            book, me = Book(), "scalar"
            act.wait_ge(sig("vectors_turned"), 1)
            act.activation(sc[:, :], ps[4][:, 0:16], ACT.Silu)
            for L in range(DEPTH):
                act.activation(vecs[:, L, 0:N1], ps[5 + L][:, 0:N1], ACT.Copy)
                act.activation(vecs[:, L, N1:N1 + N2], ps[5 + L][:, 128:128 + N2], ACT.Copy)
            scalar_turn(act, book, xt_dst)
            meet(act, me, book)
            for L in range(DEPTH):
                meet(act, me, book)
                scalar_rms(act, book)
                meet(act, me, book)
                scalar_project(act, L, "ml")
                scalar_gates(act, L)
                meet(act, me, book)
                scalar_activate(act, [regA[:, j, :] for j in range(8)], ACT.Silu)
                act.drain().then_inc(sig("mlstm_qk"), 1)
                scalar_activate(act, [regA[:, 12 + j, :] for j in range(4)], ACT.Sigmoid)
                scalar_mlstm(act, L, book)
                meet(act, me, book)
                scalar_headnorm(act, book, 4, P)
                meet(act, me, book)
                scalar_project(act, L, "hy")
                meet(act, me, book)
                scalar_filters(act, L, book)
                meet(act, me, book)
                scalar_hyena(act, L, book)
                meet(act, me, book)
                scalar_project(act, L, "df")
                meet(act, me, book)
                scalar_lambda(act, L)
                meet(act, me, book)
                scalar_attention(act, "df", L, book)
                meet(act, me, book)
                scalar_headnorm(act, book, 4, P)
                meet(act, me, book)
                scalar_project(act, L, "gq")
                meet(act, me, book)
                scalar_headnorm(act, book, 6, 64)
                meet(act, me, book)
                meet(act, me, book)
                scalar_attention(act, "gq", L, book)
                meet(act, me, book)
                scalar_merge(act, L, book)
                meet(act, me, book)
                meet(act, me, book)
                scalar_rms(act, book)
                meet(act, me, book)
                scalar_turn(act, book, rows_dst(rowsY))
                meet(act, me, book)
                scalar_router(act, L)
                meet(act, me, book)
                scalar_moe(act, L)
                meet(act, me, book)
                meet(act, me, book)
            scalar_rms(act, book)
            meet(act, me, book)
            scalar_turn(act, book, rows_dst(rowsY))
            act.drain().then_inc(sig("final_half"), 1)

        @block.vector
        def _(dve):
            book, me = Book(), "vector"
            vector_turn(dve, book, xt_dst)
            meet(dve, me, book)
            for L in range(DEPTH):
                vector_ada(dve, L)
                meet(dve, me, book)
                vector_rms(dve, book, L, 0)
                meet(dve, me, book)
                vector_project(dve, L, "ml")
                vector_gates(dve, L)
                meet(dve, me, book)
                vector_mlstm(dve, L, book)
                meet(dve, me, book)
                vector_headnorm(dve, book, [(Y[:, 4 + h, :], v(L, "ml_norm")) for h in range(4)],
                                lambda e, i, t: e.tensor_tensor(t, t, regA[:, 12 + i, :], ALU.mult))
                meet(dve, me, book)
                vector_project(dve, L, "hy")
                meet(dve, me, book)
                vector_filters(dve, L, book)
                meet(dve, me, book)
                vector_hyena(dve, L, book)
                meet(dve, me, book)
                meet(dve, me, book)
                vector_rope(dve, book, df_rope())
                vector_lambda(dve, L)
                meet(dve, me, book)
                vector_attention(dve, "df", L, book)
                meet(dve, me, book)
                vector_headnorm(dve, book, [(Y[:, h, :], small[:, 17:18]) for h in range(4)])
                meet(dve, me, book)
                meet(dve, me, book)
                vector_headnorm(dve, book, [(regB[:, j, :], v(L, "gq_norm" if j < 4 else "gk_norm")) for j in range(6)])
                meet(dve, me, book)
                vector_rope(dve, book, gq_rope())
                meet(dve, me, book)
                vector_attention(dve, "gq", L, book)
                meet(dve, me, book)
                vector_merge(dve, L, book)
                meet(dve, me, book)
                vector_out(dve, L, book)
                meet(dve, me, book)
                vector_rms(dve, book, L, 1)
                meet(dve, me, book)
                vector_turn(dve, book, rows_dst(rowsY))
                meet(dve, me, book)
                vector_router(dve, L)
                meet(dve, me, book)
                vector_moe(dve, L)
                meet(dve, me, book)
                vector_combine(dve, L)
                vector_combine_add(dve, L, book)
                dve.drain().then_inc(sig("stream_may_go_on"), 1)
                meet(dve, me, book)
            vector_rms(dve, book, 0, 2)
            meet(dve, me, book)
            vector_turn(dve, book, rows_dst(rowsY))
            dve.wait_ge(sig("final_half"), 1)
            dve.drain().then_inc(sig("final_rows"), 1)


_INS = ["x", "c", "ctx", "c_ctx", "w_ada", "b_ada", "norm1_g", "norm2_g", "w_in", "diff_lam", "diff_norm_g",
        "ml_conv_w", "ml_conv_b", "ml_gate_b", "ml_norm_g", "gqa_qnorm_g", "gqa_knorm_g",
        "hy_conv_w", "hy_conv_b", "hy_f_w1", "hy_f_b1", "hy_f_w2", "hy_f_b2", "hy_f_w3", "hy_f_freq", "hy_bias",
        "w_branch", "w_out", "moe_w_group", "moe_b_group", "moe_w_router", "moe_b_router",
        "moe_w_gate", "moe_w_up", "moe_w_down", "final_norm_g"]


def kernel(**inputs):
    import numpy as _np
    import concourse.bacc as _bacc
    from concourse import mybir as _mybir
    from concourse.bass_utils import run_bass_kernel_spmd as _run

    nc = _bacc.Bacc("TRN2", target_bir_lowering=False, num_devices=1)
    consts, ccols = shape_constants()
    arrays, args = {"constants_dram": consts}, {}
    for name in _INS:
        x = _np.ascontiguousarray(inputs[name])
        arrays[f"in_{name}_dram"] = x
        args[name] = nc.dram_tensor(f"in_{name}_dram", x.shape, _mybir.dt.from_np(x.dtype), kind="ExternalInput").ap()
    args["constants"] = nc.dram_tensor("constants_dram", consts.shape, _mybir.dt.from_np(consts.dtype),
                                       kind="ExternalInput").ap()
    shape = tuple(inputs["x"].shape)
    out = nc.dram_tensor("out_0_dram", shape, _mybir.dt.float32, kind="ExternalOutput").ap()
    backbone(nc, args, consts, ccols, out)
    r = _run(nc, [arrays], core_ids=[0])
    return r.results[0]["out_0_dram"]
```

```python
import math
from contextlib import ExitStack

import numpy as np

import concourse.bass as bass
from concourse import mybir

P = 128
D = 1024
KT = D // P
T = 512
SEG = 256
TT = T // P
DEPTH = 2
EPS = 1e-6
N_IN = 10000
HY = 512
TAPS = 256
E = 32
GROUPS, PER = 4, 8
HID = 512
MAXBLK = 40
NBT = MAXBLK + 3
FAR = 8192.0
NEG = -1.0e30

DQ, DK, DV = 0, 512, 1024
MQ, MK, MV, MO, MG = 1536, 2048, 2560, 3072, 3584
GQ, GK, GV = 3600, 4112, 4240
HU = 4368
BG = 5904

F32 = mybir.dt.float32
I32 = mybir.dt.int32
ALU = mybir.AluOpType
ACT = mybir.ActivationFunctionType
AXX = mybir.AxisListType.X

V1 = {}
_at = 0
for _name, _n in (("b_ada", 48), ("norm1", 8), ("norm2", 8), ("ml_conv", 24), ("ml_convb", 8)):
    V1[_name] = _at
    _at += _n
N1 = _at
for _name, _n in (("hy_conv", 36), ("hy_convb", 12), ("hy_bias", 8), ("diff_norm", 1), ("ml_norm", 1),
                  ("gq_norm", 1), ("gk_norm", 1), ("f_b1", 1), ("f_b2", 1), ("f_freq", 2), ("final", 8)):
    V1[_name] = _at
    _at += _n
N2 = _at - N1


def shape_constants():
    f8 = np.float64
    p = np.arange(P)
    cols, at, parts = {}, 0, []

    def add(name, a):
        nonlocal at
        a = np.asarray(a, np.float32).reshape(P, -1)
        cols[name] = (at, a.shape[1])
        at += a.shape[1]
        parts.append(a)

    add("ident", np.eye(P))
    add("ones", np.ones((P, P)))
    add("ones64", (p[:, None] // 64 == p[None, :] // 64))
    rot = np.zeros((P, P))
    for h in range(2):
        for d in range(64):
            q, r = d // 16, d % 16
            src = {0: 1, 1: 0, 2: 3, 3: 2}[q] * 16 + r
            rot[h * 64 + src, h * 64 + d] = -1.0 if q in (0, 2) else 1.0
    add("rot", rot)
    inv = (np.float32(10000.0) ** (-np.arange(16, dtype=np.float32) / np.float32(16))).astype(np.float32)
    tok = np.arange(SEG)
    ar = (tok // 64).astype(np.float32)[:, None] * inv
    ac = (tok % 64).astype(np.float32)[:, None] * inv
    ang = np.concatenate([ar, ar, ac, ac], -1)
    ang = np.concatenate([ang, ang], -1).T
    add("cos", np.cos(ang.astype(f8)))
    add("sin", np.sin(ang.astype(f8)))
    s, t = p[:, None], p[None, :]
    z = np.zeros((P, P))
    tri_f = np.where(s <= t, 0.0, NEG)
    tri_b = np.where(s >= t, 0.0, NEG)
    add("mask_f", np.concatenate([tri_f, z, z, z], 1))
    add("mask_b0", np.concatenate([tri_b, z + NEG, z, z], 1))
    add("mask_b1", np.concatenate([z, tri_b, z, z], 1))
    tt = np.arange(SEG).astype(f8)
    w = 2 * np.pi * np.outer(tt, np.arange(SEG)) / (2 * SEG)
    alt = (-1.0) ** np.arange(SEG)
    C, S = np.cos(w), np.sin(w)
    S[:, 0] = alt
    Cb = C[:, :P].copy()
    Cb[:, 0] = alt
    two = lambda a: a.reshape(2, P, -1).transpose(1, 0, 2)
    add("dft_c", two(C))
    add("dft_s", two(S))
    add("dft_cb", two(Cb))
    scale = np.full((SEG, 1), 2.0 / (2 * SEG))
    scale[0] = 1.0 / (2 * SEG)
    add("inv_c", two(C.T * scale))
    add("inv_s", two(S.T * scale))
    tf = (np.arange(TAPS, dtype=np.float32) / np.float32(TAPS))
    ld = abs(math.log(1e-2))
    alpha = np.linspace(ld / 1.5, ld / 0.3, HY).astype(np.float32)
    add("window", two(np.exp((-tf[:, None] * alpha).astype(f8)) + 0.05))
    bands = np.arange(1, 17, dtype=np.float32)
    an = np.float32(2.0 * math.pi) * tf[:, None] * bands
    emb = np.concatenate([tf[:, None], np.cos(an.astype(f8)), np.sin(an.astype(f8))], -1).T
    e = np.zeros((P, TAPS))
    e[:33] = emb
    add("emb", e)
    add("not0", (p[:, None] > 0))
    add("lt4", (p[:, None] < 4))
    add("ge4", (p[:, None] >= 4))
    add("upper", (s < t))
    add("slots", np.broadcast_to(np.arange(P), (P, P)))
    add("iota32", np.broadcast_to(np.arange(32), (P, 32)))
    add("iota_blk", np.broadcast_to(np.arange(NBT), (P, NBT)))
    add("tok_id", p[:, None] + P * np.arange(TT)[None, :])
    add("row_id", (2 * (p[:, None, None] + P * np.arange(TT)[None, :, None]) + np.arange(2)[None, None, :]))
    return np.concatenate(parts, 1), cols


def backbone(nc, a, consts, ccols, out, tap=None):
    ctx = ExitStack()
    with ctx:
        def sb(name, shape, dt=F32):
            return ctx.enter_context(nc.sbuf_tensor(name, shape, dt))

        def sem(name):
            return ctx.enter_context(nc.semaphore(name))

        ctx.enter_context(nc.allow_non_contiguous_dma("small vectors"))

        XT = sb("XT", [P, KT, T])
        hT = sb("hT", [P, KT, T])
        Y = sb("Y", [P, 16, T])
        SLOT = 2048
        NSLOT = 3
        WIDE = 8
        A0, B0, W0, S0 = 0, 8192, 16384, 16384 + NSLOT * SLOT
        AR = sb("arena", [P, 24576])
        scr = sb("scr", [P, 4, T])
        C = sb("consts", [P, consts.shape[1]])
        vrow = sb("vrow", [P, DEPTH, 2, P])
        vecs = sb("vecs", [P, DEPTH, N1 + N2])
        mods = sb("mods", [P, DEPTH, 48, 2])
        gs = sb("gs", [P, KT, 2])
        crow = sb("crow", [16, P])
        sc = sb("sc", [P, 16])
        small = sb("small", [P, 64])
        gw = sb("gw", [P, DEPTH, KT, 2, 2, 4])
        gb = sb("gb", [8, DEPTH, 2])
        aT = sb("aT", [P, 4, 8])
        lam4 = sb("lam4", [64, DEPTH, 4])
        w12 = sb("w12", [64, DEPTH, 128])
        rw = sb("rw", [P, DEPTH, KT, 36])
        rb = sb("rb", [P, DEPTH, 36])
        rt = sb("rt", [P, 4, 36])
        oh = sb("oh", [P, 4, 2, 32])
        place = sb("place", [P, 2, 4, 2])
        gate = sb("gate", [P, 4, 2])
        tab = sb("tab", [P, NBT + 1], I32)
        gidx = sb("gidx", [P, NBT], I32)
        sidx = sb("sidx", [P, NBT], I32)
        gi = sb("gi", [P, 2], I32)
        si = sb("si", [P, 2], I32)
        pend = sb("pend", [P, 4, 32])
        eps_col = sb("eps_col", [P, 1])
        ps = [ctx.enter_context(nc.psum_tensor(f"ps{i}", [P, T], F32)) for i in range(8)]
        def con(name, sub=None):
            o, n = ccols[name]
            return C[:, o:o + n]

        ident, ones = con("ident"), con("ones")

        def lo(L):
            return 0 if L < DEPTH - 1 else SEG

        def v(L, name, i=0, n=1):
            return vecs[:, L, V1[name] + i:V1[name] + i + n]

        def slot(m, k, n):
            i = chunks[m][1]
            o = W0 + i * SLOT if i < NSLOT else A0 + (i - NSLOT) * SLOT
            return AR[:, o:o + k * n].rearrange("p (k n) -> p k n", k=k)

        regA = AR[:, A0:A0 + 8192].rearrange("p (j t) -> p j t", t=T)
        regB = AR[:, B0:B0 + 8192].rearrange("p (j t) -> p j t", t=T)

        hrows = [nc.dram_tensor(f"moe_rows_{L}", (T - lo(L), D), F32, kind="Internal").ap() for L in range(DEPTH)]
        yrows = [nc.dram_tensor(f"moe_outputs_{L}", (2 * (T - lo(L)), D), F32, kind="Internal").ap()
                 for L in range(DEPTH)]

        chunks = []

        ring_at = [0]

        def chunk(fill, place_at=None):
            if place_at is None:
                place_at = ring_at[0] % NSLOT
                ring_at[0] += 1
            before = [i for i, c in enumerate(chunks) if c[1] == place_at]
            chunks.append((fill, place_at, before[-1] if before else None))
            return len(chunks) - 1

        def w_in_chunk(L, c0, n=256):
            src = a["w_in"][L, :, c0:c0 + n].rearrange("(k p) n -> p k n", p=P)
            return chunk([(lambda m: slot(m, KT, n), src)])

        tiles = []

        def feature_tiles(L, phase, c0, n, kind, out_of, extra=None, t0=0):
            for c in range(n // 256):
                m = w_in_chunk(L, c0 + 256 * c)
                for half in range(2):
                    j = 2 * c + half
                    tiles.append(dict(L=L, phase=phase, m=m, half=half, kind=kind, out=out_of(j), j=j,
                                      extra=extra, last=half == 1, tok=None, t0=t0))

        def token_tiles(L, phase, c0, n, out_of):
            w = min(n, 256)
            for c in range(n // w):
                m = w_in_chunk(L, c0 + w * c, w)
                for t in range(TT):
                    tiles.append(dict(L=L, phase=phase, m=m, kind="copy", out=out_of(t, c), tok=t, w=w,
                                      last=t == TT - 1))

        ada_m, w3_m, merge_m, wout_m = {}, {}, {}, {}

        def ada_chunk(L, c):
            return chunk([(lambda m: slot(m, KT, 256),
                           a["w_ada"][L, :, 256 * c:256 * c + 256].rearrange("(k p) n -> p k n", p=P))],
                         NSLOT + c % WIDE if L == 0 else NSLOT + WIDE // 2 + c % (WIDE // 2))

        ada_m[0] = [ada_chunk(0, c) for c in range(24)]
        for L in range(DEPTH):
            t0 = lo(L)
            feature_tiles(L, "ml", MQ, 512, "conv", lambda j: regA[:, j, :], ("ml_conv", "ml_convb", 8), t0)
            feature_tiles(L, "ml", MK, 512, "conv", lambda j: regA[:, 4 + j, :], ("ml_conv", "ml_convb", 8))
            for t in tiles[-4:]:
                t["j"] += 4
            token_tiles(L, "ml", MV, 512, lambda t, c: regA[:, 8 + t, 256 * c:256 * c + 256])
            feature_tiles(L, "ml", MO, 512, "copy", lambda j: regA[:, 12 + j, :], None, t0)
            feature_tiles(L, "hy", HU, 1536, "conv", lambda j: regB[:, j, :], ("hy_conv", "hy_convb", 12), t0)
            w3_m[L] = chunk([(lambda m: slot(m, 1, 2048)[0:64, 0, :], a["hy_f_w3"][L])])
            feature_tiles(L, "df", DQ, 512, "copy", lambda j: regA[:, j, :], None, t0)
            feature_tiles(L, "df", DK, 512, "copy", lambda j: regA[:, 4 + j, :])
            token_tiles(L, "df", DV, 512, lambda t, c: regA[:, 8 + t, 256 * c:256 * c + 256])
            feature_tiles(L, "gq", GQ, 512, "copy", lambda j: regB[:, j, :], None, t0)
            fills = []
            for g in range(2):
                src = a["w_in"][L, :, GK + 64 * g:GK + 64 * g + 64].rearrange("(k p) n -> p k n", p=P)
                for r in range(2):
                    o = 128 * g + 64 * r
                    fills.append((lambda m, o=o: slot(m, KT, 256)[:, :, o:o + 64], src))
            m = chunk(fills)
            for g in range(2):
                tiles.append(dict(L=L, phase="gq", m=m, half=g, kind="copy", out=regB[:, 4 + g, :], j=g,
                                  last=g == 1, tok=None, t0=0))
            token_tiles(L, "gq", GV, 128, lambda t, c: regB[:, 6, 128 * t:128 * t + 128])
            merge_m[L] = []
            for jj in range(4):
                for n in range(4):
                    g = w_in_chunk(L, BG + n * D + 256 * jj)
                    b = chunk([(lambda m: slot(m, 4, 256),
                                a["w_branch"][L, n, :, 256 * jj:256 * jj + 256].rearrange("(k p) n -> p k n", p=P))])
                    merge_m[L].append((g, b))
                    if L + 1 < DEPTH:
                        i2 = 4 * jj + n
                        ada_m.setdefault(L + 1, []).extend(ada_chunk(L + 1, c)
                                                           for c in range(3 * i2 // 2, 3 * (i2 + 1) // 2))
            wout_m[L] = [chunk([(lambda m: slot(m, KT, 256),
                                 a["w_out"][L, :, 256 * c:256 * c + 256].rearrange("(k p) n -> p k n", p=P))])
                         for c in range(4)]
        n_conv = 0
        for q, t in enumerate(tiles):
            t["q"] = q
            if t["kind"] == "conv":
                n_conv += 1
            t["convs"] = n_conv
        layer_end_chunk = [wout_m[L][-1] for L in range(DEPTH)]

        block = ctx.enter_context(nc.Block())

        S = {}

        def sig(name):
            if name not in S:
                S[name] = sem(name)
            return S[name]

        class Book:

            def __init__(self):
                self.n = {}

            def base(self, link, k):
                b = self.n.get(link, 0)
                self.n[link] = b + k
                return b

        def arrived(e, m):
            at = chunks[m][1]
            per = sum(len(c[0]) for c in chunks[:m + 1] if c[1] == at)
            e.wait_ge(sig(f"chunk_in_slot_{at}"), 16 * per)

        def meet(e, me, book):
            n = book.base("stage", 1) + 1
            e.drain().then_inc(sig(f"{me}_ended_stage"), 1)
            for other in ("tensor", "vector", "scalar"):
                if other != me:
                    e.wait_ge(sig(f"{other}_ended_stage"), n)

        def segs(ap):
            return ap.rearrange("p (s t) -> p s t", s=2)

        Yf = Y[:, :, :].rearrange("p j t -> p (j t)")
        rowsY = Yf[:, 0:4096].rearrange("p (t n) -> p t n", t=4)
        rowsB = AR[:, B0:B0 + 4096].rearrange("p (t n) -> p t n", t=4)
        rowsA = AR[:, A0:A0 + 8192].rearrange("p (t c n) -> p t c n", t=4, c=2)

        def tensor_turn(pe, book, src, g0=0):
            b, h = book.base("turned", 8 - g0) - g0, book.base("turned_out", 4 - g0 // 2) - g0 // 2
            for g in range(g0, 8):
                if g >= g0 + 4:
                    who = "scalar" if g % 2 == 0 else "vector"
                    pe.wait_ge(sig(f"{who}_took_turned"), h + (g - 4) // 2 + 1)
                for i in range(4):
                    last = pe.transpose(ps[g % 4][:, P * i:P * i + P], src(g, i), ident)
                last.then_inc(sig("turned"), 1)

        def scalar_turn(act, book, dst, g0=0):
            b, h = book.base("turned", 8 - g0) - g0, book.base("turned_out", 4 - g0 // 2) - g0 // 2
            for g in range(g0, 8, 2):
                act.wait_ge(sig("turned"), b + g + 1)
                act.activation(dst(g), ps[g % 4][:, :].rearrange("p (i t) -> p i t", i=4), ACT.Copy)\
                   .then_inc(sig("scalar_took_turned"), 1)

        def vector_turn(dve, book, dst, g0=0):
            b, h = book.base("turned", 8 - g0) - g0, book.base("turned_out", 4 - g0 // 2) - g0 // 2
            for g in range(g0 + 1, 8, 2):
                dve.wait_ge(sig("turned"), b + g + 1)
                dve.tensor_copy(dst(g), ps[g % 4][:, :].rearrange("p (i t) -> p i t", i=4))\
                   .then_inc(sig("vector_took_turned"), 1)

        def xt_dst(g):
            return XT[:, 4 * (g % 2):4 * (g % 2) + 4, P * (g // 2):P * (g // 2) + P]

        def rows_src(rows):
            return lambda g, i: rows[:, g // 2, P * (4 * (g % 2) + i):P * (4 * (g % 2) + i) + P]

        def rows_dst(rows):
            return lambda g: rows[:, g // 2, 512 * (g % 2):512 * (g % 2) + 512].rearrange("p (i t) -> p i t", i=4)

        def scalar_rms(act, book, t0=0):
            b = book.base("square", KT)
            c = book.base("rms", 1)
            for k in range(KT):
                if k >= 2:
                    act.wait_ge(sig("square_summed"), b + k - 1)
                act.activation(scr[:, k % 2, t0:], XT[:, k, t0:], ACT.Square).then_inc(sig("square"), 1)
            act.wait_ge(sig("square_summed"), b + KT)
            act.activation(scr[:, 2, t0:], ps[4][:, t0:], ACT.Ln, scale=1.0 / D, bias=eps_col[:, :])
            act.drain()
            act.activation(scr[:, 3, t0:], scr[:, 2, t0:], ACT.Exp, scale=-0.5).then_inc(sig("rms"), 1)

        def tensor_rms(pe, book, t0=0):
            b = book.base("square", KT)
            for k in range(KT):
                pe.wait_ge(sig("square"), b + k + 1)
                pe.matmul(ps[4][:, t0:], ones, scr[:, k % 2, t0:], start=(k == 0), stop=(k == KT - 1))\
                  .then_inc(sig("square_summed"), 1)

        def vector_rms(dve, book, L, which, t0=0):
            c = book.base("rms", 1)
            if which < 2:
                o = 24 * which
                for s in range(2):
                    dve.scalar_tensor_tensor(gs[:, :, s], mods[:, L, o + 8:o + 16, s], 1.0,
                                             v(L, ("norm1", "norm2")[which], 0, KT), ALU.add, ALU.mult)
            dve.wait_ge(sig("rms"), c + 1)
            for k in range(KT):
                dve.tensor_tensor(hT[:, k, t0:], XT[:, k, t0:], scr[:, 3, t0:], ALU.mult)
            dve.drain()
            for k in range(KT):
                if which < 2:
                    for s in range(t0 // SEG, 2):
                        h = hT[:, k, SEG * s:SEG * s + SEG]
                        dve.tensor_scalar(h, h, gs[:, k, s:s + 1], mods[:, L, o + k, s:s + 1], ALU.mult, ALU.add)
                else:
                    dve.tensor_scalar(hT[:, k, t0:], hT[:, k, t0:], v(L, "final", k), None, ALU.mult)

        def vector_headnorm(dve, book, todo, more=None):
            n = len(todo)
            b = book.base("headnorm", n)

            def square(i):
                t, g = todo[i]
                if i >= 2:
                    dve.wait_ge(sig("head_squares_summed"), b + i - 1)
                dve.tensor_tensor(scr[:, i % 2, 0:t.shape[-1]], t, t, ALU.mult).then_inc(sig("head_squares"), 1)

            square(0)
            for i in range(n):
                if i + 1 < n:
                    square(i + 1)
                t, g = todo[i]
                dve.wait_ge(sig("head_rms"), b + i + 1)
                dve.scalar_tensor_tensor(t, t, g, scr[:, 2 + i % 2, 0:t.shape[-1]], ALU.mult, ALU.mult)\
                   .then_inc(sig("head_normed"), 1)
                if more:
                    dve.drain()
                    more(dve, i, t)

        def tensor_headnorm(pe, book, widths, kernel_ones):
            n = len(widths)
            b = book.base("headnorm", n)
            for i in range(n):
                pe.wait_ge(sig("head_squares"), b + i + 1)
                if i >= 2:
                    pe.wait_ge(sig("head_rms"), b + i - 1)
                pe.matmul(ps[4 + i % 2][:, 0:widths[i]], kernel_ones, scr[:, i % 2, 0:widths[i]], start=True, stop=True)\
                  .then_inc(sig("head_squares_summed"), 1)

        def scalar_headnorm(act, book, widths, width):
            n = len(widths)
            b = book.base("headnorm", n)
            for i in range(n):
                act.wait_ge(sig("head_squares_summed"), b + i + 1)
                if i >= 2:
                    act.wait_ge(sig("head_normed"), b + i - 1)
                r = scr[:, 2 + i % 2, 0:widths[i]]
                act.activation(r, ps[4 + i % 2][:, 0:widths[i]], ACT.Ln, scale=1.0 / width, bias=eps_col[:, :])
                act.drain()
                act.activation(r, r, ACT.Exp, scale=-0.5)\
                   .then_inc(sig("head_rms"), 1)

        def tensor_project(pe, L, phase):
            for t in tiles:
                if t["L"] != L or t["phase"] != phase:
                    continue
                q, m = t["q"], t["m"]
                arrived(pe, m)
                if q >= 4:
                    pe.wait_ge(sig("projection_by_scalar"), q - 3)
                    if tiles[q - 4]["kind"] == "conv":
                        pe.wait_ge(sig("projection_by_vector"), tiles[q - 4]["convs"])
                bank = ps[q % 4]
                for k in range(KT):
                    if t["tok"] is None:
                        w = slot(m, KT, 256)[:, k, P * t["half"]:P * t["half"] + P]
                        last = pe.matmul(bank[:, t["t0"]:], w, hT[:, k, t["t0"]:], start=(k == 0), stop=(k == KT - 1))
                    else:
                        last = pe.matmul(bank[:, 0:t["w"]], hT[:, k, P * t["tok"]:P * t["tok"] + P],
                                         slot(m, KT, t["w"])[:, k, :], start=(k == 0), stop=(k == KT - 1))
                last.then_inc(sig("projected"), 1)
                if t["last"]:
                    pe.drain().then_inc(sig("chunk_used"), 1)

        def scalar_project(act, L, phase):
            for t in tiles:
                if t["L"] != L or t["phase"] != phase:
                    continue
                q = t["q"]
                act.wait_ge(sig("projected"), q + 1)
                if t["kind"] == "conv":
                    cw, cb, n = t["extra"]
                    z = t["t0"]
                    act.activation(t["out"][:, z:], ps[q % 4][:, z:], ACT.Identity, bias=v(L, cb, t["j"]),
                                   scale=v(L, cw, n + t["j"])).then_inc(sig("projection_by_scalar"), 1)
                else:
                    z, w = (0, t["w"]) if t["tok"] is not None else (t["t0"], T)
                    act.activation(t["out"][:, z:], ps[q % 4][:, z:w], ACT.Copy)\
                       .then_inc(sig("projection_by_scalar"), 1)

        def vector_project(dve, L, phase):
            for t in tiles:
                if t["L"] != L or t["phase"] != phase or t["kind"] != "conv":
                    continue
                q = t["q"]
                cw, cb, n = t["extra"]
                dve.wait_ge(sig("projection_by_scalar"), q + 1)
                z = t["t0"] // SEG
                u, p = segs(t["out"])[:, z:, :], segs(ps[q % 4][:, :])[:, z:, :]
                dve.scalar_tensor_tensor(u[:, :, 1:], p[:, :, 0:SEG - 1], v(L, cw, t["j"]), u[:, :, 1:],
                                         ALU.mult, ALU.add)
                dve.drain()
                dve.scalar_tensor_tensor(u[:, :, 0:SEG - 1], p[:, :, 1:], v(L, cw, 2 * n + t["j"]),
                                         u[:, :, 0:SEG - 1], ALU.mult, ALU.add)\
                   .then_inc(sig("projection_by_vector"), 1)
                dve.drain()

        ada_row = lambda c: scr[0:2, 3, 256 * (c % 2):256 * (c % 2) + 256]

        def tensor_ada(pe, L, cs, bank):
            def turn(c):
                pe.wait_ge(sig("ada_row_copied"), 24 * L + c + 1)
                for half in range(2):
                    o = 2 * (2 * c + half)
                    pe.transpose(bank[:, o:o + 2], ada_row(c)[:, P * half:P * half + P], ident[0:2, 0:2])

            for c in cs:
                m = ada_m[L][c]
                arrived(pe, m)
                if c >= 1:
                    turn(c - 1)
                for k in range(KT):
                    last = pe.matmul(ps[7][0:2, 0:256], sc[:, k::8], slot(m, KT, 256)[:, k, :],
                                     start=(k == 0), stop=(k == KT - 1))
                last.then_inc(sig("ada_row_summed"), 1)
                pe.drain().then_inc(sig("chunk_used"), 1)
                if c == 23:
                    turn(c)

        def scalar_ada(act, L, cs):
            for c in cs:
                act.wait_ge(sig("ada_row_summed"), 24 * L + c + 1)
                act.activation(ada_row(c), ps[7][0:2, 0:256], ACT.Copy)\
                   .then_inc(sig("ada_row_copied"), 1)

        def vector_ada(dve, L, bank):
            dve.tensor_tensor(mods[:, L, :, :], bank[:, 0:96].rearrange("p (c s) -> p c s", s=2),
                              v(L, "b_ada", 0, 48).unsqueeze(2).to_broadcast([P, 48, 2]), ALU.add)
            dve.drain()

        gt = [AR[0:8, B0 + 512 * i:B0 + 512 * i + 512] for i in range(16)]
        LI, LF, F_F, F_B, A_F, A_B, M_F, M_B, NM, NMF, ONE, TMP, TMP2 = range(13)
        Wt = lambda j: AR[:, B0 + 512 * j:B0 + 512 * (j + 1)]

        def tensor_gates(pe, L):
            for kind in range(2):
                for k in range(KT):
                    last = pe.matmul(ps[6 + kind][0:8, :], gw[:, L, k, kind, :, :].rearrange("p d h -> p (d h)"),
                                     hT[:, k, :], start=(k == 0), stop=(k == KT - 1))
            last.then_inc(sig("gates_projected"), 1)

        def vector_gates(dve, L):
            dve.wait_ge(sig("gates_projected"), L + 1)
            dve.tensor_scalar(gt[LI], ps[6][0:8, :], gb[:, L, 0:1], None, ALU.add)
            dve.tensor_scalar(gt[LF], ps[7][0:8, :], gb[:, L, 1:2], None, ALU.add)
            dve.memset(gt[ONE], 1.0)
            dve.drain()
            dve.scalar_tensor_tensor(gt[TMP], gt[LF], -1.0, gt[LF], ALU.mult, ALU.max).then_inc(sig("gate_size"), 1)
            dve.tensor_scalar(gt[LF], gt[LF], 0.0, None, ALU.min)
            dve.drain()
            dve.wait_ge(sig("gate_log"), L + 1)
            dve.tensor_tensor(gt[LF], gt[LF], gt[TMP2], ALU.subtract)
            dve.drain()
            c, l = slice(0, SEG), slice(SEG, T)
            dve.tensor_tensor_scan(gt[F_F], gt[ONE], gt[LF], 0.0, ALU.mult, ALU.add)
            dve.tensor_tensor_scan(gt[F_B][:, 0:SEG][:, ::-1], gt[ONE][:, c], gt[LF][:, 0:SEG][:, ::-1], 0.0,
                                   ALU.mult, ALU.add)
            dve.drain()
            dve.tensor_tensor_scan(gt[F_B][:, SEG:T][:, ::-1], gt[ONE][:, c], gt[LF][:, SEG:T][:, ::-1],
                                   gt[F_B][:, 0:1], ALU.mult, ALU.add)
            dve.tensor_tensor(gt[A_F], gt[LI], gt[F_F], ALU.subtract)
            dve.drain()
            dve.tensor_tensor(gt[A_B], gt[LI], gt[F_B], ALU.subtract)
            dve.tensor_tensor_scan(gt[M_F], gt[A_F], gt[A_F], 0.0, ALU.max, ALU.max)
            dve.drain()
            ab = gt[A_B][:, 0:SEG][:, ::-1]
            dve.tensor_tensor_scan(gt[M_B][:, 0:SEG][:, ::-1], ab, ab, 0.0, ALU.max, ALU.max)
            dve.drain()
            ab = gt[A_B][:, SEG:T][:, ::-1]
            dve.tensor_tensor_scan(gt[M_B][:, SEG:T][:, ::-1], ab, ab, gt[M_B][:, 0:1], ALU.max, ALU.max)
            dve.drain()
            lt, ge = con("lt4")[0:8, :], con("ge4")[0:8, :]
            for f, b in ((A_F, A_B), (M_F, M_B), (F_F, F_B)):
                dve.tensor_scalar(gt[b], gt[b], ge, None, ALU.mult)
            dve.drain()
            for f, b in ((A_F, A_B), (M_F, M_B), (F_F, F_B)):
                dve.scalar_tensor_tensor(gt[f], gt[f], lt, gt[b], ALU.mult, ALU.add)
            dve.drain()
            dve.tensor_scalar(gt[NM], gt[M_F], -1.0, None, ALU.mult)
            dve.tensor_tensor(gt[F_F], gt[F_F], gt[M_F], ALU.add)
            dve.drain()
            dve.tensor_scalar(gt[NMF], gt[F_F], -1.0, None, ALU.mult)
            dve.drain().then_inc(sig("gate_rows"), 1)
            dve.wait_ge(sig("gate_columns"), L + 1)
            dve.tensor_copy(aT[:, :, :], ps[7][:, 0:32].rearrange("p (j r) -> p j r", j=4))
            dve.drain()

        def scalar_gates(act, L):
            act.wait_ge(sig("gate_size"), L + 1)
            act.activation(gt[TMP2], gt[TMP], ACT.Exp, scale=-1.0)
            act.drain()
            act.activation(gt[TMP2], gt[TMP2], ACT.Ln, bias=1.0).then_inc(sig("gate_log"), 1)

        def tensor_gate_columns(pe, L):
            pe.wait_ge(sig("gate_rows"), L + 1)
            for j in range(4):
                last = pe.transpose(ps[7][:, 8 * j:8 * j + 8], gt[A_F][:, P * j:P * j + P], ident[0:8, 0:8])
            last.then_inc(sig("gate_columns"), 1)

        def reach(j, r, t0):
            if t0:
                zero = con("mask_f")[:, P:P + SEG]
                if j < 2:
                    return [(SEG, zero, SEG)]
                if r < 4:
                    return [(P * j, con("mask_f")[:, 0:T - P * j], T - P * j)]
            if r < 4:
                return [(P * j, con("mask_f")[:, 0:T - P * j], T - P * j)]
            if j == 0:
                return [(0, con("mask_b0"), T)]
            if j == 1:
                return [(0, con("mask_b1"), T)]
            if j == 2:
                return [(2 * P, con("mask_b0")[:, 0:P], P)]
            return [(2 * P, con("mask_b1")[:, 0:2 * P], 2 * P)]

        units_ml = [(h, h + 4 * d) for h in range(4) for d in range(2)]

        def tensor_mlstm(pe, L, book):
            b, t0 = book.base("mlstm", 8), lo(L)
            pe.wait_ge(sig("mlstm_qk"), L + 1)
            for u, (h, r) in enumerate(units_ml):
                if u >= 1:
                    pe.wait_ge(sig("mlstm_unit_done"), b + u)
                bc = ident[0:8, r:r + 1].to_broadcast([8, P])
                pe.matmul(ps[4][:, t0:], bc, gt[NM][:, t0:], start=True, stop=True)
                pe.matmul(ps[5][:, t0:], bc, gt[NMF][:, t0:], start=True, stop=True)
                if r < 4:
                    for j in range(4):
                        pe.matmul(ps[j][:, t0:], regA[:, 4 + h, P * j:P * j + P], regA[:, h, t0:], start=True, stop=True)
                pe.drain().then_inc(sig("mlstm_scores"), 1)
                for j in range(4):
                    (o, mask, w), = reach(j, r, lo(L))
                    pe.wait_ge(sig("mlstm_weighted"), 4 * (b + u) + j + 1)
                    pe.matmul(ps[6][:, o:o + w], regA[:, 8 + j, P * h:P * h + P], Wt(j)[:, o:o + w],
                              start=(j == 0), stop=(j == 3))
                    last = pe.matmul(ps[7][:, o:o + w], ones, Wt(j)[:, o:o + w], start=(j == 0), stop=(j == 3))
                last.then_inc(sig("mlstm_summed"), 1)

        def scalar_mlstm(act, L, book):
            b, t0 = book.base("mlstm", 8), lo(L)
            for u, (h, r) in enumerate(units_ml):
                act.wait_ge(sig("mlstm_scores"), b + u + 1)
                if u >= 1:
                    act.wait_ge(sig("mlstm_unit_done"), b + u)
                act.activation(scr[:, 0, t0:], ps[5][:, t0:], ACT.Exp).then_inc(sig("mlstm_floor"), 1)
                for j in range(4):
                    (o, mask, w), = reach(j, r, lo(L))
                    act.wait_ge(sig("mlstm_exponent"), 4 * (b + u) + j + 1)
                    act.activation(Wt(j)[:, o:o + w], Wt(j)[:, o:o + w], ACT.Exp)\
                       .then_inc(sig("mlstm_decay"), 1)

        def vector_mlstm(dve, L, book):
            b, t0 = book.base("mlstm", 8), lo(L)
            for u, (h, r) in enumerate(units_ml):
                dve.wait_ge(sig("mlstm_scores"), b + u + 1)
                for j in range(4):
                    (o, mask, w), = reach(j, r, lo(L))
                    dve.scalar_tensor_tensor(Wt(j)[:, o:o + w], ps[4][:, o:o + w], aT[:, j, r:r + 1], mask,
                                             ALU.add, ALU.min).then_inc(sig("mlstm_exponent"), 1)
                for j in range(4):
                    (o, mask, w), = reach(j, r, lo(L))
                    dve.wait_ge(sig("mlstm_decay"), 4 * (b + u) + j + 1)
                    dve.scalar_tensor_tensor(Wt(j)[:, o:o + w], ps[j][:, o:o + w], float(P) ** -0.5,
                                             Wt(j)[:, o:o + w], ALU.mult, ALU.mult)\
                       .then_inc(sig("mlstm_weighted"), 1)
                dve.wait_ge(sig("mlstm_summed"), b + u + 1)
                dve.wait_ge(sig("mlstm_floor"), b + u + 1)
                dve.scalar_tensor_tensor(scr[:, 1, t0:], ps[7][:, t0:], -1.0, scr[:, 0, t0:], ALU.mult, ALU.max)
                dve.drain()
                dve.tensor_tensor(scr[:, 1, t0:], ps[7][:, t0:], scr[:, 1, t0:], ALU.max)
                dve.drain()
                dve.reciprocal(scr[:, 1, t0:], scr[:, 1, t0:])
                dve.drain()
                y = Y[:, 4 + h, t0:]
                if r < 4:
                    dve.tensor_tensor(y, ps[6][:, t0:], scr[:, 1, t0:], ALU.mult)
                else:
                    dve.tensor_tensor(scr[:, 1, t0:], ps[6][:, t0:], scr[:, 1, t0:], ALU.mult)
                    dve.drain()
                    dve.tensor_tensor(y, y, scr[:, 1, t0:], ALU.add)
                dve.drain().then_inc(sig("mlstm_unit_done"), 1)

        def scalar_activate(act, list_of, fn):
            for t in list_of:
                act.activation(t, t, fn)

        def attention(kind, L, book):
            if kind == "df":
                q = lambda j, hf: regA[64 * hf:64 * hf + 64, j, :]
                k = lambda j, hf: regA[64 * hf:64 * hf + 64, 4 + j, :]
                vv = lambda j, hf, kt: regA[:, 8 + kt, P * j:P * j + P]
            else:
                q = lambda j, hf: regB[64 * hf:64 * hf + 64, j, :]
                k = lambda j, hf: regB[64 * hf:64 * hf + 64, 4 + j // 2, :]
                vv = lambda j, hf, kt: regB[:, 6, P * kt + 64 * (j // 2):P * kt + 64 * (j // 2) + 64]
            units = [(j, t) for t in range(lo(L) // P, TT) for j in range(4)]
            base = book.base("attention", len(units))
            out = lambda j, t: Y[:, (0 if kind == "df" else 8) + j, P * t:P * t + P]
            return q, k, vv, units, base, out

        PO = S0
        prob = lambda hf: AR[:, S0 + 512 * hf:S0 + 512 * hf + 512]
        turned = lambda hf: AR[:, S0 + 1024 + 512 * hf:S0 + 1536 + 512 * hf]

        def tensor_attention(pe, kind, L, book):
            q, k, vv, units, b, out = attention(kind, L, book)
            hs = 1 if kind == "df" else 2

            def scores(u):
                j, t = units[u]
                n = SEG if t < 2 else T
                if u >= 2:
                    pe.wait_ge(sig("probabilities"), b + u - 1)
                for hf in range(2):
                    last = pe.matmul(ps[2 * (u % 2) + hf][:, 0:n], q(j, hf)[:, P * t:P * t + P], k(j, hf)[:, 0:n],
                                     start=True, stop=True)
                last.then_inc(sig("scores"), 1)

            scores(0)
            for u, (j, t) in enumerate(units):
                if u + 1 < len(units):
                    scores(u + 1)
                nt = 2 if t < 2 else 4
                pe.wait_ge(sig("probabilities"), b + u + 1)
                if u >= 1:
                    pe.wait_ge(sig("turned_probabilities"), b + u)
                for hf in range(hs):
                    for kt in range(nt):
                        last = pe.transpose(ps[4 + hf][:, P * kt:P * kt + P], prob(hf)[:, P * kt:P * kt + P], ident)
                last.then_inc(sig("probabilities_turned"), 1)
                pe.wait_ge(sig("turned_probabilities"), b + u + 1)
                if u >= 2:
                    pe.wait_ge(sig("attended_out"), b + u - 1)
                for hf in range(hs):
                    o = ps[6 + u % 2][:, 0:P] if hs == 1 else ps[6 + u % 2][64 * hf:64 * hf + 64, 0:P]
                    for kt in range(nt):
                        last = pe.matmul(o, vv(j, hf, kt), turned(hf)[:, P * kt:P * kt + P],
                                         start=(kt == 0), stop=(kt == nt - 1))
                last.then_inc(sig("attended"), 1)

        def scalar_attention(act, kind, L, book):
            q, k, vv, units, b, out = attention(kind, L, book)
            hs = 1 if kind == "df" else 2
            for u, (j, t) in enumerate(units):
                n = SEG if t < 2 else T
                nt = n // P
                act.wait_ge(sig("score_maxima"), b + u + 1)
                if u >= 1:
                    act.wait_ge(sig("probabilities_turned"), b + u)
                for hf in range(2):
                    last = act.activation(prob(hf)[:, 0:n], ps[2 * (u % 2) + hf][:, 0:n], ACT.Exp, scale=0.125,
                                          bias=small[:, 2 * hf + 1:2 * hf + 2],
                                          accum_out=small[:, 4 + hf:5 + hf])
                act.drain().then_inc(sig("exponentials"), 1)
                act.wait_ge(sig("probabilities_turned"), b + u + 1)
                if u >= 1:
                    act.wait_ge(sig("attended"), b + u)
                for hf in range(hs):
                    last = act.activation(turned(hf)[:, 0:n], ps[4 + hf][:, 0:n], ACT.Copy)
                act.drain().then_inc(sig("turned_probabilities"), 1)
                act.wait_ge(sig("attended"), b + u + 1)
                act.activation(out(j, t), ps[6 + u % 2][:, 0:P], ACT.Copy).then_inc(sig("attended_out"), 1)

        def vector_attention(dve, kind, L, book):
            q, k, vv, units, b, out = attention(kind, L, book)
            for u, (j, t) in enumerate(units):
                n = SEG if t < 2 else T
                dve.wait_ge(sig("scores"), b + u + 1)
                if u >= 1:
                    dve.wait_ge(sig("exponentials"), b + u)
                for hf in range(2):
                    dve.reduce_max(small[:, 2 * hf:2 * hf + 1], ps[2 * (u % 2) + hf][:, 0:n], AXX)
                dve.drain()
                for hf in range(2):
                    dve.tensor_scalar(small[:, 2 * hf + 1:2 * hf + 2], small[:, 2 * hf:2 * hf + 1], -0.125, None,
                                      ALU.mult)
                dve.drain().then_inc(sig("score_maxima"), 1)
                dve.wait_ge(sig("exponentials"), b + u + 1)
                dve.reciprocal(small[:, 6:8], small[:, 4:6])
                dve.drain()
                if kind == "df":
                    dve.tensor_scalar(small[:, 7:8], small[:, 7:8], small[:, 16:17], None, ALU.mult)
                    dve.drain()
                for hf in range(2):
                    dve.tensor_scalar(prob(hf)[:, 0:n], prob(hf)[:, 0:n], small[:, 6 + hf:7 + hf], None, ALU.mult)
                if kind == "df":
                    dve.drain()
                    dve.tensor_tensor(prob(0)[:, 0:n], prob(0)[:, 0:n], prob(1)[:, 0:n], ALU.subtract)
                dve.drain().then_inc(sig("probabilities"), 1)

        def tensor_rope(pe, book, todo):
            b = book.base("rope", len(todo))
            for i, t in enumerate(todo):
                if i >= 2:
                    pe.wait_ge(sig("roped"), b + i - 1)
                pe.matmul(ps[6 + i % 2][:, 0:SEG], con("rot"), t[:, SEG:T], start=True, stop=True)\
                  .then_inc(sig("rotated"), 1)

        def vector_rope(dve, book, todo):
            b = book.base("rope", len(todo))
            for i, t in enumerate(todo):
                dve.wait_ge(sig("rotated"), b + i + 1)
                dve.tensor_tensor(scr[:, i % 2, 0:SEG], ps[6 + i % 2][:, 0:SEG], con("sin"), ALU.mult)
                dve.tensor_tensor(t[:, SEG:T], t[:, SEG:T], con("cos"), ALU.mult)
                dve.drain()
                dve.tensor_tensor(t[:, SEG:T], t[:, SEG:T], scr[:, i % 2, 0:SEG], ALU.add)\
                   .then_inc(sig("roped"), 1)

        def vector_lambda(dve, L):
            r = lam4[:, L, :]
            dve.tensor_tensor(small[0:64, 18:20], r[:, 0:4:2], r[:, 1:4:2], ALU.mult)
            dve.drain().then_inc(sig("lambda_products"), 1)
            dve.wait_ge(sig("lambda_exps"), L + 1)
            lam0 = 0.8 - 0.6 * math.exp(-0.3 * L)
            dve.tensor_scalar(small[:, 16:17], small[:, 20:21], small[:, 21:22], None, ALU.subtract)
            dve.drain()
            dve.tensor_scalar(small[:, 16:17], small[:, 16:17], lam0, None, ALU.add)
            dve.tensor_scalar(small[:, 17:18], v(L, "diff_norm"), 1.0 - lam0, None, ALU.mult)
            dve.drain()

        def scalar_lambda(act, L):
            act.wait_ge(sig("lambda_sums"), L + 1)
            act.activation(small[:, 20:22], ps[5][:, 0:2], ACT.Exp).then_inc(sig("lambda_exps"), 1)

        def tensor_lambda(pe, L):
            pe.wait_ge(sig("lambda_products"), L + 1)
            pe.matmul(ps[5][:, 0:2], ones[0:64, :], small[0:64, 18:20], start=True, stop=True)\
              .then_inc(sig("lambda_sums"), 1)

        KRE = lambda n, f: regA[:, 5 * n + f, :]
        KS = lambda n, f: regA[:, 5 * n + 2 + f, :]
        KRB = lambda n: regA[:, 5 * n + 4, :]
        ZT = lambda i: regA[:, 10 + i, :]
        FS = lambda i: regA[:, 10 + i, :]
        YR = lambda f: Y[:, f, :]
        YS = lambda f: Y[:, 2 + f, :]
        HA = lambda i: scr[0:64, i, 0:SEG]
        dft_c = con("dft_c").rearrange("p (t f) -> p t f", t=2)
        dft_s = con("dft_s").rearrange("p (t f) -> p t f", t=2)
        dft_cb = con("dft_cb").rearrange("p (t f) -> p t f", t=2)
        inv_c = con("inv_c").rearrange("p (f t) -> p f t", f=2)
        inv_s = con("inv_s").rearrange("p (f t) -> p f t", f=2)
        window = con("window").rearrange("p (t c) -> p t c", t=2)

        def tensor_filters(pe, L, book):
            pe.matmul(ps[0][0:64, 0:SEG], w12[0:33, L, 0:64], con("emb")[0:33, :], start=True, stop=True)\
              .then_inc(sig("filter_layer"), 1)
            pe.wait_ge(sig("filter_sine"), 2 * L + 1)
            pe.matmul(ps[1][0:64, 0:SEG], w12[:, L, 64:128], HA(0), start=True, stop=True)\
              .then_inc(sig("filter_layer"), 1)
            pe.wait_ge(sig("filter_sine"), 2 * L + 2)
            m = w3_m[L]
            arrived(pe, m)
            w3 = slot(m, 1, 2048)[0:64, 0, :]
            for n in range(2):
                if n == 1:
                    pe.wait_ge(sig("filter_windowed"), 2 * L + 1)
                for t in range(2):
                    for d in range(2):
                        last = pe.matmul(ps[2 * t + d][:, :], HA(1)[:, P * t:P * t + P],
                                         w3[:, 512 * (2 * n + d):512 * (2 * n + d) + 512], start=True, stop=True)
                last.then_inc(sig("filter_taps"), 1)
                if n == 1:
                    pe.drain().then_inc(sig("chunk_used"), 1)
                pe.wait_ge(sig("filter_windowed"), 2 * L + n + 1)
                pe.wait_ge(sig("filter_squares"), 2 * L + n + 1)
                for i in range(4):
                    last = pe.matmul(ps[4][:, :], ones, SQ(i), start=(i == 0), stop=(i == 3))
                last.then_inc(sig("filter_energy"), 1)
                pe.wait_ge(sig("filter_folded"), 2 * L + n + 1)
                for f in range(2):
                    for t in range(2):
                        pe.matmul(ps[5 + f][:, :], dft_c[:, t, P * f:P * f + P], FOLD(0, t), start=(t == 0),
                                  stop=(t == 1))
                for t in range(2):
                    last = pe.matmul(ps[7][:, :], dft_cb[:, t, :], FOLD(0, t), start=(t == 0), stop=(t == 1))
                last.then_inc(sig("filter_spectrum"), 1)
                pe.wait_ge(sig("filter_spectrum_out"), 4 * L + 2 * n + 1)
                for f in range(2):
                    for t in range(2):
                        last = pe.matmul(ps[5 + f][:, :], dft_s[:, t, P * f:P * f + P], FOLD(1, t), start=(t == 0),
                                         stop=(t == 1))
                last.then_inc(sig("filter_spectrum"), 1)

        SQ = lambda i: Y[:, i, :]
        TAP = lambda d, t: regA[:, 10 + 2 * t + d, :]
        FOLD = lambda part, t: regA[:, 10 + 2 * t + part, :]

        def sine(dve, L, i, bank, bias, freq):
            h = HA(i)
            dve.tensor_scalar(h, bank, bias[0:64, :], freq[0:64, :], ALU.add, ALU.mult)
            dve.drain()
            tmp, r = scr[0:64, 2, 0:SEG], scr[0:64, 3, 0:SEG].bitcast(I32)
            dve.tensor_scalar(tmp, h, 1.0 / (2 * math.pi), None, ALU.mult)
            dve.drain()
            magic = 12582912.0
            dve.tensor_scalar(tmp, tmp, magic, None, ALU.add)
            dve.drain()
            dve.tensor_scalar(tmp, tmp, -magic, None, ALU.add)
            dve.drain()
            hi = 6.28125
            dve.scalar_tensor_tensor(h, tmp, -hi, h, ALU.mult, ALU.add)
            dve.drain()
            dve.scalar_tensor_tensor(h, tmp, -(2 * math.pi - hi), h, ALU.mult, ALU.add)
            dve.drain()
            dve.tensor_scalar(h, h, 3.1415925, -3.1415925, ALU.min, ALU.max)
            dve.drain().then_inc(sig("filter_angle"), 1)

        def vector_filters(dve, L, book):
            dve.wait_ge(sig("filter_layer"), 2 * L + 1)
            sine(dve, L, 0, ps[0][0:64, 0:SEG], v(L, "f_b1"), v(L, "f_freq", 0))
            dve.wait_ge(sig("filter_layer"), 2 * L + 2)
            sine(dve, L, 1, ps[1][0:64, 0:SEG], v(L, "f_b2"), v(L, "f_freq", 1))
            for n in range(2):
                dve.wait_ge(sig("filter_taps"), 2 * L + n + 1)
                if n == 1:
                    dve.wait_ge(sig("filter_spectrum"), 4 * L + 2)
                for t in range(2):
                    dve.tensor_tensor(TAP(0, t), ps[2 * t][:, :], window[:, t, :], ALU.mult)
                    if t == 0:
                        dve.scalar_tensor_tensor(TAP(1, t), ps[2 * t + 1][:, :], con("not0"), window[:, t, :],
                                                 ALU.mult, ALU.mult)
                    else:
                        dve.tensor_tensor(TAP(1, t), ps[2 * t + 1][:, :], window[:, t, :], ALU.mult)
                dve.drain().then_inc(sig("filter_windowed"), 1)
                dve.wait_ge(sig("filter_root"), 2 * L + n + 1)
                for t in range(2):
                    dve.tensor_tensor(scr[:, 3, :], TAP(0, t), TAP(1, t), ALU.add)
                    dve.tensor_tensor(TAP(1, t), TAP(0, t), TAP(1, t), ALU.subtract)
                    dve.drain()
                    dve.tensor_tensor(FOLD(0, t), scr[:, 3, :], scr[:, 2, :], ALU.mult)
                    dve.tensor_tensor(FOLD(1, t), TAP(1, t), scr[:, 2, :], ALU.mult)
                    dve.drain()
                dve.drain().then_inc(sig("filter_folded"), 1)
                dve.wait_ge(sig("filter_spectrum_out"), 4 * L + 2 * n + 2)
                dve.tensor_scalar(KS(n, 0), KS(n, 0), con("not0"), None, ALU.mult)
            dve.drain()

        def scalar_filters(act, L, book):
            for i in range(2):
                act.wait_ge(sig("filter_angle"), 2 * L + i + 1)
                act.activation(HA(i), HA(i), ACT.Sin).then_inc(sig("filter_sine"), 1)
            for n in range(2):
                act.wait_ge(sig("filter_windowed"), 2 * L + n + 1)
                if n == 1:
                    act.wait_ge(sig("filter_energy"), 2 * L + 1)
                for i in range(4):
                    act.activation(SQ(i), regA[:, 10 + i, :], ACT.Square)
                act.drain().then_inc(sig("filter_squares"), 1)
                act.wait_ge(sig("filter_energy"), 2 * L + n + 1)
                act.activation(scr[:, 2, :], ps[4][:, :], ACT.Ln, bias=eps_col[:, :])
                act.drain()
                act.activation(scr[:, 2, :], scr[:, 2, :], ACT.Exp, scale=-0.5)
                act.drain().then_inc(sig("filter_root"), 1)
                act.wait_ge(sig("filter_spectrum"), 4 * L + 2 * n + 1)
                act.activation(KRE(n, 0), ps[5][:, :], ACT.Copy)
                act.activation(KRE(n, 1), ps[6][:, :], ACT.Copy)
                act.activation(KRB(n), ps[7][:, :], ACT.Copy)
                act.drain().then_inc(sig("filter_spectrum_out"), 1)
                act.wait_ge(sig("filter_spectrum"), 4 * L + 2 * n + 2)
                act.activation(KS(n, 0), ps[5][:, :], ACT.Copy)
                act.activation(KS(n, 1), ps[6][:, :], ACT.Copy)
                act.drain().then_inc(sig("filter_spectrum_out"), 1)

        units_hy = lambda L: [(n, s) for n in range(2) for s in range(lo(L) // SEG, 2)]

        def tensor_hyena(pe, L, book):
            b = book.base("hyena", len(units_hy(L)))
            for u, (n, s) in enumerate(units_hy(L)):
                if u >= 1:
                    pe.wait_ge(sig("hyena_gated"), b + u)
                for t in range(2):
                    for j in range(4):
                        last = pe.transpose(ps[t][:, P * j:P * j + P],
                                            regB[:, j, SEG * s + P * t:SEG * s + P * t + P], ident)
                last.then_inc(sig("hyena_turned"), 1)
                pe.wait_ge(sig("hyena_turned_out"), b + u + 1)
                for f in range(2):
                    for t in range(2):
                        pe.matmul(ps[2 + f][:, :], dft_c[:, t, P * f:P * f + P], ZT(t), start=(t == 0), stop=(t == 1))
                for f in range(2):
                    for t in range(2):
                        last = pe.matmul(ps[4 + f][:, :], dft_s[:, t, P * f:P * f + P], ZT(t), start=(t == 0),
                                         stop=(t == 1))
                last.then_inc(sig("hyena_spectrum"), 1)
                pe.wait_ge(sig("hyena_product"), b + u + 1)
                for j in range(4):
                    o = ps[6 + j // 2][:, SEG * (j % 2):SEG * (j % 2) + SEG]
                    for f in range(2):
                        pe.matmul(o, YR(f)[:, P * j:P * j + P], inv_c[:, f, :], start=(f == 0), stop=False)
                    for f in range(2):
                        last = pe.matmul(o, YS(f)[:, P * j:P * j + P], inv_s[:, f, :], start=False, stop=(f == 1))
                last.then_inc(sig("hyena_conv"), 1)

        def scalar_hyena(act, L, book):
            b = book.base("hyena", len(units_hy(L)))
            for u, (n, s) in enumerate(units_hy(L)):
                act.wait_ge(sig("hyena_turned"), b + u + 1)
                for t in range(2):
                    act.activation(ZT(t), ps[t][:, :], ACT.Copy)
                act.drain().then_inc(sig("hyena_turned_out"), 1)

        def vector_hyena(dve, L, book):
            b = book.base("hyena", len(units_hy(L)))
            for u, (n, s) in enumerate(units_hy(L)):
                dve.wait_ge(sig("hyena_spectrum"), b + u + 1)
                for f in range(2):
                    kb = KRB(n) if f == 0 else KRE(n, 1)
                    dve.tensor_tensor(YR(f), ps[2 + f][:, :], KRE(n, f), ALU.mult)
                    dve.tensor_tensor(YS(f), ps[2 + f][:, :], KS(n, f), ALU.mult)
                    dve.tensor_tensor(scr[:, 2 * f, :], ps[4 + f][:, :], KS(n, f), ALU.mult)
                    dve.tensor_tensor(scr[:, 2 * f + 1, :], ps[4 + f][:, :], kb, ALU.mult)
                dve.drain()
                for f in range(2):
                    dve.tensor_tensor(YR(f), YR(f), scr[:, 2 * f, :], ALU.subtract)
                    dve.tensor_tensor(YS(f), YS(f), scr[:, 2 * f + 1, :], ALU.add)
                dve.drain().then_inc(sig("hyena_product"), 1)
                dve.wait_ge(sig("hyena_conv"), b + u + 1)
                sl = slice(SEG * s, SEG * s + SEG)
                for j in range(4):
                    z = regB[:, j, sl]
                    dve.scalar_tensor_tensor(z, z, v(L, "hy_bias", 4 * n + j),
                                             ps[6 + j // 2][:, SEG * (j % 2):SEG * (j % 2) + SEG], ALU.mult, ALU.add)
                dve.drain()
                for j in range(4):
                    z = regB[:, j, sl]
                    dst = z if n == 0 else Y[:, 12 + j, sl]
                    dve.tensor_tensor(dst, z, regB[:, 4 * (n + 1) + j, sl], ALU.mult)
                dve.drain().then_inc(sig("hyena_gated"), 1)

        merged = lambda j: AR[:, A0 + 512 * j:A0 + 512 * j + 512]
        MG_UNITS = [(jj, n, half) for jj in range(4) for n in range(4) for half in range(2)]

        def tensor_merge(pe, L, book):
            b, t0 = book.base("merge", 32), lo(L)
            for i2 in range(16):
                jj, n = i2 // 4, i2 % 4
                mg, mb = merge_m[L][i2]
                for m, width in ((mg, KT), (mb, 4)):
                    arrived(pe, m)
                    for half in range(2):
                        i = 2 * i2 + half
                        if i >= 3:
                            pe.wait_ge(sig("merged"), b + i - 2)
                        bank = ps[i % 3 if m == mg else 3 + i % 3]
                        for k in range(width):
                            rhs = hT[:, k, t0:] if m == mg else Y[:, 4 * n + k, t0:]
                            last = pe.matmul(bank[:, t0:], slot(m, width, 256)[:, k, P * half:P * half + P], rhs,
                                             start=(k == 0), stop=(k == width - 1))
                        last.then_inc(sig("merge_gate" if m == mg else "merge_branch"), 1)
                    pe.drain().then_inc(sig("chunk_used"), 1)
                if L + 1 < DEPTH:
                    tensor_ada(pe, L + 1, range(3 * i2 // 2, 3 * (i2 + 1) // 2), ps[6])

        def scalar_merge(act, L, book):
            b, t0 = book.base("merge", 32), lo(L)
            for i in range(32):
                act.wait_ge(sig("merge_gate"), b + i + 1)
                if i >= 3:
                    act.wait_ge(sig("merged"), b + i - 2)
                act.activation(scr[:, i % 3, t0:], ps[i % 3][:, t0:], ACT.Sigmoid).then_inc(sig("merge_sigmoid"), 1)
                if i % 2 == 1 and L + 1 < DEPTH:
                    scalar_ada(act, L + 1, range(3 * (i // 2) // 2, 3 * (i // 2 + 1) // 2))

        def vector_merge(dve, L, book):
            b, t0 = book.base("merge", 32), lo(L)
            for i, (jj, n, half) in enumerate(MG_UNITS):
                dve.wait_ge(sig("merge_sigmoid"), b + i + 1)
                dve.wait_ge(sig("merge_branch"), b + i + 1)
                m, g = merged(2 * jj + half)[:, t0:], scr[:, i % 3, t0:]
                if n == 0:
                    dve.tensor_tensor(m, g, ps[3 + i % 3][:, t0:], ALU.mult)
                else:
                    dve.tensor_tensor(g, g, ps[3 + i % 3][:, t0:], ALU.mult)
                    dve.drain()
                    dve.tensor_tensor(m, m, g, ALU.add)
                dve.drain().then_inc(sig("merged"), 1)

        def tensor_out(pe, L, book):
            b, t0 = book.base("out", 8), lo(L)
            for j in range(8):
                m = wout_m[L][j // 2]
                arrived(pe, m)
                if j >= 4:
                    pe.wait_ge(sig("residual_added"), b + j - 3)
                for k in range(KT):
                    last = pe.matmul(ps[j % 4][:, t0:], slot(m, KT, 256)[:, k, P * (j % 2):P * (j % 2) + P],
                                     merged(k)[:, t0:], start=(k == 0), stop=(k == KT - 1))
                last.then_inc(sig("out_projected"), 1)
                if j % 2 == 1:
                    pe.drain().then_inc(sig("chunk_used"), 1)

        def vector_out(dve, L, book):
            b = book.base("out", 8)
            for j in range(8):
                dve.wait_ge(sig("out_projected"), b + j + 1)
                for s in range(lo(L) // SEG, 2):
                    x = XT[:, j, SEG * s:SEG * s + SEG]
                    dve.scalar_tensor_tensor(x, ps[j % 4][:, SEG * s:SEG * s + SEG], mods[:, L, 16 + j, s:s + 1], x,
                                             ALU.mult, ALU.add)
                dve.drain().then_inc(sig("residual_added"), 1)

        work = scr[:, :, :].rearrange("p a t -> p (a t)")
        wk = lambda o, *shape: work[:, o:o + int(np.prod(shape))]
        iota32 = con("iota32")

        def tensor_router(pe, L):
            tiles_ = range(lo(L) // P, TT)
            for t in tiles_:
                for k in range(KT):
                    last = pe.matmul(ps[4][:, 36 * t:36 * t + 36], hT[:, k, P * t:P * t + P], rw[:, L, k, :],
                                     start=(k == 0), stop=(k == KT - 1))
            last.then_inc(sig("router_logits"), 1)
            pe.wait_ge(sig("experts_chosen"), L + 1)
            for t in tiles_:
                pe.matmul(ps[5][:, 32 * t:32 * t + 32], con("upper"), both[:, t, :], start=True,
                          stop=(t == tiles_[0]))
                for e in range(tiles_[0], t):
                    pe.matmul(ps[5][:, 32 * t:32 * t + 32], ones, both[:, e, :], start=False, stop=(e == t - 1))
            for t in tiles_:
                last = pe.matmul(ps[6][:, 0:32], ones, both[:, t, :], start=(t == tiles_[0]), stop=(t == TT - 1))
            last.then_inc(sig("experts_counted"), 1)
            pe.wait_ge(sig("places_hot"), L + 1)
            for t in tiles_:
                for c in range(2):
                    last = pe.matmul(ps[7][:, 0:3 * NBT], hot_slot(t, c), hot_blk(t, c),
                                     start=(t == tiles_[0] and c == 0), stop=(t == TT - 1 and c == 1))
            last.then_inc(sig("slot_rows"), 1)

        def scalar_router(act, L):
            act.wait_ge(sig("group_margins"), L + 1)
            act.activation(wk(0, 16), wk(0, 16), ACT.Exp).then_inc(sig("group_exps"), 1)
            act.wait_ge(sig("expert_margin"), L + 1)
            act.activation(wk(16, 4), wk(16, 4), ACT.Exp).then_inc(sig("expert_exp"), 1)

        both = pend
        hot_slot = lambda t, c: AR[:, B0 + 1024 + P * (2 * t + c):B0 + 1024 + P * (2 * t + c) + P]
        hot_blk = lambda t, c: AR[:, B0 + 2048 + 3 * NBT * (2 * t + c):B0 + 2048 + 3 * NBT * (2 * t + c + 1)]

        def vector_router(dve, L):
            z = lo(L) // P
            n4 = 4 - z

            def rows_of(o, *shape):
                w = wk(o, 4, *shape).rearrange("p (t n) -> p t n", t=4)
                return w[:, z:, :]

            def first_hot(vals, n, m_o, hot):
                mx = rows_of(m_o, 1)
                dve.tensor_reduce(mx, vals, AXX, ALU.max)
                dve.drain()
                eq = rows_of(1900, n)
                dve.tensor_tensor(eq, vals, mx.to_broadcast([P, n4, n]), ALU.is_equal)
                dve.drain()
                dve.scalar_tensor_tensor(eq, eq, -100.0, iota32[:, 0:n].unsqueeze(1).to_broadcast([P, n4, n]),
                                         ALU.mult, ALU.add)
                dve.drain()
                mi = rows_of(1990, 1)
                dve.tensor_reduce(mi, eq, AXX, ALU.min)
                dve.drain()
                dve.tensor_tensor(hot, eq, mi.to_broadcast([P, n4, n]), ALU.is_equal)
                dve.drain()

            dve.wait_ge(sig("router_logits"), L + 1)
            dve.tensor_tensor(rt[:, z:, :], ps[4][:, 36 * z:144].rearrange("p (t n) -> p t n", n=36),
                              rb[:, L, :].unsqueeze(1).to_broadcast([P, n4, 36]), ALU.add)
            dve.drain()
            hg = rows_of(40, 4)
            first_hot(rt[:, z:, 0:4], 4, 32, hg)
            gm = rows_of(0, 4)
            dve.memset(wk(0, 20), 0.0)
            dve.drain()
            dve.tensor_tensor(gm, rt[:, z:, 0:4], rows_of(32, 1).to_broadcast([P, n4, 4]), ALU.subtract)
            dve.drain().then_inc(sig("group_margins"), 1)
            el = rows_of(64, 32).rearrange("p t (g e) -> p t g e", g=4)
            dve.tensor_tensor(el, rt[:, z:, 4:36].rearrange("p t (g e) -> p t g e", g=4),
                              hg.unsqueeze(3).to_broadcast([P, n4, 4, 8]), ALU.mult)
            dve.drain()
            ein = rows_of(192, 8)
            dve.tensor_reduce(ein, rows_of(64, 32).rearrange("p t (g e) -> p t e g", g=4), AXX, ALU.add)
            dve.drain()
            h1, h2, e2 = rows_of(224, 8), rows_of(256, 8), rows_of(288, 8)
            first_hot(ein, 8, 320, h1)
            dve.tensor_scalar(e2, h1, -2.0e38, 1.0e38, ALU.mult, ALU.add)
            dve.drain()
            dve.tensor_tensor(e2, e2, ein, ALU.min)
            dve.drain()
            first_hot(e2, 8, 324, h2)
            dve.tensor_tensor(rows_of(16, 1), rows_of(324, 1), rows_of(320, 1), ALU.subtract)
            dve.drain().then_inc(sig("expert_margin"), 1)
            for c, h in ((0, h1), (1, h2)):
                for t in range(n4):
                    dve.tensor_tensor(oh[:, z + t, c, :].rearrange("p (g e) -> p g e", g=4),
                                      hg[:, t, :].unsqueeze(2).to_broadcast([P, 4, 8]),
                                      h[:, t, :].unsqueeze(1).to_broadcast([P, 4, 8]), ALU.mult)
            dve.drain()
            dve.tensor_tensor(both[:, z:, :], oh[:, z:, 0, :], oh[:, z:, 1, :], ALU.add)
            dve.drain().then_inc(sig("experts_chosen"), 1)
            dve.wait_ge(sig("group_exps"), L + 1)
            dve.wait_ge(sig("expert_exp"), L + 1)
            dve.tensor_reduce(rows_of(328, 1), gm, AXX, ALU.add)
            dve.tensor_scalar(rows_of(332, 1), rows_of(16, 1), 1.0, None, ALU.add)
            dve.drain()
            dve.tensor_tensor(rows_of(328, 1), rows_of(328, 1), rows_of(332, 1), ALU.mult)
            dve.drain()
            dve.reciprocal(gate[:, z:, 0:1], rows_of(328, 1))
            dve.drain()
            dve.tensor_tensor(gate[:, z:, 1:2], gate[:, z:, 0:1], rows_of(16, 1), ALU.mult)
            dve.wait_ge(sig("experts_counted"), L + 1)
            nb, ends, st = wk(372, 32), wk(404, 32), wk(436, 32)
            dve.tensor_scalar(nb, ps[6][:, 0:32], 0.0, None, ALU.is_gt)
            pos, blk = rows_of(500, 32), rows_of(640, 32)
            dve.tensor_copy(pos, ps[5][:, 32 * z:128].rearrange("p (t e) -> p t e", e=32))
            dve.drain()
            dve.tensor_scalar(blk, pos, float(P), None, ALU.is_ge)
            for j in range(1, 4):
                dve.scalar_tensor_tensor(nb, ps[6][:, 0:32], float(P * j), nb, ALU.is_gt, ALU.add)
                dve.drain()
                if j > 1:
                    dve.scalar_tensor_tensor(blk, pos, float(P * j), blk, ALU.is_ge, ALU.add)
                    dve.drain()
            dve.scalar_tensor_tensor(pos, blk, -float(P), pos, ALU.mult, ALU.add)
            dve.tensor_tensor_scan(ends, nb, nb, 0.0, ALU.add, ALU.bypass)
            dve.drain()
            dve.tensor_tensor(st, ends, nb, ALU.subtract)
            dve.drain()
            dve.tensor_tensor(blk, blk, st.unsqueeze(1).to_broadcast([P, n4, 32]), ALU.add)
            dve.drain()
            for i, val in ((0, pos), (1, blk)):
                for c in range(2):
                    w = rows_of(800, 32)
                    dve.tensor_tensor(w, oh[:, z:, c, :], val, ALU.mult)
                    dve.drain()
                    dve.tensor_reduce(place[:, i, z:, c:c + 1], w, AXX, ALU.add)
                    dve.drain()
            iota_blk = con("iota_blk")
            tok_id, row_id = con("tok_id"), con("row_id")
            for t in range(z, 4):
                for c in range(2):
                    sl, bk = place[:, 0, t, c:c + 1], place[:, 1, t, c:c + 1]
                    hb = hot_blk(t, c)
                    dve.tensor_scalar(hot_slot(t, c), con("slots"), sl, None, ALU.is_equal)
                    dve.tensor_scalar(hb[:, 0:NBT], iota_blk, bk, tok_id[:, t - z:t - z + 1], ALU.is_equal, ALU.mult)
                    dve.tensor_scalar(hb[:, NBT:2 * NBT], iota_blk, bk, row_id[:, 2 * (t - z) + c:2 * (t - z) + c + 1],
                                      ALU.is_equal, ALU.mult)
                    dve.tensor_scalar(hb[:, 2 * NBT:3 * NBT], iota_blk, bk, None, ALU.is_equal)
            dve.drain().then_inc(sig("places_hot"), 1)
            cmp_ = AR[:, B0 + 4096:B0 + 4096 + NBT * 32].rearrange("p (b e) -> p b e", b=NBT)
            dve.tensor_tensor(cmp_, ends.unsqueeze(1).to_broadcast([P, NBT, 32]),
                              iota_blk.unsqueeze(2).to_broadcast([P, NBT, 32]), ALU.is_le)
            dve.drain()
            tf = wk(1000, NBT + 1)
            pr = wk(1100, NBT)
            dve.tensor_reduce(tf[:, 0:NBT], cmp_, AXX, ALU.add)
            dve.tensor_scalar(pr, iota_blk, 2.0, ends[:, 31:32], ALU.mult, ALU.is_lt)
            dve.drain()
            dve.tensor_scalar(tf[:, 0:NBT], tf[:, 0:NBT], float(E - 1), None, ALU.min)
            dve.tensor_reduce(tf[:, NBT:NBT + 1], pr, AXX, ALU.add)
            dve.drain()
            dve.tensor_copy(tab[:, :], tf)
            dve.wait_ge(sig("slot_rows"), L + 1)
            far = wk(1200, NBT)
            dve.tensor_scalar(far, ps[7][:, 2 * NBT:3 * NBT], -FAR, FAR, ALU.mult, ALU.add)
            dve.drain()
            for i, idx in ((0, gidx), (1, sidx)):
                r = wk(1300 + 100 * i, NBT)
                dve.tensor_tensor(r, ps[7][:, NBT * i:NBT * i + NBT], far, ALU.add)
                dve.drain()
                dve.tensor_copy(idx[:, :], r)
            dve.drain().then_inc(sig("moe_tables"), 1)

        part = [(0, KT), (4096, KT), (8192, 4)]
        wexp = lambda h, j: AR[:, 12288 * h + part[j][0]:12288 * h + part[j][0] + 4096]\
            .rearrange("p (k n) -> p k n", k=part[j][1])
        act_t = scr[:, 2, :]
        hid_t = scr[:, 3, :]
        xrow = lambda h: Yf[:, 1024 * h:1024 * h + 1024]
        xe = lambda h: Yf[:, 4096 + 1024 * h:5120 + 1024 * h].rearrange("p (k s) -> p k s", k=KT)
        yb = lambda h: Yf[:, 6144 + 1024 * h:7168 + 1024 * h]
        names = ("w_gate", "w_up", "w_down")

        def pairs(e, L):
            e.wait_ge(sig("moe_tables"), L + 1)
            return e.value_load(tab[0:1, NBT:NBT + 1], min_val=1, max_val=MAXBLK // 2)

        def lk(name, L):
            return sig(f"{name}_layer{L}")

        def sync_moe(sp, L):
            n = pairs(sp, L)
            with sp.Fori(0, n) as i:
                for h in range(2):
                    e = sp.value_load(tab[0:1, bass.ds(2 * i + h, 1)], min_val=0, max_val=E - 1)
                    for j, name in enumerate(names):
                        sp.wait_ge(lk("gate_up" if j < 2 else "down", L), 2 * i + (h + 1))
                        src = a["moe_" + name][L][bass.ds(e, 1), :, :]
                        src = src.rearrange("o (k p) n -> p (o k) n", p=P)
                        sp.dma_start(wexp(h, j), src).then_inc(lk(f"{name}_{h}_loaded", L), 16)

        def tensor_moe(pe, L):
            n = pairs(pe, L)
            pe.drain().then_inc(lk("gate_up", L), 2)
            pe.drain().then_inc(lk("down", L), 2)

            def turn_rows(n_loaded, h):
                pe.wait_ge(lk(f"rows_{h}_loaded", L), n_loaded)
                for k in range(KT):
                    last = pe.transpose(ps[k // 4][:, P * (k % 4):P * (k % 4) + P], xrow(h)[:, P * k:P * k + P],
                                        ident)
                last.then_inc(lk("rows_turned", L), 1)

            turn_rows(16, 0)
            with pe.Fori(0, n) as i:
                for h in range(2):
                    b = 2 * i + h
                    pe.wait_ge(lk("turned_out", L), b + 1)
                    for j in range(2):
                        pe.wait_ge(lk(f"{names[j]}_{h}_loaded", L), 16 * i + 16)
                        for k in range(KT):
                            last = pe.matmul(ps[2 + j][:, :], xe(h)[:, k, :], wexp(h, j)[:, k, :],
                                             start=(k == 0), stop=(k == KT - 1))
                    last.then_inc(lk("gate_up", L), 1)
                    turn_rows(16 * i + 16 * (h + 1), 1 - h)
                    pe.wait_ge(lk("hidden", L), b + 1)
                    for k in range(4):
                        last = pe.transpose(ps[4][:, P * k:P * k + P], act_t[:, P * k:P * k + P], ident)
                    last.then_inc(lk("hidden_turned", L), 1)
                    pe.wait_ge(lk("hidden_out", L), b + 1)
                    pe.wait_ge(lk("w_down_%d_loaded" % h, L), 16 * i + 16)
                    pe.wait_ge(lk("output_copied", L), 2 * b + 2)
                    for c in range(2):
                        for k in range(4):
                            last = pe.matmul(ps[5 + c][:, :], hid_t[:, P * k:P * k + P],
                                             wexp(h, 2)[:, k, 512 * c:512 * c + 512], start=(k == 0), stop=(k == 3))
                    last.then_inc(lk("down", L), 1)

        def scalar_moe(act, L):
            n = pairs(act, L)
            act.drain().then_inc(lk("output_copied", L), 1)

            def take(b, h):
                act.wait_ge(lk("rows_turned", L), b + 1)
                for c in range(2):
                    act.activation(xe(h)[:, 4 * c:4 * c + 4, :],
                                   ps[c][:, :].rearrange("p (k s) -> p k s", k=4), ACT.Copy)
                act.drain().then_inc(lk("turned_out", L), 1)

            take(0, 0)
            with act.Fori(0, n) as i:
                for h in range(2):
                    b = 2 * i + h
                    act.wait_ge(lk("gate_up", L), b + 3)
                    act.activation(act_t, ps[2][:, :], ACT.Silu).then_inc(lk("silu", L), 1)
                    take(b + 1, 1 - h)
                    act.wait_ge(lk("hidden_turned", L), b + 1)
                    act.activation(hid_t, ps[4][:, :], ACT.Copy).then_inc(lk("hidden_out", L), 1)
                    act.wait_ge(lk("down", L), b + 3)
                    act.wait_ge(lk(f"output_{h}_written", L), 16 * i + 16)
                    act.activation(yb(h)[:, 0:512], ps[5][:, :], ACT.Copy).then_inc(lk("output_copied", L), 1)

        def vector_moe(dve, L):
            n = pairs(dve, L)
            dve.drain().then_inc(lk("output_copied", L), 1)
            with dve.Fori(0, n) as i:
                for h in range(2):
                    b = 2 * i + h
                    dve.wait_ge(lk("silu", L), b + 1)
                    dve.tensor_tensor(act_t, act_t, ps[3][:, :], ALU.mult).then_inc(lk("hidden", L), 1)
                    dve.wait_ge(lk("down", L), b + 3)
                    dve.wait_ge(lk(f"output_{h}_written", L), 16 * i + 16)
                    dve.tensor_copy(yb(h)[:, 512:1024], ps[6][:, :]).then_inc(lk("output_copied", L), 1)

        def pool_moe(pool, L):
            n = pairs(pool, L)
            pool.wait_ge(sig("rows_in_dram"), 16 * (L + 1))
            for h in range(2):
                pool.dma_start(yb(h)[0:1, :], hrows[L][0:1, :]).then_inc(lk(f"output_{h}_written", L), 16)
            last_token = pool.to_reg(T - lo(L) - 1)
            last_output = pool.to_reg(2 * (T - lo(L)) - 1)

            def gather(b, h):
                pool.tensor_copy(gi[:, h:h + 1], gidx[:, b])
                pool.drain()
                pool.indirect_dma_start(out=xrow(h), out_offset=None, in_=hrows[L],
                                        in_offset=bass.IndirectOffsetOnAxis(ap=gi[:, h:h + 1], axis=0),
                                        bounds_check=last_token, oob_is_err=False)\
                    .then_inc(lk(f"rows_{h}_loaded", L), 16)

            for b in range(3):
                if b == 2:
                    pool.wait_ge(lk("rows_turned", L), 1)
                gather(slice(b, b + 1), b % 2)
            with pool.Fori(0, n) as i:
                for h in range(2):
                    b = 2 * i + h
                    pool.wait_ge(lk("rows_turned", L), b + 2)
                    pool.sem_inc(lk("pool_steps", L), 1)
                    gather(bass.ds(b + 3, 1), 1 - h)
                    pool.wait_ge(lk("output_copied", L), 2 * b + 4)
                    pool.sem_inc(lk("pool_steps", L), 1)
                    pool.tensor_copy(si[:, h:h + 1], sidx[:, bass.ds(b, 1)])
                    pool.drain()
                    pool.indirect_dma_start(out=yrows[L],
                                            out_offset=bass.IndirectOffsetOnAxis(ap=si[:, h:h + 1], axis=0),
                                            in_=yb(h), in_offset=None, bounds_check=last_output, oob_is_err=False)\
                        .then_inc(lk(f"output_{h}_written", L), 16)
            for h in range(2):
                pool.wait_ge(lk(f"output_{h}_written", L), 16 * n + 16)
            pool.sem_inc(lk("pool_steps", L), 1)
            z = lo(L) // P
            pool.dma_start(rowsA[:, z:, :, :],
                           yrows[L].rearrange("(t p c) n -> p t c n", p=P, c=2))\
                .then_inc(sig("rows_gathered"), 16)

        def vector_combine(dve, L):
            dve.wait_ge(sig("rows_gathered"), 16 * (L + 1))
            for t in range(lo(L) // P, 4):
                dve.tensor_scalar(rowsA[:, t, 0, :], rowsA[:, t, 0, :], gate[:, t, 0:1], None, ALU.mult)
            dve.drain()
            for t in range(lo(L) // P, 4):
                dve.scalar_tensor_tensor(rowsB[:, t, :], rowsA[:, t, 1, :], gate[:, t, 1:2], rowsA[:, t, 0, :],
                                         ALU.mult, ALU.add)
            dve.drain().then_inc(sig("rows_combined"), 1)

        def tensor_combine(pe, L, book):
            pe.wait_ge(sig("rows_combined"), L + 1)
            g0 = 2 * (lo(L) // P)
            b = book.base("combine", 8 - g0) - g0
            for g in range(g0, 8):
                if g >= g0 + 4:
                    pe.wait_ge(sig("combined_added"), b + g - 3)
                for i in range(4):
                    last = pe.transpose(ps[g % 4][:, P * i:P * i + P], rows_src(rowsB)(g, i), ident)
                last.then_inc(sig("combined_turned"), 1)

        def vector_combine_add(dve, L, book):
            g0 = 2 * (lo(L) // P)
            b = book.base("combine", 8 - g0) - g0
            for g in range(g0, 8):
                dve.wait_ge(sig("combined_turned"), b + g + 1)
                t, kg = g // 2, g % 2
                for i in range(4):
                    k = 4 * kg + i
                    x = XT[:, k, P * t:P * t + P]
                    dve.scalar_tensor_tensor(x, ps[g % 4][:, P * i:P * i + P], mods[:, L, 40 + k, t // 2:t // 2 + 1],
                                             x, ALU.mult, ALU.add)
                dve.drain().then_inc(sig("combined_added"), 1)

        def load_vectors(eng, L, done):
            n = 0

            def load(dst, src):
                nonlocal n
                eng.dma_start(dst, src).then_inc(sig(done), 16)
                n += 1

            def at(name, i, k):
                o = V1[name] + i
                return (vrow[o:o + k, L, 0, :] if o < N1 else vrow[o - N1:o - N1 + k, L, 1, :])

            fold = lambda x: x.rearrange("(k p) -> k p", p=P)
            row = lambda x: x.rearrange("(o n) -> o n", o=1)
            load(at("b_ada", 0, 48), fold(a["b_ada"][L]))
            load(at("norm1", 0, 8), fold(a["norm1_g"][L]))
            load(at("norm2", 0, 8), fold(a["norm2_g"][L]))
            load(at("ml_conv", 0, 24), a["ml_conv_w"][L].rearrange("j (k p) -> (j k) p", p=P))
            load(at("ml_convb", 0, 8), fold(a["ml_conv_b"][L]))
            load(at("hy_conv", 0, 36), a["hy_conv_w"][L].rearrange("j (k p) -> (j k) p", p=P))
            load(at("hy_convb", 0, 12), fold(a["hy_conv_b"][L]))
            load(at("hy_bias", 0, 8), a["hy_bias"][L].rearrange("j (k p) -> (j k) p", p=P))
            load(at("diff_norm", 0, 1), row(a["diff_norm_g"][L]))
            load(at("ml_norm", 0, 1), row(a["ml_norm_g"][L]))
            for half in range(2):
                load(at("gq_norm", 0, 1)[:, 64 * half:64 * half + 64], row(a["gqa_qnorm_g"][L]))
                load(at("gk_norm", 0, 1)[:, 64 * half:64 * half + 64], row(a["gqa_knorm_g"][L]))
            load(at("f_b1", 0, 1)[:, 0:64], row(a["hy_f_b1"][L]))
            load(at("f_b2", 0, 1)[:, 0:64], row(a["hy_f_b2"][L]))
            load(at("f_freq", 0, 2)[:, 0:64], a["hy_f_freq"][L])
            load(at("final", 0, 8), fold(a["final_norm_g"]))
            for kind in range(2):
                for d in range(2):
                    c0 = MG + 8 * d + 4 * kind
                    load(gw[:, L, :, kind, d, :], a["w_in"][L, :, c0:c0 + 4].rearrange("(k p) n -> p k n", p=P))
                    load(gb[4 * d:4 * d + 4, L, kind:kind + 1],
                         a["ml_gate_b"][L, d, kind, :].rearrange("(h o) -> h o", o=1))
            load(lam4[:, L, :], a["diff_lam"][L].rearrange("j n -> n j"))
            load(w12[0:33, L, 0:64], a["hy_f_w1"][L])
            load(w12[:, L, 64:128], a["hy_f_w2"][L])
            load(rw[:, L, :, 0:4], a["moe_w_group"][L].rearrange("(k p) n -> p k n", p=P))
            load(rw[:, L, :, 4:36], a["moe_w_router"][L].rearrange("(k p) n -> p k n", p=P))
            load(rb[:, L, 0:4], a["moe_b_group"][L].partition_broadcast(P))
            load(rb[:, L, 4:36], a["moe_b_router"][L].partition_broadcast(P))
            return n

        def tensor_vectors(pe, L, bank):
            pe.wait_ge(sig(f"vectors_loaded_{L}"), 16 * n_loads)
            pe.transpose(bank[:, 0:N1], vrow[0:N1, L, 0, :], ident[0:N1, 0:N1])
            pe.transpose(bank[:, 128:128 + N2], vrow[0:N2, L, 1, :], ident[0:N2, 0:N2])\
              .then_inc(sig("vectors_turned"), 1)

        def scalar_vectors(act, L, bank):
            act.wait_ge(sig("vectors_turned"), L + 1)
            act.activation(vecs[:, L, 0:N1], bank[:, 0:N1], ACT.Copy)
            act.activation(vecs[:, L, N1:N1 + N2], bank[:, 128:128 + N2], ACT.Copy)

        @block.sync
        def _(sp):
            sp.dma_start(C[:, :], a["constants"]).then_inc(sig("inputs"), 16)
            sp.dma_start(rowsY[:, 0:2, :], a["ctx"][0].rearrange("(t p) n -> p t n", p=P)).then_inc(sig("inputs"), 16)
            sp.dma_start(rowsY[:, 2:4, :], a["x"][0].rearrange("(t p) n -> p t n", p=P)).then_inc(sig("inputs"), 16)

            def stream(lo_, hi):
                for m in range(lo_, hi):
                    fills, at_slot, before = chunks[m]
                    if m in ada_m[1]:
                        for who in ("tensor", "scalar", "vector"):
                            sp.wait_ge(sig(f"{who}_ended_stage"), 16)
                    if before is not None:
                        sp.wait_ge(sig("chunk_used"), before + 1)
                    for dst, src in fills:
                        sp.dma_start(dst(m), src).then_inc(sig(f"chunk_in_slot_{at_slot}"), 16)

            at = 0
            for L in range(DEPTH):
                stream(at, layer_end_chunk[L] + 1)
                at = layer_end_chunk[L] + 1
                sp.wait_ge(sig("chunk_used"), at)
                sync_moe(sp, L)
                if L + 1 < DEPTH:
                    sp.wait_ge(sig("tensor_left_experts"), L + 1)
            sp.wait_ge(sig("final_rows"), 1)
            sp.dma_start(out[0].rearrange("(t p) n -> p t n", p=P), rowsY[:, 2:4, :]).then_inc(sig("written"), 16)
            sp.wait_ge(sig("written"), 16)

        n_loads = 33

        @block.gpsimd
        def _(pool):
            pool.memset(vrow[:, :, :, :], 0.0)
            pool.memset(eps_col[:, :], EPS)
            pool.drain().then_inc(sig("rows_cleared"), 1)
            pool.wait_ge(sig("rows_cleared"), 1)
            for L in range(1, DEPTH):
                assert load_vectors(pool, L, f"vectors_loaded_{L}") == n_loads
            for L in range(DEPTH):
                pool_moe(pool, L)

        df_rope = lambda: [regA[:, j, :] for j in range(8)]
        gq_rope = lambda: [regB[:, j, :] for j in range(6)]
        hidden_src = lambda g, i: hT[:, 4 * (g % 2) + i, P * (g // 2):P * (g // 2) + P]

        @block.tensor
        def _(pe):
            book, me = Book(), "tensor"
            pe.wait_ge(sig("inputs"), 48)
            pe.wait_ge(sig("conditioning"), 32)
            pe.transpose(ps[4][:, 0:16], crow[:, :], ident[0:16, 0:16]).then_inc(sig("conditioning_turned"), 1)
            tensor_turn(pe, book, rows_src(rowsY))
            pe.wait_ge(sig("conditioned"), 1)
            tensor_ada(pe, 0, range(24), ps[5])
            tensor_vectors(pe, 0, ps[6])
            meet(pe, me, book)
            for L in range(DEPTH):
                t0 = lo(L)
                tensor_rms(pe, book)
                meet(pe, me, book)
                tensor_project(pe, L, "ml")
                tensor_gates(pe, L)
                tensor_gate_columns(pe, L)
                meet(pe, me, book)
                tensor_mlstm(pe, L, book)
                meet(pe, me, book)
                tensor_headnorm(pe, book, [T - t0] * 4, ones)
                meet(pe, me, book)
                tensor_project(pe, L, "hy")
                meet(pe, me, book)
                tensor_filters(pe, L, book)
                meet(pe, me, book)
                tensor_hyena(pe, L, book)
                meet(pe, me, book)
                tensor_project(pe, L, "df")
                meet(pe, me, book)
                tensor_rope(pe, book, df_rope())
                tensor_lambda(pe, L)
                meet(pe, me, book)
                tensor_attention(pe, "df", L, book)
                meet(pe, me, book)
                tensor_headnorm(pe, book, [T - t0] * 4, ones)
                meet(pe, me, book)
                tensor_project(pe, L, "gq")
                meet(pe, me, book)
                tensor_headnorm(pe, book, [T - t0] * 4 + [T] * 2, con("ones64"))
                meet(pe, me, book)
                tensor_rope(pe, book, gq_rope())
                meet(pe, me, book)
                tensor_attention(pe, "gq", L, book)
                meet(pe, me, book)
                tensor_merge(pe, L, book)
                meet(pe, me, book)
                tensor_out(pe, L, book)
                if L + 1 < DEPTH:
                    tensor_vectors(pe, L + 1, ps[7])
                meet(pe, me, book)
                tensor_rms(pe, book, t0)
                meet(pe, me, book)
                tensor_turn(pe, book, hidden_src, 2 * (t0 // P))
                tensor_router(pe, L)
                meet(pe, me, book)
                tensor_moe(pe, L)
                pe.drain().then_inc(sig("tensor_left_experts"), 1)
                meet(pe, me, book)
                tensor_combine(pe, L, book)
                meet(pe, me, book)
            tensor_rms(pe, book, SEG)
            meet(pe, me, book)
            tensor_turn(pe, book, hidden_src, 4)

        @block.scalar
        def _(act):
            book, me = Book(), "scalar"
            act.dma_start(crow[0:8, :], a["c_ctx"].rearrange("(k p) -> k p", p=P)).then_inc(sig("conditioning"), 16)
            act.dma_start(crow[8:16, :], a["c"][0].rearrange("(k p) -> k p", p=P)).then_inc(sig("conditioning"), 16)
            act.wait_ge(sig("rows_cleared"), 1)
            assert load_vectors(act, 0, "vectors_loaded_0") == n_loads
            act.wait_ge(sig("conditioning_turned"), 1)
            act.activation(sc[:, :], ps[4][:, 0:16], ACT.Silu).then_inc(sig("conditioned"), 1)
            scalar_turn(act, book, xt_dst)
            scalar_ada(act, 0, range(24))
            scalar_vectors(act, 0, ps[6])
            meet(act, me, book)
            for L in range(DEPTH):
                t0 = lo(L)
                scalar_rms(act, book)
                meet(act, me, book)
                scalar_project(act, L, "ml")
                scalar_gates(act, L)
                meet(act, me, book)
                scalar_activate(act, [regA[:, j, t0 if j < 4 else 0:] for j in range(8)], ACT.Silu)
                act.drain().then_inc(sig("mlstm_qk"), 1)
                scalar_activate(act, [regA[:, 12 + j, t0:] for j in range(4)], ACT.Sigmoid)
                scalar_mlstm(act, L, book)
                meet(act, me, book)
                scalar_headnorm(act, book, [T - t0] * 4, P)
                meet(act, me, book)
                scalar_project(act, L, "hy")
                meet(act, me, book)
                scalar_filters(act, L, book)
                meet(act, me, book)
                scalar_hyena(act, L, book)
                meet(act, me, book)
                scalar_project(act, L, "df")
                meet(act, me, book)
                scalar_lambda(act, L)
                meet(act, me, book)
                scalar_attention(act, "df", L, book)
                meet(act, me, book)
                scalar_headnorm(act, book, [T - t0] * 4, P)
                meet(act, me, book)
                scalar_project(act, L, "gq")
                meet(act, me, book)
                scalar_headnorm(act, book, [T - t0] * 4 + [T] * 2, 64)
                meet(act, me, book)
                meet(act, me, book)
                scalar_attention(act, "gq", L, book)
                meet(act, me, book)
                scalar_merge(act, L, book)
                meet(act, me, book)
                if L + 1 < DEPTH:
                    scalar_vectors(act, L + 1, ps[7])
                meet(act, me, book)
                scalar_rms(act, book, t0)
                meet(act, me, book)
                scalar_turn(act, book, rows_dst(rowsY), 2 * (t0 // P))
                act.drain()
                act.wait_ge(sig("vector_half_turned"), L + 1)
                z = t0 // P
                act.dma_start(hrows[L].rearrange("(t p) n -> p t n", p=P), rowsY[:, z:, :])\
                   .then_inc(sig("rows_in_dram"), 16)
                scalar_router(act, L)
                meet(act, me, book)
                scalar_moe(act, L)
                meet(act, me, book)
                meet(act, me, book)
            scalar_rms(act, book, SEG)
            meet(act, me, book)
            scalar_turn(act, book, rows_dst(rowsY), 4)
            act.drain().then_inc(sig("final_half"), 1)

        @block.vector
        def _(dve):
            book, me = Book(), "vector"
            vector_turn(dve, book, xt_dst)
            meet(dve, me, book)
            vector_ada(dve, 0, ps[5])
            for L in range(DEPTH):
                t0 = lo(L)
                vector_rms(dve, book, L, 0)
                meet(dve, me, book)
                vector_project(dve, L, "ml")
                vector_gates(dve, L)
                meet(dve, me, book)
                vector_mlstm(dve, L, book)
                meet(dve, me, book)
                vector_headnorm(dve, book, [(Y[:, 4 + h, t0:], v(L, "ml_norm")) for h in range(4)],
                                lambda e, i, t: e.tensor_tensor(t, t, regA[:, 12 + i, t0:], ALU.mult))
                meet(dve, me, book)
                vector_project(dve, L, "hy")
                meet(dve, me, book)
                vector_filters(dve, L, book)
                meet(dve, me, book)
                vector_hyena(dve, L, book)
                meet(dve, me, book)
                meet(dve, me, book)
                vector_rope(dve, book, df_rope())
                vector_lambda(dve, L)
                meet(dve, me, book)
                vector_attention(dve, "df", L, book)
                meet(dve, me, book)
                vector_headnorm(dve, book, [(Y[:, h, t0:], small[:, 17:18]) for h in range(4)])
                meet(dve, me, book)
                meet(dve, me, book)
                vector_headnorm(dve, book, [(regB[:, j, t0 if j < 4 else 0:], v(L, "gq_norm" if j < 4 else "gk_norm"))
                                            for j in range(6)])
                meet(dve, me, book)
                vector_rope(dve, book, gq_rope())
                meet(dve, me, book)
                vector_attention(dve, "gq", L, book)
                meet(dve, me, book)
                vector_merge(dve, L, book)
                meet(dve, me, book)
                vector_out(dve, L, book)
                meet(dve, me, book)
                vector_rms(dve, book, L, 1, t0)
                if L + 1 < DEPTH:
                    vector_ada(dve, L + 1, ps[6])
                meet(dve, me, book)
                vector_turn(dve, book, rows_dst(rowsY), 2 * (t0 // P))
                dve.drain().then_inc(sig("vector_half_turned"), 1)
                vector_router(dve, L)
                meet(dve, me, book)
                vector_moe(dve, L)
                meet(dve, me, book)
                vector_combine(dve, L)
                vector_combine_add(dve, L, book)
                meet(dve, me, book)
            vector_rms(dve, book, 0, 2, SEG)
            meet(dve, me, book)
            vector_turn(dve, book, rows_dst(rowsY), 4)
            dve.wait_ge(sig("final_half"), 1)
            dve.drain().then_inc(sig("final_rows"), 1)


_INS = ["x", "c", "ctx", "c_ctx", "w_ada", "b_ada", "norm1_g", "norm2_g", "w_in", "diff_lam", "diff_norm_g",
        "ml_conv_w", "ml_conv_b", "ml_gate_b", "ml_norm_g", "gqa_qnorm_g", "gqa_knorm_g",
        "hy_conv_w", "hy_conv_b", "hy_f_w1", "hy_f_b1", "hy_f_w2", "hy_f_b2", "hy_f_w3", "hy_f_freq", "hy_bias",
        "w_branch", "w_out", "moe_w_group", "moe_b_group", "moe_w_router", "moe_b_router",
        "moe_w_gate", "moe_w_up", "moe_w_down", "final_norm_g"]


def kernel(**inputs):
    import numpy as _np
    import concourse.bacc as _bacc
    from concourse import mybir as _mybir
    from concourse.bass_utils import run_bass_kernel_spmd as _run

    nc = _bacc.Bacc("TRN2", target_bir_lowering=False, num_devices=1)
    consts, ccols = shape_constants()
    arrays, args = {"constants_dram": consts}, {}
    for name in _INS:
        x = _np.ascontiguousarray(inputs[name])
        arrays[f"in_{name}_dram"] = x
        args[name] = nc.dram_tensor(f"in_{name}_dram", x.shape, _mybir.dt.from_np(x.dtype), kind="ExternalInput").ap()
    args["constants"] = nc.dram_tensor("constants_dram", consts.shape, _mybir.dt.from_np(consts.dtype),
                                       kind="ExternalInput").ap()
    shape = tuple(inputs["x"].shape)
    out = nc.dram_tensor("out_0_dram", shape, _mybir.dt.float32, kind="ExternalOutput").ap()
    backbone(nc, args, consts, ccols, out)
    r = _run(nc, [arrays], core_ids=[0])
    return r.results[0]["out_0_dram"]
```

```python
import math
from contextlib import ExitStack
from itertools import chain, count

import numpy as np

import concourse.bass as bass
from concourse import mybir

P = 128
D = 1024
KT = D // P
T = 512
SEG = 256
TT = T // P
DEPTH = 2
EPS = 1e-6
HY = 512
TAPS = 256
E = 32
MAXBLK = 40
NBT = MAXBLK + 3
FAR = 8192.0
NEG = -1.0e30

DQ, DK, DV = 0, 512, 1024
MQ, MK, MV, MO, MG = 1536, 2048, 2560, 3072, 3584
GQ, GK, GV = 3600, 4112, 4240
HU = 4368
BG = 5904

F32 = mybir.dt.float32
I32 = mybir.dt.int32
ALU = mybir.AluOpType
ACT = mybir.ActivationFunctionType
AXX = mybir.AxisListType.X

V1 = {}
_at = 0
for _name, _n in (("b_ada", 48), ("norm1", 8), ("norm2", 8), ("ml_conv", 24), ("ml_convb", 8)):
    V1[_name] = _at
    _at += _n
N1 = _at
for _name, _n in (("hy_conv", 36), ("hy_convb", 12), ("hy_bias", 8), ("diff_norm", 1), ("ml_norm", 1),
                  ("gq_norm", 1), ("gk_norm", 1), ("f_b1", 1), ("f_b2", 1), ("f_freq", 2), ("final", 8)):
    V1[_name] = _at
    _at += _n
N2 = _at - N1


def shape_constants():
    f8 = np.float64
    p = np.arange(P)
    cols, at, parts = {}, 0, []

    def add(name, a):
        nonlocal at
        a = np.asarray(a, np.float32).reshape(P, -1)
        cols[name] = (at, a.shape[1])
        at += a.shape[1]
        parts.append(a)

    add("ident", np.eye(P))
    add("ones", np.ones((P, P)))
    add("ones64", (p[:, None] // 64 == p[None, :] // 64))
    rot = np.zeros((P, P))
    for h in range(2):
        for d in range(64):
            q, r = d // 16, d % 16
            src = {0: 1, 1: 0, 2: 3, 3: 2}[q] * 16 + r
            rot[h * 64 + src, h * 64 + d] = -1.0 if q in (0, 2) else 1.0
    add("rot", rot)
    inv = (np.float32(10000.0) ** (-np.arange(16, dtype=np.float32) / np.float32(16))).astype(np.float32)
    tok = np.arange(SEG)
    ar = (tok // 64).astype(np.float32)[:, None] * inv
    ac = (tok % 64).astype(np.float32)[:, None] * inv
    ang = np.concatenate([ar, ar, ac, ac], -1)
    ang = np.concatenate([ang, ang], -1).T
    add("cos", np.cos(ang.astype(f8)))
    add("sin", np.sin(ang.astype(f8)))
    s, t = p[:, None], p[None, :]
    z = np.zeros((P, P))
    tri_f = np.where(s <= t, 0.0, NEG)
    tri_b = np.where(s >= t, 0.0, NEG)
    add("mask_f", np.concatenate([tri_f, z, z, z], 1))
    add("mask_b0", np.concatenate([tri_b, z + NEG, z, z], 1))
    add("mask_b1", np.concatenate([z, tri_b, z, z], 1))
    tt = np.arange(SEG).astype(f8)
    w = 2 * np.pi * np.outer(tt, np.arange(SEG)) / (2 * SEG)
    alt = (-1.0) ** np.arange(SEG)
    C, S = np.cos(w), np.sin(w)
    S[:, 0] = alt
    Cb = C[:, :P].copy()
    Cb[:, 0] = alt
    two = lambda a: a.reshape(2, P, -1).transpose(1, 0, 2)
    add("dft_c", two(C))
    add("dft_s", two(S))
    add("dft_cb", two(Cb))
    scale = np.full((SEG, 1), 2.0 / (2 * SEG))
    scale[0] = 1.0 / (2 * SEG)
    add("inv_c", two(C.T * scale))
    add("inv_s", two(S.T * scale))
    tf = (np.arange(TAPS, dtype=np.float32) / np.float32(TAPS))
    ld = abs(math.log(1e-2))
    alpha = np.linspace(ld / 1.5, ld / 0.3, HY).astype(np.float32)
    add("window", two(np.exp((-tf[:, None] * alpha).astype(f8)) + 0.05))
    bands = np.arange(1, 17, dtype=np.float32)
    an = np.float32(2.0 * math.pi) * tf[:, None] * bands
    emb = np.concatenate([tf[:, None], np.cos(an.astype(f8)), np.sin(an.astype(f8))], -1).T
    e = np.zeros((P, TAPS))
    e[:33] = emb
    add("emb", e)
    add("not0", (p[:, None] > 0))
    add("lt4", (p[:, None] < 4))
    add("ge4", (p[:, None] >= 4))
    add("upper", (s < t))
    add("slots", np.broadcast_to(np.arange(P), (P, P)))
    add("iota32", np.broadcast_to(np.arange(32), (P, 32)))
    add("iota_blk", np.broadcast_to(np.arange(NBT), (P, NBT)))
    add("tok_id", p[:, None] + P * np.arange(TT)[None, :])
    add("row_id", (2 * (p[:, None, None] + P * np.arange(TT)[None, :, None]) + np.arange(2)[None, None, :]))
    return np.concatenate(parts, 1), cols


def backbone(nc, a, consts, ccols, out):
    ctx = ExitStack()
    with ctx:
        def sb(name, shape, dt=F32):
            return ctx.enter_context(nc.sbuf_tensor(name, shape, dt))

        def sem(name):
            return ctx.enter_context(nc.semaphore(name))

        ctx.enter_context(nc.allow_non_contiguous_dma("small vectors"))

        XT = sb("XT", [P, KT, T])
        hT = sb("hT", [P, KT, T])
        Y = sb("Y", [P, 16, T])
        SLOT = 2048
        NSLOT = 3
        WIDE = 8
        A0, B0, W0, S0 = 0, 8192, 16384, 16384 + NSLOT * SLOT
        AR = sb("arena", [P, 24576])
        scr = sb("scr", [P, 4, T])
        C = sb("consts", [P, consts.shape[1]])
        vrow = sb("vrow", [P, DEPTH, 2, P])
        vecs = sb("vecs", [P, DEPTH, N1 + N2])
        mods = sb("mods", [P, DEPTH, 48, 2])
        gs = sb("gs", [P, KT, 2])
        crow = sb("crow", [16, P])
        sc = sb("sc", [P, 16])
        small = sb("small", [P, 64])
        gw = sb("gw", [P, DEPTH, KT, 2, 2, 4])
        gb = sb("gb", [8, DEPTH, 2])
        aT = sb("aT", [P, 4, 8])
        lam4 = sb("lam4", [64, DEPTH, 4])
        w12 = sb("w12", [64, DEPTH, 128])
        rw = sb("rw", [P, DEPTH, KT, 36])
        rb = sb("rb", [P, DEPTH, 36])
        rt = sb("rt", [P, 4, 36])
        oh = sb("oh", [P, 4, 2, 32])
        place = sb("place", [P, 2, 4, 2])
        gate = sb("gate", [P, 4, 2])
        tab = sb("tab", [P, NBT + 1], I32)
        gidx = sb("gidx", [P, NBT], I32)
        sidx = sb("sidx", [P, NBT], I32)
        gi = sb("gi", [P, 2], I32)
        si = sb("si", [P, 2], I32)
        pend = sb("pend", [P, 4, 32])
        eps_col = sb("eps_col", [P, 1])
        ps = [ctx.enter_context(nc.psum_tensor(f"ps{i}", [P, T], F32)) for i in range(8)]

        def con(name):
            o, n = ccols[name]
            return C[:, o:o + n]

        ident, ones = con("ident"), con("ones")
        EARLY = 2 * P

        def lo(L):
            return 0 if L < DEPTH - 1 else SEG

        def v(L, name, i=0, n=1):
            return vecs[:, L, V1[name] + i:V1[name] + i + n]

        def slot(m, k, n):
            i = chunks[m][1]
            o = W0 + i * SLOT if i < NSLOT else A0 + (i - NSLOT) * SLOT
            return AR[:, o:o + k * n].rearrange("p (k n) -> p k n", k=k)

        regA = AR[:, A0:A0 + 8192].rearrange("p (j t) -> p j t", t=T)
        regB = AR[:, B0:B0 + 8192].rearrange("p (j t) -> p j t", t=T)

        hrows = [nc.dram_tensor(f"moe_rows_{L}", (T - lo(L), D), F32, kind="Internal").ap() for L in range(DEPTH)]
        yrows = [nc.dram_tensor(f"moe_outputs_{L}", (2 * (T - lo(L)), D), F32, kind="Internal").ap()
                 for L in range(DEPTH)]

        chunks = []

        ring_at = [0]

        def chunk(fill, place_at=None):
            if place_at is None:
                place_at = ring_at[0] % NSLOT
                ring_at[0] += 1
            before = [i for i, c in enumerate(chunks) if c[1] == place_at]
            chunks.append((fill, place_at, before[-1] if before else None))
            return len(chunks) - 1

        def w_in_chunk(L, c0, n=256):
            src = a["w_in"][L, :, c0:c0 + n].rearrange("(k p) n -> p k n", p=P)
            return chunk([(lambda m: slot(m, KT, n), src)])

        tiles = []

        def feature_tiles(L, phase, c0, n, kind, out_of, extra=None, t0=0):
            for c in range(n // 256):
                m = w_in_chunk(L, c0 + 256 * c)
                for half in range(2):
                    j = 2 * c + half
                    tiles.append(dict(L=L, phase=phase, m=m, half=half, kind=kind, out=out_of(j), j=j,
                                      extra=extra, last=half == 1, tok=None, t0=t0))

        def token_tiles(L, phase, c0, n, out_of):
            w = min(n, 256)
            for c in range(n // w):
                m = w_in_chunk(L, c0 + w * c, w)
                for t in range(TT):
                    tiles.append(dict(L=L, phase=phase, m=m, kind="copy", out=out_of(t, c), tok=t, w=w,
                                      last=t == TT - 1))

        ada_m, merge_m, wout_m = {}, {}, {}

        def ada_chunk(L, c):
            return chunk([(lambda m: slot(m, KT, 256),
                           a["w_ada"][L, :, 256 * c:256 * c + 256].rearrange("(k p) n -> p k n", p=P))],
                         NSLOT + c % WIDE if L == 0 else NSLOT + WIDE // 2 + c % (WIDE // 2))

        ada_m[0] = [ada_chunk(0, c) for c in range(24)]
        for L in range(DEPTH):
            t0 = lo(L)
            feature_tiles(L, "ml", MQ, 512, "conv", lambda j: regA[:, j, :], ("ml_conv", "ml_convb", 8), t0)
            feature_tiles(L, "ml", MK, 512, "conv", lambda j: regA[:, 4 + j, :], ("ml_conv", "ml_convb", 8))
            for t in tiles[-4:]:
                t["j"] += 4
            token_tiles(L, "ml", MV, 512, lambda t, c: regA[:, 8 + t, 256 * c:256 * c + 256])
            feature_tiles(L, "ml", MO, 512, "copy", lambda j: regA[:, 12 + j, :], None, t0)
            feature_tiles(L, "hy", HU, 1536, "conv", lambda j: regB[:, j, :], ("hy_conv", "hy_convb", 12), t0)
            feature_tiles(L, "df", DQ, 512, "copy", lambda j: regA[:, j, :], None, t0)
            feature_tiles(L, "df", DK, 512, "copy", lambda j: regA[:, 4 + j, :])
            token_tiles(L, "df", DV, 512, lambda t, c: regA[:, 8 + t, 256 * c:256 * c + 256])
            feature_tiles(L, "gq", GQ, 512, "copy", lambda j: regB[:, j, :], None, t0)
            fills = []
            for g in range(2):
                src = a["w_in"][L, :, GK + 64 * g:GK + 64 * g + 64].rearrange("(k p) n -> p k n", p=P)
                for r in range(2):
                    o = 128 * g + 64 * r
                    fills.append((lambda m, o=o: slot(m, KT, 256)[:, :, o:o + 64], src))
            m = chunk(fills)
            for g in range(2):
                tiles.append(dict(L=L, phase="gq", m=m, half=g, kind="copy", out=regB[:, 4 + g, :], j=g,
                                  last=g == 1, tok=None, t0=0))
            token_tiles(L, "gq", GV, 128, lambda t, c: regB[:, 6, 128 * t:128 * t + 128])
            merge_m[L] = []
            for jj in range(4):
                for n in range(4):
                    g = w_in_chunk(L, BG + n * D + 256 * jj)
                    b = chunk([(lambda m: slot(m, 4, 256),
                                a["w_branch"][L, n, :, 256 * jj:256 * jj + 256].rearrange("(k p) n -> p k n", p=P))])
                    merge_m[L].append((g, b))
                    if L + 1 < DEPTH:
                        i2 = 4 * jj + n - 1
                        ada_m.setdefault(L + 1, []).extend(
                            ada_chunk(L + 1, c) for c in (range(2 * i2, min(2 * i2 + 2, 24)) if i2 >= 0 else ()))
            wout_m[L] = [chunk([(lambda m: slot(m, KT, 256),
                                 a["w_out"][L, :, 256 * c:256 * c + 256].rearrange("(k p) n -> p k n", p=P))])
                         for c in range(4)]
        n_conv = 0
        for q, t in enumerate(tiles):
            t["q"] = q
            if t["kind"] == "conv":
                n_conv += 1
            t["convs"] = n_conv
        layer_end_chunk = [wout_m[L][-1] for L in range(DEPTH)]

        block = ctx.enter_context(nc.Block())

        S = {}

        def sig(name):
            if name not in S:
                S[name] = sem(name)
            return S[name]

        class Book:

            def __init__(self):
                self.n = {}

            def base(self, link, k):
                b = self.n.get(link, 0)
                self.n[link] = b + k
                return b

        def arrived(e, m):
            at = chunks[m][1]
            per = sum(len(c[0]) for c in chunks[:m + 1] if c[1] == at)
            e.wait_ge(sig(f"chunk_in_slot_{at}"), 16 * per)

        def meet(e, me, book):
            n = book.base("stage", 1) + 1
            e.drain().then_inc(sig(f"{me}_ended_stage"), 1)
            for other in ("tensor", "vector", "scalar"):
                if other != me:
                    e.wait_ge(sig(f"{other}_ended_stage"), n)

        def segs(ap):
            return ap.rearrange("p (s t) -> p s t", s=2)

        Yf = Y[:, :, :].rearrange("p j t -> p (j t)")
        rowsY = Yf[:, 0:4096].rearrange("p (t n) -> p t n", t=4)
        rowsB = AR[:, B0:B0 + 4096].rearrange("p (t n) -> p t n", t=4)
        rowsA = AR[:, A0:A0 + 8192].rearrange("p (t c n) -> p t c n", t=4, c=2)

        def tensor_turn(pe, book, src, g0=0):
            b, h = book.base("turned", 8 - g0) - g0, book.base("turned_out", 4 - g0 // 2) - g0 // 2
            for g in range(g0, 8):
                if g >= g0 + 4:
                    who = "scalar" if g % 2 == 0 else "vector"
                    pe.wait_ge(sig(f"{who}_took_turned"), h + (g - 4) // 2 + 1)
                for i in range(4):
                    last = pe.transpose(ps[g % 4][:, P * i:P * i + P], src(g, i), ident)
                last.then_inc(sig("turned"), 1)

        def scalar_turn(act, book, dst, g0=0):
            b, h = book.base("turned", 8 - g0) - g0, book.base("turned_out", 4 - g0 // 2) - g0 // 2
            for g in range(g0, 8, 2):
                act.wait_ge(sig("turned"), b + g + 1)
                act.activation(dst(g), ps[g % 4][:, :].rearrange("p (i t) -> p i t", i=4), ACT.Copy)\
                   .then_inc(sig("scalar_took_turned"), 1)

        def vector_turn(dve, book, dst, g0=0):
            b, h = book.base("turned", 8 - g0) - g0, book.base("turned_out", 4 - g0 // 2) - g0 // 2
            for g in range(g0 + 1, 8, 2):
                dve.wait_ge(sig("turned"), b + g + 1)
                dve.tensor_copy(dst(g), ps[g % 4][:, :].rearrange("p (i t) -> p i t", i=4))\
                   .then_inc(sig("vector_took_turned"), 1)

        def xt_dst(g):
            return XT[:, 4 * (g % 2):4 * (g % 2) + 4, P * (g // 2):P * (g // 2) + P]

        def rows_src(rows):
            return lambda g, i: rows[:, g // 2, P * (4 * (g % 2) + i):P * (4 * (g % 2) + i) + P]

        def rows_dst(rows):
            return lambda g: rows[:, g // 2, 512 * (g % 2):512 * (g % 2) + 512].rearrange("p (i t) -> p i t", i=4)

        def scalar_rms(act, book, L, which, t0=0):
            b = book.base("square", KT)
            for k in range(KT):
                if which == 1:
                    act.wait_ge(sig("residual_added"), KT * L + k + 1)
                if k >= 2:
                    act.wait_ge(sig("square_summed"), b + k - 1)
                act.activation(scr[:, k % 2, t0:], XT[:, k, t0:], ACT.Square).then_inc(sig("square"), 1)
            act.wait_ge(sig("square_summed"), b + KT)
            act.activation(scr[:, 2, t0:], ps[4][:, t0:], ACT.Ln, scale=1.0 / D, bias=eps_col[:, :])
            act.drain()
            act.activation(scr[:, 3, t0:], scr[:, 2, t0:], ACT.Exp, scale=-0.5).then_inc(sig("rms"), 1)
            if which == 2:
                return
            n = book.base("scaled", KT)
            for k in range(KT):
                act.wait_ge(sig("stream_scaled"), n + k + 1)
                for s in range(t0 // SEG, 2):
                    h = hT[:, k, SEG * s:SEG * s + SEG]
                    last = act.activation(h, h, ACT.Identity, scale=gs[:, k, s:s + 1],
                                          bias=mods[:, L, 24 * which + k, s:s + 1])
                last.then_inc(sig("hidden"), 1)

        def tensor_rms(pe, book, t0=0):
            b = book.base("square", KT)
            for k in range(KT):
                pe.wait_ge(sig("square"), b + k + 1)
                pe.matmul(ps[4][:, t0:], ones, scr[:, k % 2, t0:], start=(k == 0), stop=(k == KT - 1))\
                  .then_inc(sig("square_summed"), 1)

        def vector_rms(dve, book, L, which, t0=0):
            c = book.base("rms", 1)
            if which < 2:
                o = 24 * which
                for s in range(2):
                    dve.scalar_tensor_tensor(gs[:, :, s], mods[:, L, o + 8:o + 16, s], 1.0,
                                             v(L, ("norm1", "norm2")[which], 0, KT), ALU.add, ALU.mult)
                dve.drain()
            dve.wait_ge(sig("rms"), c + 1)
            for k in range(KT):
                if which < 2:
                    dve.tensor_tensor(hT[:, k, t0:], XT[:, k, t0:], scr[:, 3, t0:], ALU.mult)\
                       .then_inc(sig("stream_scaled"), 1)
                else:
                    dve.scalar_tensor_tensor(hT[:, k, t0:], XT[:, k, t0:], v(L, "final", k), scr[:, 3, t0:],
                                             ALU.mult, ALU.mult).then_inc(sig("hidden"), 1)

        def hidden_tile(e, L, which, k=KT - 1):
            e.wait_ge(sig("hidden"), KT * (2 * L + which) + k + 1)

        def head_tiles(L, phase):
            z = lo(L)
            ml = [(Y[:, 4 + h, z:], v(L, "ml_norm"), P, ones, None, regA[:, 12 + h, z:]) for h in range(4)]
            if phase == "hy":
                return ml
            q0 = [t["q"] for t in tiles if t["L"] == L and t["phase"] == "gq"][0]
            return [(Y[:, h, z:], small[:, 17:18], P, ones, None, None) for h in range(4)] + \
                   [(regB[:, j, z if j < 4 else 0:], v(L, "gq_norm" if j < 4 else "gk_norm"), 64, con("ones64"),
                     q0 + j, None) for j in range(6)]

        def vector_headnorm(dve, book, todo, sum_at):
            b = book.base("headnorm", len(todo))
            for step in range(-1, sum_at[-1] + 2):
                for p, at in enumerate(sum_at):
                    pair = (2 * p, 2 * p + 1)
                    if step == at + 1:
                        for i in pair:
                            t, g, _, _, _, gated_by = todo[i]
                            dve.wait_ge(sig("head_rms"), b + i + 1)
                            r = scr[:, 2 + i % 2, 0:t.shape[-1]]
                            last = dve.scalar_tensor_tensor(t, t, g, r, ALU.mult, ALU.mult)
                            if gated_by is not None:
                                dve.drain()
                                last = dve.tensor_tensor(t, t, gated_by, ALU.mult)
                            last.then_inc(sig("head_normed"), 1)
                    if step == at - 1:
                        if p >= 1:
                            dve.wait_ge(sig("head_squares_summed"), b + 2 * p)
                        for i in pair:
                            t, q = todo[i][0], todo[i][4]
                            if q is not None:
                                dve.wait_ge(sig("projection_by_scalar"), q + 1)
                            dve.tensor_tensor(scr[:, i % 2, 0:t.shape[-1]], t, t, ALU.mult)\
                               .then_inc(sig("head_squares"), 1)
                if step <= sum_at[-1]:
                    yield

        def tensor_headnorm(pe, book, todo, sum_at):
            b = book.base("headnorm", len(todo))
            for step in range(sum_at[-1] + 1):
                for p, at in enumerate(sum_at):
                    if step == at:
                        if p >= 1:
                            pe.wait_ge(sig("head_rms"), b + 2 * p)
                        for i in (2 * p, 2 * p + 1):
                            t, g, width, sums, q, gated_by = todo[i]
                            w = t.shape[-1]
                            pe.wait_ge(sig("head_squares"), b + i + 1)
                            pe.matmul(ps[4 + i % 2][:, 0:w], sums, scr[:, i % 2, 0:w], start=True, stop=True)\
                              .then_inc(sig("head_squares_summed"), 1)
                yield

        def scalar_headnorm(act, book, todo, sum_at):
            b = book.base("headnorm", len(todo))
            for step in range(sum_at[-1] + 1):
                for p, at in enumerate(sum_at):
                    if step == at:
                        if p >= 1:
                            act.wait_ge(sig("head_normed"), b + 2 * p)
                        for i in (2 * p, 2 * p + 1):
                            t, width = todo[i][0], todo[i][2]
                            w = t.shape[-1]
                            act.wait_ge(sig("head_squares_summed"), b + i + 1)
                            act.activation(scr[:, 2 + i % 2, 0:w], ps[4 + i % 2][:, 0:w], ACT.Ln, scale=1.0 / width,
                                           bias=eps_col[:, :])
                        act.drain()
                        for i in (2 * p, 2 * p + 1):
                            r = scr[:, 2 + i % 2, 0:todo[i][0].shape[-1]]
                            act.activation(r, r, ACT.Exp, scale=-0.5).then_inc(sig("head_rms"), 1)
                yield

        HY_SUMS, GQ_SUMS = (0, 1), (0, 1, 2, 4, 6)

        def started(steps):
            next(steps)
            return steps

        def tensor_project(pe, L, phase, between=()):
            between = iter(between)
            for t in tiles:
                if t["L"] != L or t["phase"] != phase:
                    continue
                q, m = t["q"], t["m"]
                arrived(pe, m)
                if q >= 4:
                    pe.wait_ge(sig("projection_by_scalar"), q - 3)
                    if tiles[q - 4]["kind"] == "conv":
                        pe.wait_ge(sig("projection_by_vector"), tiles[q - 4]["convs"])
                bank = ps[q % 4]
                first = t is [x for x in tiles if x["L"] == L][0]
                for k in range(KT):
                    if first:
                        hidden_tile(pe, L, 0, k)
                    if t["tok"] is None:
                        w = slot(m, KT, 256)[:, k, P * t["half"]:P * t["half"] + P]
                        last = pe.matmul(bank[:, t["t0"]:], w, hT[:, k, t["t0"]:], start=(k == 0), stop=(k == KT - 1))
                    else:
                        last = pe.matmul(bank[:, 0:t["w"]], hT[:, k, P * t["tok"]:P * t["tok"] + P],
                                         slot(m, KT, t["w"])[:, k, :], start=(k == 0), stop=(k == KT - 1))
                last.then_inc(sig("projected"), 1)
                if t["last"]:
                    pe.drain().then_inc(sig("chunk_used"), 1)
                next(between, None)
            for _ in between:
                pass

        def scalar_project(act, L, phase, between=()):
            between = iter(between)
            for t in tiles:
                if t["L"] != L or t["phase"] != phase:
                    continue
                q = t["q"]
                act.wait_ge(sig("projected"), q + 1)
                if t["kind"] == "conv":
                    cw, cb, n = t["extra"]
                    z = t["t0"]
                    act.activation(t["out"][:, z:], ps[q % 4][:, z:], ACT.Identity, bias=v(L, cb, t["j"]),
                                   scale=v(L, cw, n + t["j"])).then_inc(sig("projection_by_scalar"), 1)
                else:
                    z, w = (0, t["w"]) if t["tok"] is not None else (t["t0"], T)
                    act.activation(t["out"][:, z:], ps[q % 4][:, z:w], ACT.Copy)\
                       .then_inc(sig("projection_by_scalar"), 1)
                next(between, None)
            for _ in between:
                pass

        def vector_project(dve, L, phase, between=()):
            between = iter(between)
            for t in tiles:
                if t["L"] != L or t["phase"] != phase:
                    continue
                if t["kind"] == "conv":
                    q = t["q"]
                    cw, cb, n = t["extra"]
                    dve.wait_ge(sig("projection_by_scalar"), q + 1)
                    z = t["t0"] // SEG
                    u, p = segs(t["out"])[:, z:, :], segs(ps[q % 4][:, :])[:, z:, :]
                    dve.scalar_tensor_tensor(u[:, :, 1:], p[:, :, 0:SEG - 1], v(L, cw, t["j"]), u[:, :, 1:],
                                             ALU.mult, ALU.add)
                    dve.drain()
                    dve.scalar_tensor_tensor(u[:, :, 0:SEG - 1], p[:, :, 1:], v(L, cw, 2 * n + t["j"]),
                                             u[:, :, 0:SEG - 1], ALU.mult, ALU.add)\
                       .then_inc(sig("projection_by_vector"), 1)
                    dve.drain()
                next(between, None)
            for _ in between:
                pass

        ada_row = lambda c: scr[0:2, 3, 256 * (c % 2):256 * (c % 2) + 256]
        row_bank = lambda c: ps[(7, 4)[c % 2]]

        def tensor_ada(pe, cs, bank):
            def turn(c):
                pe.wait_ge(sig("ada_row_copied"), c + 1)
                for half in range(2):
                    o = 2 * (2 * c + half)
                    pe.transpose(bank[:, o:o + 2], ada_row(c)[:, P * half:P * half + P], ident[0:2, 0:2])

            for c in cs:
                m = ada_m[0][c]
                arrived(pe, m)
                for k in range(KT):
                    last = pe.matmul(row_bank(c)[0:2, 0:256], sc[:, k::8], slot(m, KT, 256)[:, k, :],
                                     start=(k == 0), stop=(k == KT - 1))
                last.then_inc(sig("ada_row_summed"), 1)
                pe.drain().then_inc(sig("chunk_used"), 1)
                if c >= 1:
                    turn(c - 1)
                if c == 23:
                    turn(c)

        def scalar_ada(act, cs):
            for c in cs:
                act.wait_ge(sig("ada_row_summed"), c + 1)
                act.activation(ada_row(c), row_bank(c)[0:2, 0:256], ACT.Copy).then_inc(sig("ada_row_copied"), 1)

        ada_acc = lambda c, s: AR[:, S0 + 512 * (c % 2) + 256 * s:S0 + 512 * (c % 2) + 256 * s + 256]
        ada_of_merge = lambda i2: range(2 * i2, min(2 * i2 + 2, 24)) if i2 >= 0 else ()

        def vector_ada_weigh(dve, L, cs):
            for c in cs:
                m = ada_m[L][c]
                arrived(dve, m)
                if c >= 2:
                    dve.wait_ge(sig("chunk_used"), ada_m[L][c - 2] + 1)
                for k in range(KT):
                    for s in range(2):
                        acc, w, by = ada_acc(c, s), slot(m, KT, 256)[:, k, :], sc[:, 8 * s + k:8 * s + k + 1]
                        if k == 0:
                            dve.tensor_scalar(acc, w, by, None, ALU.mult)
                        else:
                            dve.scalar_tensor_tensor(acc, w, by, acc, ALU.mult, ALU.add)
                    dve.drain()
                dve.drain().then_inc(sig("ada_weighed"), 1)

        def tensor_ada_sum(pe, L, cs, bank):
            for c in cs:
                pe.wait_ge(sig("ada_weighed"), 24 * (L - 1) + c + 1)
                for half in range(2):
                    for s in range(2):
                        o = 2 * (2 * c + half) + s
                        pe.matmul(bank[:, o:o + 1], ada_acc(c, s)[:, P * half:P * half + P], ones[:, 0:1],
                                  start=True, stop=True)
                pe.drain().then_inc(sig("chunk_used"), 1)

        def vector_ada(dve, L, bank):
            dve.tensor_tensor(mods[:, L, :, :], bank[:, 0:96].rearrange("p (c s) -> p c s", s=2),
                              v(L, "b_ada", 0, 48).unsqueeze(2).to_broadcast([P, 48, 2]), ALU.add)
            dve.drain()

        gt = [AR[0:8, B0 + 512 * i:B0 + 512 * i + 512] for i in range(16)]
        LI, LF, F_F, F_B, A_F, A_B, M_F, M_B, NM, NMF, ONE, TMP, TMP2 = range(13)
        Wt = lambda u, j: AR[:, B0 + 512 * (j + 12 * (u % 2)):B0 + 512 * (j + 12 * (u % 2) + 1)]
        floor_t = lambda u: scr[:, u % 2, :]

        def tensor_gates(pe, L):
            for kind in range(2):
                for k in range(KT):
                    last = pe.matmul(ps[6 + kind][0:8, :], gw[:, L, k, kind, :, :].rearrange("p d h -> p (d h)"),
                                     hT[:, k, :], start=(k == 0), stop=(k == KT - 1))
            last.then_inc(sig("gates_projected"), 1)
            yield

        def vector_gates(dve, L):
            dve.wait_ge(sig("gates_projected"), L + 1)
            dve.tensor_scalar(gt[LI], ps[6][0:8, :], gb[:, L, 0:1], None, ALU.add)
            dve.tensor_scalar(gt[LF], ps[7][0:8, :], gb[:, L, 1:2], None, ALU.add)
            dve.memset(gt[ONE], 1.0)
            dve.drain()
            dve.scalar_tensor_tensor(gt[TMP], gt[LF], -1.0, gt[LF], ALU.mult, ALU.max).then_inc(sig("gate_size"), 1)
            dve.tensor_scalar(gt[LF], gt[LF], 0.0, None, ALU.min)
            dve.drain()
            dve.wait_ge(sig("gate_log"), L + 1)
            dve.tensor_tensor(gt[LF], gt[LF], gt[TMP2], ALU.subtract)
            dve.drain()
            c, l = slice(0, SEG), slice(SEG, T)
            dve.tensor_tensor_scan(gt[F_F], gt[ONE], gt[LF], 0.0, ALU.mult, ALU.add)
            dve.tensor_tensor_scan(gt[F_B][:, 0:SEG][:, ::-1], gt[ONE][:, c], gt[LF][:, 0:SEG][:, ::-1], 0.0,
                                   ALU.mult, ALU.add)
            dve.drain()
            dve.tensor_tensor_scan(gt[F_B][:, SEG:T][:, ::-1], gt[ONE][:, c], gt[LF][:, SEG:T][:, ::-1],
                                   gt[F_B][:, 0:1], ALU.mult, ALU.add)
            dve.tensor_tensor(gt[A_F], gt[LI], gt[F_F], ALU.subtract)
            dve.drain()
            dve.tensor_tensor(gt[A_B], gt[LI], gt[F_B], ALU.subtract)
            dve.tensor_tensor_scan(gt[M_F], gt[A_F], gt[A_F], 0.0, ALU.max, ALU.max)
            dve.drain()
            ab = gt[A_B][:, 0:SEG][:, ::-1]
            dve.tensor_tensor_scan(gt[M_B][:, 0:SEG][:, ::-1], ab, ab, 0.0, ALU.max, ALU.max)
            dve.drain()
            ab = gt[A_B][:, SEG:T][:, ::-1]
            dve.tensor_tensor_scan(gt[M_B][:, SEG:T][:, ::-1], ab, ab, gt[M_B][:, 0:1], ALU.max, ALU.max)
            dve.drain()
            lt, ge = con("lt4")[0:8, :], con("ge4")[0:8, :]
            for f, b in ((A_F, A_B), (M_F, M_B), (F_F, F_B)):
                dve.tensor_scalar(gt[b], gt[b], ge, None, ALU.mult)
            dve.drain()
            for f, b in ((A_F, A_B), (M_F, M_B), (F_F, F_B)):
                dve.scalar_tensor_tensor(gt[f], gt[f], lt, gt[b], ALU.mult, ALU.add)
            dve.drain()
            dve.tensor_scalar(gt[NM], gt[M_F], -1.0, None, ALU.mult)
            dve.tensor_tensor(gt[F_F], gt[F_F], gt[M_F], ALU.add)
            dve.drain()
            dve.tensor_scalar(gt[NMF], gt[F_F], -1.0, None, ALU.mult)
            dve.drain().then_inc(sig("gate_rows"), 1)
            yield

        def vector_gate_columns(dve, L):
            dve.wait_ge(sig("gate_columns"), L + 1)
            dve.tensor_copy(aT[:, :, :], ps[7][:, 0:32].rearrange("p (j r) -> p j r", j=4))
            dve.drain()

        def scalar_gates(act, L):
            act.wait_ge(sig("gate_size"), L + 1)
            act.activation(gt[TMP2], gt[TMP], ACT.Exp, scale=-1.0)
            act.drain()
            act.activation(gt[TMP2], gt[TMP2], ACT.Ln, bias=1.0).then_inc(sig("gate_log"), 1)
            yield

        def tensor_gate_columns(pe, L):
            pe.wait_ge(sig("gate_rows"), L + 1)
            for j in range(4):
                last = pe.transpose(ps[7][:, 8 * j:8 * j + 8], gt[A_F][:, P * j:P * j + P], ident[0:8, 0:8])
            last.then_inc(sig("gate_columns"), 1)

        def reach(j, r, t0):
            if t0:
                zero = con("mask_f")[:, P:P + SEG]
                if j < 2:
                    return [(SEG, zero, SEG)]
                if r < 4:
                    return [(P * j, con("mask_f")[:, 0:T - P * j], T - P * j)]
            if r < 4:
                return [(P * j, con("mask_f")[:, 0:T - P * j], T - P * j)]
            if j == 0:
                return [(0, con("mask_b0"), T)]
            if j == 1:
                return [(0, con("mask_b1"), T)]
            if j == 2:
                return [(2 * P, con("mask_b0")[:, 0:P], P)]
            return [(2 * P, con("mask_b1")[:, 0:2 * P], 2 * P)]

        units_ml = [(h, h + 4 * d) for h in range(4) for d in range(2)]

        def tensor_mlstm(pe, L, book):
            b, t0 = book.base("mlstm", 8), lo(L)

            def floors(u):
                r = units_ml[u][1]
                if u >= 1:
                    pe.wait_ge(sig("mlstm_exponent"), 4 * (b + u))
                    pe.wait_ge(sig("mlstm_floor"), b + u)
                bc = ident[0:8, r:r + 1].to_broadcast([8, P])
                pe.matmul(ps[4][:, t0:], bc, gt[NM][:, t0:], start=True, stop=True)
                pe.matmul(ps[5][:, t0:], bc, gt[NMF][:, t0:], start=True, stop=True)\
                  .then_inc(sig("mlstm_maxima"), 1)

            def scores(u):
                h, r = units_ml[u]
                if r >= 4:
                    return
                if u >= 1:
                    pe.wait_ge(sig("mlstm_weighted"), 4 * (b + u))
                for j in range(4):
                    last = pe.matmul(ps[j][:, t0:], regA[:, 4 + h, P * j:P * j + P], regA[:, h, t0:],
                                     start=True, stop=True)
                last.then_inc(sig("mlstm_scores"), 1)

            floors(0)
            pe.wait_ge(sig("mlstm_qk"), L + 1)
            scores(0)
            for u, (h, r) in enumerate(units_ml):
                if u + 1 < 8:
                    floors(u + 1)
                    scores(u + 1)
                if u >= 1:
                    pe.wait_ge(sig("mlstm_copied"), b + u)
                for j in range(4):
                    (o, mask, w), = reach(j, r, lo(L))
                    pe.wait_ge(sig("mlstm_weighted"), 4 * (b + u) + j + 1)
                    pe.matmul(ps[6][:, o:o + w], regA[:, 8 + j, P * h:P * h + P], Wt(u, j)[:, o:o + w],
                              start=(j == 0), stop=(j == 3))
                    last = pe.matmul(ps[7][:, o:o + w], ones, Wt(u, j)[:, o:o + w], start=(j == 0), stop=(j == 3))
                last.then_inc(sig("mlstm_summed"), 1)

        def scalar_mlstm(act, L, book):
            b, t0 = book.base("mlstm", 8), lo(L)

            def copies(u):
                act.wait_ge(sig("mlstm_summed"), b + u + 1)
                if u >= 1:
                    act.wait_ge(sig("mlstm_unit_done"), b + u)
                act.activation(scr[:, 2, t0:], ps[7][:, t0:], ACT.Abs)
                act.activation(scr[:, 3, t0:], ps[6][:, t0:], ACT.Copy).then_inc(sig("mlstm_copied"), 1)

            for u, (h, r) in enumerate(units_ml):
                if u >= 2:
                    copies(u - 2)
                    act.wait_ge(sig("mlstm_unit_done"), b + u - 1)
                act.wait_ge(sig("mlstm_maxima"), b + u + 1)
                act.activation(floor_t(u)[:, t0:], ps[5][:, t0:], ACT.Exp).then_inc(sig("mlstm_floor"), 1)
                for j in range(4):
                    (o, mask, w), = reach(j, r, lo(L))
                    act.wait_ge(sig("mlstm_exponent"), 4 * (b + u) + j + 1)
                    act.activation(Wt(u, j)[:, o:o + w], Wt(u, j)[:, o:o + w], ACT.Exp)\
                       .then_inc(sig("mlstm_decay"), 1)
            for u in (6, 7):
                copies(u)

        def vector_mlstm(dve, L, book):
            b, t0 = book.base("mlstm", 8), lo(L)

            def exponents(u):
                r = units_ml[u][1]
                dve.wait_ge(sig("mlstm_maxima"), b + u + 1)
                if u >= 2:
                    dve.wait_ge(sig("mlstm_summed"), b + u - 1)
                for j in range(4):
                    (o, mask, w), = reach(j, r, lo(L))
                    dve.scalar_tensor_tensor(Wt(u, j)[:, o:o + w], ps[4][:, o:o + w], aT[:, j, r:r + 1], mask,
                                             ALU.add, ALU.min).then_inc(sig("mlstm_exponent"), 1)

            def finish(u):
                h, r = units_ml[u]
                dve.wait_ge(sig("mlstm_copied"), b + u + 1)
                w, num = scr[:, 2, t0:], scr[:, 3, t0:]
                dve.tensor_tensor(w, w, floor_t(u)[:, t0:], ALU.max)
                dve.drain()
                dve.reciprocal(w, w)
                dve.drain()
                y = Y[:, 4 + h, t0:]
                if r < 4:
                    dve.tensor_tensor(y, num, w, ALU.mult).then_inc(sig("mlstm_unit_done"), 1)
                else:
                    dve.tensor_tensor(w, num, w, ALU.mult)
                    dve.drain()
                    dve.tensor_tensor(y, y, w, ALU.add).then_inc(sig("mlstm_unit_done"), 1)
                dve.drain()

            def weighted(u):
                dve.wait_ge(sig("mlstm_scores"), (b + u) // 2 + 1)
                for j in range(4):
                    (o, mask, w), = reach(j, units_ml[u][1], lo(L))
                    dve.wait_ge(sig("mlstm_decay"), 4 * (b + u) + j + 1)
                    dve.scalar_tensor_tensor(Wt(u, j)[:, o:o + w], ps[j][:, o:o + w], float(P) ** -0.5,
                                             Wt(u, j)[:, o:o + w], ALU.mult, ALU.mult)\
                       .then_inc(sig("mlstm_weighted"), 1)

            exponents(0)
            weighted(0)
            exponents(1)
            for u in range(8):
                if u + 1 < 8:
                    weighted(u + 1)
                finish(u)
                if u + 2 < 8:
                    exponents(u + 2)

        def scalar_activate(act, list_of, fn):
            for t in list_of:
                act.activation(t, t, fn)

        def attention(kind, L, book):
            if kind == "df":
                q = lambda j, hf: regA[64 * hf:64 * hf + 64, j, :]
                k = lambda j, hf: regA[64 * hf:64 * hf + 64, 4 + j, :]
                vv = lambda j, hf, kt: regA[:, 8 + kt, P * j:P * j + P]
            else:
                q = lambda j, hf: regB[64 * hf:64 * hf + 64, j, :]
                k = lambda j, hf: regB[64 * hf:64 * hf + 64, 4 + j // 2, :]
                vv = lambda j, hf, kt: regB[:, 6, P * kt + 64 * (j // 2):P * kt + 64 * (j // 2) + 64]
            units = [(j, t) for t in range(lo(L) // P, TT) for j in range(4)]
            base = book.base("attention", len(units))
            out = lambda j, t: Y[:, (0 if kind == "df" else 8) + j, P * t:P * t + P]
            return q, k, vv, units, base, out

        def prob(kind, u, hf):
            o = (S0 if u % 2 == 0 else B0 if kind == "df" else A0) + 512 * hf
            return AR[:, o:o + 512]

        def turned(kind, u, hf):
            o = (S0 if u % 2 == 0 else B0 if kind == "df" else A0) + 1024 + 512 * hf
            return AR[:, o:o + 512]

        stat = lambda u, i, n=1: small[:, 32 + 8 * (u % 2) + i:32 + 8 * (u % 2) + i + n]

        def tensor_attention(pe, kind, L, book):
            q, k, vv, units, b, out = attention(kind, L, book)
            hs = 1 if kind == "df" else 2

            def scores(u):
                j, t = units[u]
                n = SEG if t < 2 else T
                if u >= 2:
                    pe.wait_ge(sig("exponentials"), b + u - 1)
                for hf in range(2):
                    last = pe.matmul(ps[2 * (u % 2) + hf][:, 0:n], q(j, hf)[:, P * t:P * t + P], k(j, hf)[:, 0:n],
                                     start=True, stop=True)
                last.then_inc(sig("scores"), 1)

            def turn(u):
                nt = 2 if units[u][1] < 2 else 4
                pe.wait_ge(sig("probabilities"), b + u + 1)
                if u >= 1:
                    pe.wait_ge(sig("turned_probabilities"), b + u)
                for hf in range(hs):
                    for kt in range(nt):
                        last = pe.transpose(ps[4 + hf][:, P * kt:P * kt + P],
                                            prob(kind, u, hf)[:, P * kt:P * kt + P], ident)
                last.then_inc(sig("probabilities_turned"), 1)

            def apply(u):
                j, t = units[u]
                nt = 2 if t < 2 else 4
                pe.wait_ge(sig("turned_probabilities"), b + u + 1)
                if u >= 2:
                    pe.wait_ge(sig("attended_out"), b + u - 1)
                for hf in range(hs):
                    o = ps[6 + u % 2][:, 0:P] if hs == 1 else ps[6 + u % 2][64 * hf:64 * hf + 64, 0:P]
                    for kt in range(nt):
                        last = pe.matmul(o, vv(j, hf, kt), turned(kind, u, hf)[:, P * kt:P * kt + P],
                                         start=(kt == 0), stop=(kt == nt - 1))
                last.then_inc(sig("attended"), 1)

            scores(0)
            scores(1)
            for u in range(len(units)):
                turn(u)
                if u + 2 < len(units):
                    scores(u + 2)
                if u >= 1:
                    apply(u - 1)
            apply(len(units) - 1)

        def scalar_attention(act, kind, L, book):
            q, k, vv, units, b, out = attention(kind, L, book)
            hs = 1 if kind == "df" else 2
            width = lambda u: SEG if units[u][1] < 2 else T

            def exponentials(u):
                n = width(u)
                act.wait_ge(sig("score_maxima"), b + u + 1)
                if u >= 2:
                    act.wait_ge(sig("probabilities_turned"), b + u - 1)
                for hf in range(2):
                    act.activation(prob(kind, u, hf)[:, 0:n], ps[2 * (u % 2) + hf][:, 0:n], ACT.Exp, scale=0.125,
                                   bias=stat(u, 2 + hf), accum_out=stat(u, 4 + hf))
                act.drain().then_inc(sig("exponentials"), 1)

            def copy_turned(u):
                act.wait_ge(sig("probabilities_turned"), b + u + 1)
                if u >= 2:
                    act.wait_ge(sig("attended"), b + u - 1)
                for hf in range(hs):
                    act.activation(turned(kind, u, hf)[:, 0:width(u)], ps[4 + hf][:, 0:width(u)], ACT.Copy)
                act.drain().then_inc(sig("turned_probabilities"), 1)

            def copy_out(u):
                act.wait_ge(sig("attended"), b + u + 1)
                act.activation(out(*units[u]), ps[6 + u % 2][:, 0:P], ACT.Copy).then_inc(sig("attended_out"), 1)

            for u in range(len(units) + 2):
                if u < len(units):
                    exponentials(u)
                if 1 <= u <= len(units):
                    copy_turned(u - 1)
                if u >= 2:
                    copy_out(u - 2)

        def vector_attention(dve, kind, L, book):
            q, k, vv, units, b, out = attention(kind, L, book)

            def maxima(u):
                n = SEG if units[u][1] < 2 else T
                dve.wait_ge(sig("scores"), b + u + 1)
                for hf in range(2):
                    dve.reduce_max(stat(u, hf), ps[2 * (u % 2) + hf][:, 0:n], AXX)
                dve.drain()
                dve.tensor_scalar(stat(u, 2, 2), stat(u, 0, 2), -0.125, None, ALU.mult)\
                   .then_inc(sig("score_maxima"), 1)

            def normalise(u):
                n = SEG if units[u][1] < 2 else T
                dve.wait_ge(sig("exponentials"), b + u + 1)
                dve.reciprocal(stat(u, 6, 2), stat(u, 4, 2))
                dve.drain()
                p0, p1 = prob(kind, u, 0)[:, 0:n], prob(kind, u, 1)[:, 0:n]
                if kind == "df":
                    dve.tensor_scalar(p1, p1, stat(u, 7), small[:, 16:17], ALU.mult, ALU.mult)
                    dve.drain()
                    dve.scalar_tensor_tensor(p0, p0, stat(u, 6), p1, ALU.mult, ALU.subtract)\
                       .then_inc(sig("probabilities"), 1)
                else:
                    dve.tensor_scalar(p0, p0, stat(u, 6), None, ALU.mult)
                    dve.tensor_scalar(p1, p1, stat(u, 7), None, ALU.mult).then_inc(sig("probabilities"), 1)

            for u in range(len(units)):
                maxima(u)
                normalise(u)

        def rope_tiles(L, phase):
            q0 = [t["q"] for t in tiles if t["L"] == L and t["phase"] == phase][0]
            if phase == "df":
                return [(regA[:, j, :], q0 + j, None, scr[:, j % 2, 0:SEG]) for j in range(8)]
            return [(regB[:, j, :], q0 + j, 4 + j + 1, regA[:, j % 2, 0:SEG]) for j in range(6)]

        def tensor_rope(pe, book, todo, normed_before=0):
            b = book.base("rope", len(todo))
            for i, (t, q, normed, work) in enumerate(todo):
                pe.wait_ge(sig("projection_by_scalar"), q + 1)
                if normed is not None:
                    pe.wait_ge(sig("head_normed"), normed_before + normed)
                if i >= 2:
                    pe.wait_ge(sig("roped"), b + i - 1)
                pe.matmul(ps[6 + i % 2][:, 0:SEG], con("rot"), t[:, SEG:T], start=True, stop=True)\
                  .then_inc(sig("rotated"), 1)
                yield

        def vector_rope(dve, book, todo):
            b = book.base("rope", len(todo))
            for i, (t, q, normed, work) in enumerate(todo):
                dve.wait_ge(sig("rotated"), b + i + 1)
                dve.tensor_tensor(work, ps[6 + i % 2][:, 0:SEG], con("sin"), ALU.mult)
                dve.tensor_tensor(t[:, SEG:T], t[:, SEG:T], con("cos"), ALU.mult)
                dve.drain()
                dve.tensor_tensor(t[:, SEG:T], t[:, SEG:T], work, ALU.add).then_inc(sig("roped"), 1)
                yield

        def steps_apart(first, second, lag):
            for i in count():
                done = next(first, "end") == "end"
                if i >= lag:
                    done = next(second, "end") == "end" and done
                if done:
                    return
                yield

        def idle(n):
            for _ in range(n):
                yield

        def vector_lambda(dve, L):
            r = lam4[:, L, :]
            dve.tensor_tensor(small[0:64, 18:20], r[:, 0:4:2], r[:, 1:4:2], ALU.mult)
            dve.drain().then_inc(sig("lambda_products"), 1)
            dve.wait_ge(sig("lambda_exps"), L + 1)
            lam0 = 0.8 - 0.6 * math.exp(-0.3 * L)
            dve.tensor_scalar(small[:, 16:17], small[:, 20:21], small[:, 21:22], None, ALU.subtract)
            dve.drain()
            dve.tensor_scalar(small[:, 16:17], small[:, 16:17], lam0, None, ALU.add)
            dve.tensor_scalar(small[:, 17:18], v(L, "diff_norm"), 1.0 - lam0, None, ALU.mult)
            dve.drain()

        def scalar_lambda(act, L):
            act.wait_ge(sig("lambda_sums"), L + 1)
            act.activation(small[:, 20:22], ps[5][:, 0:2], ACT.Exp).then_inc(sig("lambda_exps"), 1)

        def tensor_lambda(pe, L):
            pe.wait_ge(sig("lambda_products"), L + 1)
            pe.matmul(ps[5][:, 0:2], ones[0:64, :], small[0:64, 18:20], start=True, stop=True)\
              .then_inc(sig("lambda_sums"), 1)

        KRE = lambda n, f: regA[:, 5 * n + f, :]
        KS = lambda n, f: regA[:, 5 * n + 2 + f, :]
        KRB = lambda n: regA[:, 5 * n + 4, :]
        ZT = lambda i: regA[:, 10 + i, :]
        YR = lambda f: Y[:, f, :]
        YS = lambda f: Y[:, 2 + f, :]
        HA = lambda i: scr[0:64, i, 0:SEG]
        dft_c = con("dft_c").rearrange("p (t f) -> p t f", t=2)
        dft_s = con("dft_s").rearrange("p (t f) -> p t f", t=2)
        dft_cb = con("dft_cb").rearrange("p (t f) -> p t f", t=2)
        inv_c = con("inv_c").rearrange("p (f t) -> p f t", f=2)
        inv_s = con("inv_s").rearrange("p (f t) -> p f t", f=2)
        window = con("window").rearrange("p (t c) -> p t c", t=2)

        def tensor_filters(pe, L, book):
            pe.wait_ge(sig("head_rms"), book.n["headnorm"])
            pe.matmul(ps[4][0:64, 0:SEG], w12[0:33, L, 0:64], con("emb")[0:33, :], start=True, stop=True)\
              .then_inc(sig("filter_layer"), 1)
            yield
            pe.wait_ge(sig("filter_sine"), 2 * L + 1)
            pe.matmul(ps[5][0:64, 0:SEG], w12[:, L, 64:128], HA(0), start=True, stop=True)\
              .then_inc(sig("filter_layer"), 1)
            yield
            pe.wait_ge(sig("filter_sine"), 2 * L + 2)
            pe.wait_ge(sig("filter_weights"), 16 * (L + 1))
            for n in range(2):
                if n == 1:
                    pe.wait_ge(sig("filter_root"), 2 * L + 1)
                    pe.wait_ge(sig("filter_spectrum_out"), 4 * L + 2)
                for t in range(2):
                    for d in range(2):
                        last = pe.matmul(ps[4 + 2 * t + d][:, :], HA(1)[:, P * t:P * t + P],
                                         w3[:, 512 * (2 * n + d):512 * (2 * n + d) + 512], start=True, stop=True)
                last.then_inc(sig("filter_taps"), 1)
                yield
                pe.wait_ge(sig("filter_windowed"), 2 * L + n + 1)
                pe.wait_ge(sig("filter_squares"), 2 * L + n + 1)
                for i in range(4):
                    last = pe.matmul(ps[4][:, :], ones, SQ(i), start=(i == 0), stop=(i == 3))
                last.then_inc(sig("filter_energy"), 1)
                yield
                pe.wait_ge(sig("filter_folded"), 2 * L + n + 1)
                for f in range(2):
                    for t in range(2):
                        pe.matmul(ps[5 + f][:, :], dft_c[:, t, P * f:P * f + P], FOLD(0, t), start=(t == 0),
                                  stop=(t == 1))
                for t in range(2):
                    last = pe.matmul(ps[7][:, :], dft_cb[:, t, :], FOLD(0, t), start=(t == 0), stop=(t == 1))
                last.then_inc(sig("filter_spectrum"), 1)
                yield
                pe.wait_ge(sig("filter_spectrum_out"), 4 * L + 2 * n + 1)
                for f in range(2):
                    for t in range(2):
                        last = pe.matmul(ps[5 + f][:, :], dft_s[:, t, P * f:P * f + P], FOLD(1, t), start=(t == 0),
                                         stop=(t == 1))
                last.then_inc(sig("filter_spectrum"), 1)
                yield

        w3 = AR[0:64, B0 + 512 * 12:B0 + 512 * 16]
        SQ = lambda i: Y[:, i, :]
        TAP = lambda d, t: regA[:, 10 + 2 * t + d, :]
        FOLD = lambda part, t: regA[:, 10 + 2 * t + part, :]

        def sine(dve, L, i, bank, bias, freq):
            h = HA(i)
            dve.tensor_scalar(h, bank, bias[0:64, :], freq[0:64, :], ALU.add, ALU.mult)
            dve.drain()
            tmp, r = scr[0:64, 2, 0:SEG], scr[0:64, 3, 0:SEG].bitcast(I32)
            dve.tensor_scalar(tmp, h, 1.0 / (2 * math.pi), None, ALU.mult)
            dve.drain()
            magic = 12582912.0
            dve.tensor_scalar(tmp, tmp, magic, None, ALU.add)
            dve.drain()
            dve.tensor_scalar(tmp, tmp, -magic, None, ALU.add)
            dve.drain()
            hi = 6.28125
            dve.scalar_tensor_tensor(h, tmp, -hi, h, ALU.mult, ALU.add)
            dve.drain()
            dve.scalar_tensor_tensor(h, tmp, -(2 * math.pi - hi), h, ALU.mult, ALU.add)
            dve.drain()
            dve.tensor_scalar(h, h, 3.1415925, -3.1415925, ALU.min, ALU.max)
            dve.drain().then_inc(sig("filter_angle"), 1)

        def vector_filters(dve, L, book):
            dve.wait_ge(sig("filter_layer"), 2 * L + 1)
            sine(dve, L, 0, ps[4][0:64, 0:SEG], v(L, "f_b1"), v(L, "f_freq", 0))
            yield
            dve.wait_ge(sig("filter_layer"), 2 * L + 2)
            sine(dve, L, 1, ps[5][0:64, 0:SEG], v(L, "f_b2"), v(L, "f_freq", 1))
            yield
            for n in range(2):
                dve.wait_ge(sig("filter_taps"), 2 * L + n + 1)
                if n == 1:
                    dve.wait_ge(sig("filter_spectrum"), 4 * L + 2)
                for t in range(2):
                    dve.tensor_tensor(TAP(0, t), ps[4 + 2 * t][:, :], window[:, t, :], ALU.mult)
                    if t == 0:
                        dve.scalar_tensor_tensor(TAP(1, t), ps[4 + 2 * t + 1][:, :], con("not0"), window[:, t, :],
                                                 ALU.mult, ALU.mult)
                    else:
                        dve.tensor_tensor(TAP(1, t), ps[4 + 2 * t + 1][:, :], window[:, t, :], ALU.mult)
                dve.drain().then_inc(sig("filter_windowed"), 1)
                yield
                dve.wait_ge(sig("filter_root"), 2 * L + n + 1)
                for t in range(2):
                    dve.tensor_tensor(scr[:, 3, :], TAP(0, t), TAP(1, t), ALU.add)
                    dve.tensor_tensor(TAP(1, t), TAP(0, t), TAP(1, t), ALU.subtract)
                    dve.drain()
                    dve.tensor_tensor(FOLD(0, t), scr[:, 3, :], scr[:, 2, :], ALU.mult)
                    dve.tensor_tensor(FOLD(1, t), TAP(1, t), scr[:, 2, :], ALU.mult)
                    dve.drain()
                dve.drain().then_inc(sig("filter_folded"), 1)
                yield
                yield
                dve.wait_ge(sig("filter_spectrum_out"), 4 * L + 2 * n + 2)
                dve.tensor_scalar(KS(n, 0), KS(n, 0), con("not0"), None, ALU.mult)
                yield

        def scalar_filters(act, L, book):
            for i in range(2):
                act.wait_ge(sig("filter_angle"), 2 * L + i + 1)
                act.activation(HA(i), HA(i), ACT.Sin).then_inc(sig("filter_sine"), 1)
                yield
            for n in range(2):
                act.wait_ge(sig("filter_windowed"), 2 * L + n + 1)
                if n == 1:
                    act.wait_ge(sig("filter_energy"), 2 * L + 1)
                for i in range(4):
                    act.activation(SQ(i), regA[:, 10 + i, :], ACT.Square)
                act.drain().then_inc(sig("filter_squares"), 1)
                yield
                act.wait_ge(sig("filter_energy"), 2 * L + n + 1)
                act.activation(scr[:, 2, :], ps[4][:, :], ACT.Ln, bias=eps_col[:, :])
                act.drain()
                act.activation(scr[:, 2, :], scr[:, 2, :], ACT.Exp, scale=-0.5)
                act.drain().then_inc(sig("filter_root"), 1)
                yield
                act.wait_ge(sig("filter_spectrum"), 4 * L + 2 * n + 1)
                act.activation(KRE(n, 0), ps[5][:, :], ACT.Copy)
                act.activation(KRE(n, 1), ps[6][:, :], ACT.Copy)
                act.activation(KRB(n), ps[7][:, :], ACT.Copy)
                act.drain().then_inc(sig("filter_spectrum_out"), 1)
                yield
                act.wait_ge(sig("filter_spectrum"), 4 * L + 2 * n + 2)
                act.activation(KS(n, 0), ps[5][:, :], ACT.Copy)
                act.activation(KS(n, 1), ps[6][:, :], ACT.Copy)
                act.drain().then_inc(sig("filter_spectrum_out"), 1)
                yield

        units_hy = lambda L: [(n, s) for n in range(2) for s in range(lo(L) // SEG, 2)]

        def tensor_hyena(pe, L, book):
            units = units_hy(L)
            b = book.base("hyena", len(units))

            def turn(u):
                s = units[u][1]
                for done in range(u):
                    if units[done][1] == s:
                        pe.wait_ge(sig("hyena_gated"), b + done + 1)
                if u >= 1:
                    pe.wait_ge(sig("hyena_turned_out"), b + u)
                for t in range(2):
                    for j in range(4):
                        last = pe.transpose(ps[t][:, P * j:P * j + P],
                                            regB[:, j, SEG * s + P * t:SEG * s + P * t + P], ident)
                last.then_inc(sig("hyena_turned"), 1)

            turn(0)
            for u in range(len(units)):
                pe.wait_ge(sig("hyena_turned_out"), b + u + 1)
                if u >= 1:
                    pe.wait_ge(sig("hyena_product"), 2 * (b + u))
                for f in range(2):
                    for table, bank in ((dft_c, ps[2 + f]), (dft_s, ps[4 + f])):
                        for t in range(2):
                            last = pe.matmul(bank[:, :], table[:, t, P * f:P * f + P], ZT(t), start=(t == 0),
                                             stop=(t == 1))
                    last.then_inc(sig("hyena_spectrum"), 1)
                early = u + 1 < len(units) and units[u + 1][1] != units[u][1]
                if early:
                    turn(u + 1)
                if u >= 1:
                    pe.wait_ge(sig("hyena_gated"), b + u)
                for j in range(4):
                    o = ps[6 + j // 2][:, SEG * (j % 2):SEG * (j % 2) + SEG]
                    if j == 0:
                        pe.wait_ge(sig("hyena_product"), 2 * (b + u) + 2)
                    for f in range(2):
                        pe.matmul(o, YR(f)[:, P * j:P * j + P], inv_c[:, f, :], start=(f == 0), stop=False)
                        last = pe.matmul(o, YS(f)[:, P * j:P * j + P], inv_s[:, f, :], start=False, stop=(f == 1))
                last.then_inc(sig("hyena_conv"), 1)
                if u + 1 < len(units) and not early:
                    turn(u + 1)

        def scalar_hyena(act, L, book):
            b = book.base("hyena", len(units_hy(L)))
            for u in range(len(units_hy(L))):
                act.wait_ge(sig("hyena_turned"), b + u + 1)
                if u >= 1:
                    act.wait_ge(sig("hyena_spectrum"), 2 * (b + u))
                for t in range(2):
                    act.activation(ZT(t), ps[t][:, :], ACT.Copy)
                act.drain().then_inc(sig("hyena_turned_out"), 1)

        def vector_hyena(dve, L, book):
            b = book.base("hyena", len(units_hy(L)))
            for u, (n, s) in enumerate(units_hy(L)):
                for f in range(2):
                    dve.wait_ge(sig("hyena_spectrum"), 2 * (b + u) + f + 1)
                    kb = KRB(n) if f == 0 else KRE(n, 1)
                    dve.tensor_tensor(YR(f), ps[2 + f][:, :], KRE(n, f), ALU.mult)
                    dve.tensor_tensor(YS(f), ps[2 + f][:, :], KS(n, f), ALU.mult)
                    dve.tensor_tensor(scr[:, 2 * f, :], ps[4 + f][:, :], KS(n, f), ALU.mult)
                    dve.tensor_tensor(scr[:, 2 * f + 1, :], ps[4 + f][:, :], kb, ALU.mult)
                    dve.drain()
                    dve.tensor_tensor(YR(f), YR(f), scr[:, 2 * f, :], ALU.subtract)
                    dve.tensor_tensor(YS(f), YS(f), scr[:, 2 * f + 1, :], ALU.add)
                    dve.drain().then_inc(sig("hyena_product"), 1)
                dve.wait_ge(sig("hyena_conv"), b + u + 1)
                sl = slice(SEG * s, SEG * s + SEG)
                for j in range(4):
                    z = regB[:, j, sl]
                    dve.scalar_tensor_tensor(z, z, v(L, "hy_bias", 4 * n + j),
                                             ps[6 + j // 2][:, SEG * (j % 2):SEG * (j % 2) + SEG], ALU.mult, ALU.add)
                dve.drain()
                for j in range(4):
                    z = regB[:, j, sl]
                    dst = z if n == 0 else Y[:, 12 + j, sl]
                    dve.tensor_tensor(dst, z, regB[:, 4 * (n + 1) + j, sl], ALU.mult)
                dve.drain().then_inc(sig("hyena_gated"), 1)

        merged = lambda j: AR[:, A0 + 512 * j:A0 + 512 * j + 512]
        MG_UNITS = [(jj, n, half) for jj in range(4) for n in range(4) for half in range(2)]

        def tensor_merge(pe, L, book):
            b, t0 = book.base("merge", 32), lo(L)
            for i2 in range(16):
                jj, n = i2 // 4, i2 % 4
                mg, mb = merge_m[L][i2]
                for m, width in ((mg, KT), (mb, 4)):
                    arrived(pe, m)
                    for half in range(2):
                        i = 2 * i2 + half
                        if i >= 3:
                            pe.wait_ge(sig("merged"), b + i - 2)
                        bank = ps[i % 3 if m == mg else 3 + i % 3]
                        for k in range(width):
                            rhs = hT[:, k, t0:] if m == mg else Y[:, 4 * n + k, t0:]
                            last = pe.matmul(bank[:, t0:], slot(m, width, 256)[:, k, P * half:P * half + P], rhs,
                                             start=(k == 0), stop=(k == width - 1))
                        last.then_inc(sig("merge_gate" if m == mg else "merge_branch"), 1)
                    pe.drain().then_inc(sig("chunk_used"), 1)
                if L + 1 < DEPTH:
                    tensor_ada_sum(pe, L + 1, ada_of_merge(i2 - 1), ps[6])

        def scalar_merge(act, L, book):
            b, t0 = book.base("merge", 32), lo(L)
            for i in range(32):
                act.wait_ge(sig("merge_gate"), b + i + 1)
                if i >= 3:
                    act.wait_ge(sig("merged"), b + i - 2)
                act.activation(scr[:, i % 3, t0:], ps[i % 3][:, t0:], ACT.Sigmoid).then_inc(sig("merge_sigmoid"), 1)

        def vector_merge(dve, L, book):
            b, t0 = book.base("merge", 32), lo(L)
            for i, (jj, n, half) in enumerate(MG_UNITS):
                dve.wait_ge(sig("merge_sigmoid"), b + i + 1)
                dve.wait_ge(sig("merge_branch"), b + i + 1)
                m, g = merged(2 * jj + half)[:, t0:], scr[:, i % 3, t0:]
                if n == 0:
                    dve.tensor_tensor(m, g, ps[3 + i % 3][:, t0:], ALU.mult)
                else:
                    dve.tensor_tensor(g, g, ps[3 + i % 3][:, t0:], ALU.mult)
                    dve.drain()
                    dve.tensor_tensor(m, m, g, ALU.add)
                dve.drain().then_inc(sig("merged"), 1)
                if half == 1 and L + 1 < DEPTH:
                    vector_ada_weigh(dve, L + 1, ada_of_merge(i // 2))

        def tensor_out(pe, L, book):
            b, t0 = book.base("out", 8), lo(L)
            for j in range(8):
                m = wout_m[L][j // 2]
                arrived(pe, m)
                if j >= 4:
                    pe.wait_ge(sig("residual_added"), b + j - 3)
                for k in range(KT):
                    last = pe.matmul(ps[j % 4][:, t0:], slot(m, KT, 256)[:, k, P * (j % 2):P * (j % 2) + P],
                                     merged(k)[:, t0:], start=(k == 0), stop=(k == KT - 1))
                last.then_inc(sig("out_projected"), 1)
                if j % 2 == 1:
                    pe.drain().then_inc(sig("chunk_used"), 1)

        def vector_out(dve, L, book):
            b = book.base("out", 8)
            for j in range(8):
                dve.wait_ge(sig("out_projected"), b + j + 1)
                for s in range(lo(L) // SEG, 2):
                    x = XT[:, j, SEG * s:SEG * s + SEG]
                    dve.scalar_tensor_tensor(x, ps[j % 4][:, SEG * s:SEG * s + SEG], mods[:, L, 16 + j, s:s + 1], x,
                                             ALU.mult, ALU.add)
                dve.drain().then_inc(sig("residual_added"), 1)

        work = scr[:, :, :].rearrange("p a t -> p (a t)")
        wk = lambda o, *shape: work[:, o:o + int(np.prod(shape))]
        iota32 = con("iota32")

        def tensor_router(pe, L):
            tiles_ = range(lo(L) // P, TT)
            for t in tiles_:
                for k in range(KT):
                    last = pe.matmul(ps[4][:, 36 * t:36 * t + 36], hT[:, k, P * t:P * t + P], rw[:, L, k, :],
                                     start=(k == 0), stop=(k == KT - 1))
            last.then_inc(sig("router_logits"), 1)
            pe.wait_ge(sig("experts_chosen"), L + 1)
            for t in tiles_:
                pe.matmul(ps[5][:, 32 * t:32 * t + 32], con("upper"), both[:, t, :], start=True,
                          stop=(t == tiles_[0]))
                for e in range(tiles_[0], t):
                    pe.matmul(ps[5][:, 32 * t:32 * t + 32], ones, both[:, e, :], start=False, stop=(e == t - 1))
            for t in tiles_:
                last = pe.matmul(ps[6][:, 0:32], ones, both[:, t, :], start=(t == tiles_[0]), stop=(t == TT - 1))
            last.then_inc(sig("experts_counted"), 1)
            pe.wait_ge(sig("places_hot"), L + 1)
            for t in tiles_:
                for c in range(2):
                    last = pe.matmul(ps[7][:, 0:3 * NBT], hot_slot(t, c), hot_blk(t, c),
                                     start=(t == tiles_[0] and c == 0), stop=(t == TT - 1 and c == 1))
            last.then_inc(sig("slot_rows"), 1)

        def scalar_router(act, L):
            act.wait_ge(sig("margins"), L + 1)
            act.activation(wk(0, 20), wk(0, 20), ACT.Exp).then_inc(sig("margin_exps"), 1)

        both = pend
        R0 = 12288 + 8192
        hot_slot = lambda t, c: AR[:, R0 + P * (2 * t + c):R0 + P * (2 * t + c) + P]
        hot_blk = lambda t, c: AR[:, R0 + 1024 + 3 * NBT * (2 * t + c):R0 + 1024 + 3 * NBT * (2 * t + c + 1)]

        def vector_router(dve, L):
            z = lo(L) // P
            n4 = 4 - z

            def rows_of(o, *shape):
                w = wk(o, 4, *shape).rearrange("p (t n) -> p t n", t=4)
                return w[:, z:, :]

            def first_hot(vals, n, m_o, hot):
                mx = rows_of(m_o, 1)
                dve.tensor_reduce(mx, vals, AXX, ALU.max)
                dve.drain()
                eq = rows_of(1900, n)
                dve.tensor_tensor(eq, vals, mx.to_broadcast([P, n4, n]), ALU.is_equal)
                dve.drain()
                dve.scalar_tensor_tensor(eq, eq, -100.0, iota32[:, 0:n].unsqueeze(1).to_broadcast([P, n4, n]),
                                         ALU.mult, ALU.add)
                dve.drain()
                mi = rows_of(1990, 1)
                dve.tensor_reduce(mi, eq, AXX, ALU.min)
                dve.drain()
                dve.tensor_tensor(hot, eq, mi.to_broadcast([P, n4, n]), ALU.is_equal)
                dve.drain()

            dve.wait_ge(sig("router_logits"), L + 1)
            dve.tensor_tensor(rt[:, z:, :], ps[4][:, 36 * z:144].rearrange("p (t n) -> p t n", n=36),
                              rb[:, L, :].unsqueeze(1).to_broadcast([P, n4, 36]), ALU.add)
            dve.drain()
            hg = rows_of(40, 4)
            first_hot(rt[:, z:, 0:4], 4, 32, hg)
            gm = rows_of(0, 4)
            dve.memset(wk(0, 20), 0.0)
            dve.drain()
            dve.tensor_tensor(gm, rt[:, z:, 0:4], rows_of(32, 1).to_broadcast([P, n4, 4]), ALU.subtract)
            dve.drain()
            el = rows_of(64, 32).rearrange("p t (g e) -> p t g e", g=4)
            dve.tensor_tensor(el, rt[:, z:, 4:36].rearrange("p t (g e) -> p t g e", g=4),
                              hg.unsqueeze(3).to_broadcast([P, n4, 4, 8]), ALU.mult)
            dve.drain()
            ein = rows_of(192, 8)
            dve.tensor_reduce(ein, rows_of(64, 32).rearrange("p t (g e) -> p t e g", g=4), AXX, ALU.add)
            dve.drain()
            h1, h2, e2 = rows_of(224, 8), rows_of(256, 8), rows_of(288, 8)
            first_hot(ein, 8, 320, h1)
            dve.tensor_scalar(e2, h1, -2.0e38, 1.0e38, ALU.mult, ALU.add)
            dve.drain()
            dve.tensor_tensor(e2, e2, ein, ALU.min)
            dve.drain()
            first_hot(e2, 8, 324, h2)
            dve.tensor_tensor(rows_of(16, 1), rows_of(324, 1), rows_of(320, 1), ALU.subtract)
            dve.drain().then_inc(sig("margins"), 1)
            for c, h in ((0, h1), (1, h2)):
                for t in range(n4):
                    dve.tensor_tensor(oh[:, z + t, c, :].rearrange("p (g e) -> p g e", g=4),
                                      hg[:, t, :].unsqueeze(2).to_broadcast([P, 4, 8]),
                                      h[:, t, :].unsqueeze(1).to_broadcast([P, 4, 8]), ALU.mult)
            dve.drain()
            dve.tensor_tensor(both[:, z:, :], oh[:, z:, 0, :], oh[:, z:, 1, :], ALU.add)
            dve.drain().then_inc(sig("experts_chosen"), 1)
            dve.wait_ge(sig("margin_exps"), L + 1)
            dve.tensor_reduce(rows_of(328, 1), gm, AXX, ALU.add)
            dve.tensor_scalar(rows_of(332, 1), rows_of(16, 1), 1.0, None, ALU.add)
            dve.drain()
            dve.tensor_tensor(rows_of(328, 1), rows_of(328, 1), rows_of(332, 1), ALU.mult)
            dve.drain()
            dve.reciprocal(gate[:, z:, 0:1], rows_of(328, 1))
            dve.drain()
            dve.tensor_tensor(gate[:, z:, 1:2], gate[:, z:, 0:1], rows_of(16, 1), ALU.mult)
            dve.wait_ge(sig("experts_counted"), L + 1)
            nb, ends, st = wk(372, 32), wk(404, 32), wk(436, 32)
            dve.tensor_scalar(nb, ps[6][:, 0:32], 0.0, None, ALU.is_gt)
            pos, blk = rows_of(500, 32), rows_of(640, 32)
            dve.tensor_copy(pos, ps[5][:, 32 * z:128].rearrange("p (t e) -> p t e", e=32))
            dve.drain()
            dve.tensor_scalar(blk, pos, float(P), None, ALU.is_ge)
            for j in range(1, 4):
                dve.scalar_tensor_tensor(nb, ps[6][:, 0:32], float(P * j), nb, ALU.is_gt, ALU.add)
                dve.drain()
                if j > 1:
                    dve.scalar_tensor_tensor(blk, pos, float(P * j), blk, ALU.is_ge, ALU.add)
                    dve.drain()
            dve.scalar_tensor_tensor(pos, blk, -float(P), pos, ALU.mult, ALU.add)
            dve.tensor_tensor_scan(ends, nb, nb, 0.0, ALU.add, ALU.bypass)
            dve.drain()
            iota_blk = con("iota_blk")
            cmp_ = AR[:, R0 + 2304:R0 + 2304 + NBT * 32].rearrange("p (b e) -> p b e", b=NBT)
            dve.tensor_tensor(cmp_, ends.unsqueeze(1).to_broadcast([P, NBT, 32]),
                              iota_blk.unsqueeze(2).to_broadcast([P, NBT, 32]), ALU.is_le)
            dve.drain()
            tf = wk(1000, NBT + 1)
            pr = wk(1100, NBT)
            dve.tensor_reduce(tf[:, 0:NBT], cmp_, AXX, ALU.add)
            dve.tensor_scalar(pr, iota_blk, 2.0, ends[:, 31:32], ALU.mult, ALU.is_lt)
            dve.drain()
            dve.tensor_scalar(tf[:, 0:NBT], tf[:, 0:NBT], float(E - 1), None, ALU.min)
            dve.tensor_reduce(tf[:, NBT:NBT + 1], pr, AXX, ALU.add)
            dve.drain()
            dve.tensor_copy(tab[:, :], tf)
            dve.drain().then_inc(sig("block_experts"), 1)
            dve.tensor_tensor(st, ends, nb, ALU.subtract)
            dve.drain()
            dve.tensor_tensor(blk, blk, st.unsqueeze(1).to_broadcast([P, n4, 32]), ALU.add)
            dve.drain()
            for i, val in ((0, pos), (1, blk)):
                for c in range(2):
                    w = rows_of(800, 32)
                    dve.tensor_tensor(w, oh[:, z:, c, :], val, ALU.mult)
                    dve.drain()
                    dve.tensor_reduce(place[:, i, z:, c:c + 1], w, AXX, ALU.add)
                    dve.drain()
            n8 = 2 * n4
            sl, bk = (place[:, i, z:, :].rearrange("p t c -> p (t c)").unsqueeze(2) for i in range(2))
            hs = AR[:, R0 + 2 * P * z:R0 + 8 * P].rearrange("p (u n) -> p u n", u=n8)
            hb = AR[:, R0 + 8 * P + 6 * NBT * z:R0 + 8 * P + 24 * NBT].rearrange("p (u n) -> p u n", u=n8)
            tok_id = con("tok_id")[:, 0:n4].unsqueeze(2).unsqueeze(3).to_broadcast([P, n4, 2, NBT])
            row_id = con("row_id")[:, 0:n8].unsqueeze(2).to_broadcast([P, n8, NBT])
            dve.tensor_tensor(hs, con("slots").unsqueeze(1).to_broadcast([P, n8, P]), sl.to_broadcast([P, n8, P]),
                              ALU.is_equal)
            dve.tensor_tensor(hb[:, :, 2 * NBT:], iota_blk.unsqueeze(1).to_broadcast([P, n8, NBT]),
                              bk.to_broadcast([P, n8, NBT]), ALU.is_equal)
            dve.drain()
            dve.tensor_tensor(hb[:, :, NBT:2 * NBT], hb[:, :, 2 * NBT:], row_id, ALU.mult)
            by_tile = hb.rearrange("p (t c) n -> p t c n", c=2)
            dve.tensor_tensor(by_tile[:, :, :, 0:NBT], by_tile[:, :, :, 2 * NBT:], tok_id, ALU.mult)
            dve.drain().then_inc(sig("places_hot"), 1)
            dve.wait_ge(sig("slot_rows"), L + 1)
            far = wk(1200, NBT)
            dve.tensor_scalar(far, ps[7][:, 2 * NBT:3 * NBT], -FAR, FAR, ALU.mult, ALU.add)
            dve.drain()
            for i, idx in ((0, gidx), (1, sidx)):
                r = wk(1300 + 100 * i, NBT)
                dve.tensor_tensor(r, ps[7][:, NBT * i:NBT * i + NBT], far, ALU.add)
                dve.drain()
                dve.tensor_copy(idx[:, :], r)
            dve.drain().then_inc(sig("moe_tables"), 1)

        part = [(0, KT), (4096, KT), (8192, 4)]
        wexp = lambda h, j: AR[:, 12288 * h + part[j][0]:12288 * h + part[j][0] + 4096]\
            .rearrange("p (k n) -> p k n", k=part[j][1])
        act_t = scr[:, 2, :]
        hid_t = scr[:, 3, :]
        xrow = lambda h: Yf[:, 1024 * h:1024 * h + 1024]
        xe = lambda h: Yf[:, 4096 + 1024 * h:5120 + 1024 * h].rearrange("p (k s) -> p k s", k=KT)
        yb = lambda h: Yf[:, 6144 + 1024 * h:7168 + 1024 * h]
        names = ("w_gate", "w_up", "w_down")

        def pairs(e, L, tables="moe_tables"):
            e.wait_ge(sig(tables), L + 1)
            return e.value_load(tab[0:1, NBT:NBT + 1], min_val=1, max_val=MAXBLK // 2)

        def lk(name, L):
            return sig(f"{name}_layer{L}")

        def sync_moe(sp, L):
            n = pairs(sp, L, "block_experts")
            with sp.Fori(0, n) as i:
                for h in range(2):
                    e = sp.value_load(tab[0:1, bass.ds(2 * i + h, 1)], min_val=0, max_val=E - 1)
                    for j, name in enumerate(names):
                        if j < 2:
                            sp.wait_ge(lk("gate_up", L), 4 * i + (2 * h + j + 1))
                        else:
                            sp.wait_ge(lk("down", L), 2 * i + (h + 1))
                        if h == 0 and j == 2:
                            sp.wait_ge(lk("rows_0_loaded", L), 16)
                        src = a["moe_" + name][L][bass.ds(e, 1), :, :]
                        src = src.rearrange("o (k p) n -> p (o k) n", p=P)
                        sp.dma_start(wexp(h, j), src).then_inc(lk(f"{name}_{h}_loaded", L), 16)

        def tensor_moe(pe, L):
            n = pairs(pe, L)

            def turn_rows(n_loaded, h):
                pe.wait_ge(lk(f"rows_{h}_loaded", L), n_loaded)
                for k in range(KT):
                    last = pe.transpose(ps[k // 4][:, P * (k % 4):P * (k % 4) + P], xrow(h)[:, P * k:P * k + P],
                                        ident)
                last.then_inc(lk("rows_turned", L), 1)

            turn_rows(16, 0)
            with pe.Fori(0, n) as i:
                for h in range(2):
                    b = 2 * i + h
                    pe.wait_ge(lk("turned_out", L), b + 1)
                    for j in range(2):
                        pe.wait_ge(lk(f"{names[j]}_{h}_loaded", L), 16 * i + 16)
                        for k in range(KT):
                            last = pe.matmul(ps[2 + j][:, :], xe(h)[:, k, :], wexp(h, j)[:, k, :],
                                             start=(k == 0), stop=(k == KT - 1))
                        last.then_inc(lk("gate_up", L), 1)
                    pe.wait_ge(lk("hidden", L), b + 1)
                    for k in range(4):
                        last = pe.transpose(ps[4][:, P * k:P * k + P], act_t[:, P * k:P * k + P], ident)
                    last.then_inc(lk("hidden_turned", L), 1)
                    turn_rows(16 * i + 16 * (h + 1), 1 - h)
                    pe.wait_ge(lk("hidden_out", L), b + 1)
                    pe.wait_ge(lk("w_down_%d_loaded" % h, L), 16 * i + 16)
                    pe.wait_ge(lk("output_copied", L), 2 * b + 2)
                    for c in range(2):
                        for k in range(4):
                            last = pe.matmul(ps[5 + c][:, :], hid_t[:, P * k:P * k + P],
                                             wexp(h, 2)[:, k, 512 * c:512 * c + 512], start=(k == 0), stop=(k == 3))
                    last.then_inc(lk("down", L), 1)

        def scalar_moe(act, L):
            n = pairs(act, L)
            act.drain().then_inc(lk("output_copied", L), 1)

            def take(b, h):
                act.wait_ge(lk("rows_turned", L), b + 1)
                for c in range(2):
                    act.activation(xe(h)[:, 4 * c:4 * c + 4, :],
                                   ps[c][:, :].rearrange("p (k s) -> p k s", k=4), ACT.Copy)
                act.drain().then_inc(lk("turned_out", L), 1)

            take(0, 0)
            with act.Fori(0, n) as i:
                for h in range(2):
                    b = 2 * i + h
                    act.wait_ge(lk("gate_up", L), 2 * b + 5)
                    act.activation(act_t, ps[2][:, :], ACT.Silu).then_inc(lk("silu", L), 1)
                    act.wait_ge(lk("hidden_turned", L), b + 1)
                    act.activation(hid_t, ps[4][:, :], ACT.Copy).then_inc(lk("hidden_out", L), 1)
                    take(b + 1, 1 - h)
                    act.wait_ge(lk("down", L), b + 3)
                    act.wait_ge(lk(f"output_{h}_written", L), 16 * i + 16)
                    act.activation(yb(h)[:, 0:512], ps[5][:, :], ACT.Copy).then_inc(lk("output_copied", L), 1)

        def vector_moe(dve, L):
            n = pairs(dve, L)
            dve.drain().then_inc(lk("output_copied", L), 1)
            with dve.Fori(0, n) as i:
                for h in range(2):
                    b = 2 * i + h
                    dve.wait_ge(lk("silu", L), b + 1)
                    dve.wait_ge(lk("gate_up", L), 2 * b + 6)
                    dve.tensor_tensor(act_t, act_t, ps[3][:, :], ALU.mult).then_inc(lk("hidden", L), 1)
                    dve.wait_ge(lk("down", L), b + 3)
                    dve.wait_ge(lk(f"output_{h}_written", L), 16 * i + 16)
                    dve.tensor_copy(yb(h)[:, 512:1024], ps[6][:, :]).then_inc(lk("output_copied", L), 1)

        def pool_moe(pool, L):
            pool.wait_ge(sig("rows_in_dram"), 16 * (L + 1))
            pool.sem_inc(sig("pool_steps"), 1)
            for h in range(2):
                pool.dma_start(yb(h)[0:1, :], hrows[L][0:1, :]).then_inc(lk(f"output_{h}_written", L), 16)
            n = pairs(pool, L)
            last_token = pool.to_reg(T - lo(L) - 1)
            last_output = pool.to_reg(2 * (T - lo(L)) - 1)

            def gather(b, h):
                pool.tensor_copy(gi[:, h:h + 1], gidx[:, b])
                pool.drain()
                pool.indirect_dma_start(out=xrow(h), out_offset=None, in_=hrows[L],
                                        in_offset=bass.IndirectOffsetOnAxis(ap=gi[:, h:h + 1], axis=0),
                                        bounds_check=last_token, oob_is_err=False)\
                    .then_inc(lk(f"rows_{h}_loaded", L), 16)

            for b in range(3):
                if b == 2:
                    pool.wait_ge(lk("rows_turned", L), 1)
                gather(slice(b, b + 1), b % 2)
            with pool.Fori(0, n) as i:
                for h in range(2):
                    b = 2 * i + h
                    pool.wait_ge(lk("rows_turned", L), b + 2)
                    pool.sem_inc(sig("pool_steps"), 1)
                    gather(bass.ds(b + 3, 1), 1 - h)
                    pool.wait_ge(lk("output_copied", L), 2 * b + 4)
                    pool.sem_inc(sig("pool_steps"), 1)
                    pool.tensor_copy(si[:, h:h + 1], sidx[:, bass.ds(b, 1)])
                    pool.drain()
                    pool.indirect_dma_start(out=yrows[L],
                                            out_offset=bass.IndirectOffsetOnAxis(ap=si[:, h:h + 1], axis=0),
                                            in_=yb(h), in_offset=None, bounds_check=last_output, oob_is_err=False)\
                        .then_inc(lk(f"output_{h}_written", L), 16)
            for h in range(2):
                pool.wait_ge(lk(f"output_{h}_written", L), 16 * n + 16)
            pool.sem_inc(sig("pool_steps"), 1)
            z = lo(L) // P
            for t in range(z, TT):
                pool.dma_start(rowsA[:, t, :, :],
                               yrows[L][2 * P * (t - z):2 * P * (t - z + 1), :].rearrange("(p c) n -> p c n", c=2))\
                    .then_inc(sig(f"rows_gathered_{t}"), 16)

        def tensor_combine(pe, L, book):
            g0 = 2 * (lo(L) // P)
            b = book.base("combine", 8 - g0) - g0
            for g in range(g0, 8):
                pe.wait_ge(sig("rows_combined"), (b + g) // 2 + 1)
                if g >= g0 + 4:
                    pe.wait_ge(sig("combined_added"), b + g - 3)
                for i in range(4):
                    last = pe.transpose(ps[g % 4][:, P * i:P * i + P], rows_src(rowsB)(g, i), ident)
                last.then_inc(sig("combined_turned"), 1)

        def vector_combine(dve, L, book):
            g0 = 2 * (lo(L) // P)
            b = book.base("combine", 8 - g0) - g0

            def weigh(t):
                dve.wait_ge(sig(f"rows_gathered_{t}"), 16 * sum(lo(l) <= P * t for l in range(L + 1)))
                dve.tensor_scalar(rowsA[:, t, 0, :], rowsA[:, t, 0, :], gate[:, t, 0:1], None, ALU.mult)
                dve.drain()
                dve.scalar_tensor_tensor(rowsB[:, t, :], rowsA[:, t, 1, :], gate[:, t, 1:2], rowsA[:, t, 0, :],
                                         ALU.mult, ALU.add).then_inc(sig("rows_combined"), 1)

            weigh(g0 // 2)
            for g in range(g0, 8):
                t, kg = g // 2, g % 2
                if kg == 0 and t + 1 < TT:
                    weigh(t + 1)
                dve.wait_ge(sig("combined_turned"), b + g + 1)
                for i in range(4):
                    k = 4 * kg + i
                    x = XT[:, k, P * t:P * t + P]
                    dve.scalar_tensor_tensor(x, ps[g % 4][:, P * i:P * i + P], mods[:, L, 40 + k, t // 2:t // 2 + 1],
                                             x, ALU.mult, ALU.add)
                dve.drain().then_inc(sig("combined_added"), 1)

        def load_vectors(eng, L, done):
            n = 0

            def load(dst, src):
                nonlocal n
                eng.dma_start(dst, src).then_inc(sig(done), 16)
                n += 1

            def at(name, i, k):
                o = V1[name] + i
                return (vrow[o:o + k, L, 0, :] if o < N1 else vrow[o - N1:o - N1 + k, L, 1, :])

            fold = lambda x: x.rearrange("(k p) -> k p", p=P)
            row = lambda x: x.rearrange("(o n) -> o n", o=1)
            load(at("b_ada", 0, 48), fold(a["b_ada"][L]))
            load(at("norm1", 0, 8), fold(a["norm1_g"][L]))
            load(at("norm2", 0, 8), fold(a["norm2_g"][L]))
            load(at("ml_conv", 0, 24), a["ml_conv_w"][L].rearrange("j (k p) -> (j k) p", p=P))
            load(at("ml_convb", 0, 8), fold(a["ml_conv_b"][L]))
            load(at("hy_conv", 0, 36), a["hy_conv_w"][L].rearrange("j (k p) -> (j k) p", p=P))
            load(at("hy_convb", 0, 12), fold(a["hy_conv_b"][L]))
            load(at("hy_bias", 0, 8), a["hy_bias"][L].rearrange("j (k p) -> (j k) p", p=P))
            load(at("diff_norm", 0, 1), row(a["diff_norm_g"][L]))
            load(at("ml_norm", 0, 1), row(a["ml_norm_g"][L]))
            for half in range(2):
                load(at("gq_norm", 0, 1)[:, 64 * half:64 * half + 64], row(a["gqa_qnorm_g"][L]))
                load(at("gk_norm", 0, 1)[:, 64 * half:64 * half + 64], row(a["gqa_knorm_g"][L]))
            load(at("f_b1", 0, 1)[:, 0:64], row(a["hy_f_b1"][L]))
            load(at("f_b2", 0, 1)[:, 0:64], row(a["hy_f_b2"][L]))
            load(at("f_freq", 0, 2)[:, 0:64], a["hy_f_freq"][L])
            load(at("final", 0, 8), fold(a["final_norm_g"]))
            for kind in range(2):
                for d in range(2):
                    c0 = MG + 8 * d + 4 * kind
                    load(gw[:, L, :, kind, d, :], a["w_in"][L, :, c0:c0 + 4].rearrange("(k p) n -> p k n", p=P))
                    load(gb[4 * d:4 * d + 4, L, kind:kind + 1],
                         a["ml_gate_b"][L, d, kind, :].rearrange("(h o) -> h o", o=1))
            load(lam4[:, L, :], a["diff_lam"][L].rearrange("j n -> n j"))
            load(w12[0:33, L, 0:64], a["hy_f_w1"][L])
            load(w12[:, L, 64:128], a["hy_f_w2"][L])
            load(rw[:, L, :, 0:4], a["moe_w_group"][L].rearrange("(k p) n -> p k n", p=P))
            load(rw[:, L, :, 4:36], a["moe_w_router"][L].rearrange("(k p) n -> p k n", p=P))
            load(rb[:, L, 0:4], a["moe_b_group"][L].partition_broadcast(P))
            load(rb[:, L, 4:36], a["moe_b_router"][L].partition_broadcast(P))
            return n

        def tensor_vectors(pe, L, bank):
            pe.wait_ge(sig(f"vectors_loaded_{L}"), 16 * n_loads)
            pe.transpose(bank[:, 0:N1], vrow[0:N1, L, 0, :], ident[0:N1, 0:N1])
            pe.transpose(bank[:, 128:128 + N2], vrow[0:N2, L, 1, :], ident[0:N2, 0:N2])\
              .then_inc(sig("vectors_turned"), 1)

        def scalar_vectors(act, L, bank):
            act.wait_ge(sig("vectors_turned"), L + 1)
            act.activation(vecs[:, L, 0:N1], bank[:, 0:N1], ACT.Copy)
            act.activation(vecs[:, L, N1:N1 + N2], bank[:, 128:128 + N2], ACT.Copy)

        @block.sync
        def _(sp):
            sp.dma_start(C[:, 0:EARLY], a["constants"][:, 0:EARLY]).then_inc(sig("early_constants"), 16)

            def stream(lo_, hi):
                for m in range(lo_, hi):
                    fills, at_slot, before = chunks[m]
                    if m in ada_m[1]:
                        sp.wait_ge(sig("attention_left"), 1)
                    if before is not None:
                        sp.wait_ge(sig("chunk_used"), before + 1)
                    for dst, src in fills:
                        sp.dma_start(dst(m), src).then_inc(sig(f"chunk_in_slot_{at_slot}"), 16)

            stream(0, 4)
            sp.dma_start(rowsY[:, 0:2, :], a["ctx"][0].rearrange("(t p) n -> p t n", p=P)).then_inc(sig("inputs"), 16)
            sp.dma_start(rowsY[:, 2:4, :], a["x"][0].rearrange("(t p) n -> p t n", p=P)).then_inc(sig("inputs"), 16)
            stream(4, 12)
            sp.dma_start(C[:, EARLY:], a["constants"][:, EARLY:]).then_inc(sig("constants"), 16)
            at = 12
            for L in range(DEPTH):
                stream(at, layer_end_chunk[L] + 1)
                at = layer_end_chunk[L] + 1
                sp.wait_ge(sig("chunk_used"), at)
                sync_moe(sp, L)
                if L + 1 < DEPTH:
                    sp.wait_ge(sig("tensor_left_experts"), L + 1)
            sp.wait_ge(sig("final_rows"), 1)
            sp.dma_start(out[0].rearrange("(t p) n -> p t n", p=P), rowsY[:, 2:4, :]).then_inc(sig("written"), 16)
            sp.wait_ge(sig("written"), 16)

        n_loads = 33

        @block.gpsimd
        def _(pool):
            pool.memset(vrow[:, :, :, :], 0.0)
            pool.memset(eps_col[:, :], EPS)
            pool.drain().then_inc(sig("rows_cleared"), 1)
            pool.wait_ge(sig("rows_cleared"), 1)
            for L in range(DEPTH):
                assert load_vectors(pool, L, f"vectors_loaded_{L}") == n_loads
            for L in range(DEPTH):
                pool.wait_ge(sig("mlstm_left"), L + 1)
                pool.sem_inc(sig("pool_steps"), 1)
                pool.dma_start(w3, a["hy_f_w3"][L]).then_inc(sig("filter_weights"), 16)
                pool_moe(pool, L)

        hidden_src = lambda g, i: hT[:, 4 * (g % 2) + i, P * (g // 2):P * (g // 2) + P]

        @block.tensor
        def _(pe):
            book, me = Book(), "tensor"
            pe.wait_ge(sig("early_constants"), 16)
            pe.wait_ge(sig("conditioning"), 32)
            pe.transpose(ps[4][:, 0:16], crow[:, :], ident[0:16, 0:16]).then_inc(sig("conditioning_turned"), 1)
            pe.wait_ge(sig("conditioned"), 1)
            tensor_ada(pe, range(4), ps[5])
            pe.wait_ge(sig("inputs"), 32)
            tensor_turn(pe, book, rows_src(rowsY))
            tensor_ada(pe, range(4, 24), ps[5])
            tensor_vectors(pe, 0, ps[6])
            pe.wait_ge(sig("constants"), 16)
            meet(pe, me, book)
            for L in range(DEPTH):
                t0 = lo(L)
                tensor_rms(pe, book)
                tensor_project(pe, L, "ml", chain(idle(8), tensor_gates(pe, L)))
                tensor_gate_columns(pe, L)
                meet(pe, me, book)
                tensor_mlstm(pe, L, book)
                meet(pe, me, book)
                pe.drain().then_inc(sig("mlstm_left"), 1)
                tensor_project(pe, L, "hy", chain(tensor_headnorm(pe, book, head_tiles(L, "hy"), HY_SUMS),
                                                  tensor_filters(pe, L, book)))
                meet(pe, me, book)
                tensor_hyena(pe, L, book)
                meet(pe, me, book)
                tensor_project(pe, L, "df", chain(idle(1), tensor_rope(pe, book, rope_tiles(L, "df"))))
                tensor_lambda(pe, L)
                meet(pe, me, book)
                tensor_attention(pe, "df", L, book)
                meet(pe, me, book)
                heads = head_tiles(L, "gq")
                normed = book.n["headnorm"]
                tensor_project(pe, L, "gq", steps_apart(tensor_headnorm(pe, book, heads, GQ_SUMS),
                                                        tensor_rope(pe, book, rope_tiles(L, "gq"), normed), 5))
                meet(pe, me, book)
                tensor_attention(pe, "gq", L, book)
                pe.drain().then_inc(sig("attention_left"), 1)
                meet(pe, me, book)
                if L + 1 < DEPTH:
                    tensor_vectors(pe, L + 1, ps[7])
                tensor_merge(pe, L, book)
                meet(pe, me, book)
                tensor_out(pe, L, book)
                tensor_rms(pe, book, t0)
                hidden_tile(pe, L, 1)
                tensor_turn(pe, book, hidden_src, 2 * (t0 // P))
                pe.drain().then_inc(lk("gate_up", L), 4)
                pe.drain().then_inc(lk("down", L), 2)
                tensor_router(pe, L)
                meet(pe, me, book)
                tensor_moe(pe, L)
                pe.drain().then_inc(sig("tensor_left_experts"), 1)
                meet(pe, me, book)
                tensor_combine(pe, L, book)
                meet(pe, me, book)
            tensor_rms(pe, book, SEG)
            hidden_tile(pe, DEPTH, 0)
            tensor_turn(pe, book, hidden_src, 4)

        @block.scalar
        def _(act):
            book, me = Book(), "scalar"
            act.dma_start(crow[0:8, :], a["c_ctx"].rearrange("(k p) -> k p", p=P)).then_inc(sig("conditioning"), 16)
            act.dma_start(crow[8:16, :], a["c"][0].rearrange("(k p) -> k p", p=P)).then_inc(sig("conditioning"), 16)
            act.wait_ge(sig("conditioning_turned"), 1)
            act.activation(sc[:, :], ps[4][:, 0:16], ACT.Silu).then_inc(sig("conditioned"), 1)
            scalar_ada(act, range(4))
            scalar_turn(act, book, xt_dst)
            scalar_ada(act, range(4, 24))
            scalar_vectors(act, 0, ps[6])
            meet(act, me, book)
            for L in range(DEPTH):
                t0 = lo(L)
                scalar_rms(act, book, L, 0)
                scalar_project(act, L, "ml", chain(idle(8), scalar_gates(act, L)))
                meet(act, me, book)
                scalar_activate(act, [regA[:, j, t0 if j < 4 else 0:] for j in range(8)], ACT.Silu)
                act.drain().then_inc(sig("mlstm_qk"), 1)
                scalar_activate(act, [regA[:, 12 + j, t0:] for j in range(4)], ACT.Sigmoid)
                scalar_mlstm(act, L, book)
                meet(act, me, book)
                scalar_project(act, L, "hy", chain(scalar_headnorm(act, book, head_tiles(L, "hy"), HY_SUMS),
                                                   scalar_filters(act, L, book)))
                meet(act, me, book)
                scalar_hyena(act, L, book)
                meet(act, me, book)
                scalar_project(act, L, "df")
                scalar_lambda(act, L)
                meet(act, me, book)
                scalar_attention(act, "df", L, book)
                meet(act, me, book)
                scalar_project(act, L, "gq", scalar_headnorm(act, book, head_tiles(L, "gq"), GQ_SUMS))
                meet(act, me, book)
                scalar_attention(act, "gq", L, book)
                meet(act, me, book)
                if L + 1 < DEPTH:
                    scalar_vectors(act, L + 1, ps[7])
                scalar_merge(act, L, book)
                meet(act, me, book)
                scalar_rms(act, book, L, 1, t0)
                scalar_turn(act, book, rows_dst(rowsY), 2 * (t0 // P))
                act.drain()
                act.wait_ge(sig("vector_took_turned"), book.n["turned_out"])
                z = t0 // P
                act.dma_start(hrows[L].rearrange("(t p) n -> p t n", p=P), rowsY[:, z:, :])\
                   .then_inc(sig("rows_in_dram"), 16)
                scalar_router(act, L)
                meet(act, me, book)
                scalar_moe(act, L)
                meet(act, me, book)
                meet(act, me, book)
            scalar_rms(act, book, 0, 2, SEG)
            scalar_turn(act, book, rows_dst(rowsY), 4)
            act.drain().then_inc(sig("final_half"), 1)

        @block.vector
        def _(dve):
            book, me = Book(), "vector"
            vector_turn(dve, book, xt_dst)
            meet(dve, me, book)
            vector_ada(dve, 0, ps[5])
            for L in range(DEPTH):
                t0 = lo(L)
                vector_rms(dve, book, L, 0)
                vector_project(dve, L, "ml", chain(idle(8), vector_gates(dve, L)))
                vector_gate_columns(dve, L)
                meet(dve, me, book)
                vector_mlstm(dve, L, book)
                meet(dve, me, book)
                vector_project(dve, L, "hy", chain(started(vector_headnorm(dve, book, head_tiles(L, "hy"), HY_SUMS)),
                                                   vector_filters(dve, L, book)))
                meet(dve, me, book)
                vector_hyena(dve, L, book)
                meet(dve, me, book)
                vector_project(dve, L, "df", chain(idle(1), vector_rope(dve, book, rope_tiles(L, "df"))))
                vector_lambda(dve, L)
                meet(dve, me, book)
                vector_attention(dve, "df", L, book)
                meet(dve, me, book)
                vector_project(dve, L, "gq", steps_apart(started(vector_headnorm(dve, book, head_tiles(L, "gq"), GQ_SUMS)),
                                                         vector_rope(dve, book, rope_tiles(L, "gq")), 5))
                meet(dve, me, book)
                vector_attention(dve, "gq", L, book)
                meet(dve, me, book)
                vector_merge(dve, L, book)
                meet(dve, me, book)
                if L + 1 < DEPTH:
                    vector_ada(dve, L + 1, ps[6])
                vector_out(dve, L, book)
                vector_rms(dve, book, L, 1, t0)
                vector_turn(dve, book, rows_dst(rowsY), 2 * (t0 // P))
                vector_router(dve, L)
                meet(dve, me, book)
                vector_moe(dve, L)
                meet(dve, me, book)
                vector_combine(dve, L, book)
                meet(dve, me, book)
            vector_rms(dve, book, 0, 2, SEG)
            vector_turn(dve, book, rows_dst(rowsY), 4)
            dve.wait_ge(sig("final_half"), 1)
            dve.drain().then_inc(sig("final_rows"), 1)


_INS = ["x", "c", "ctx", "c_ctx", "w_ada", "b_ada", "norm1_g", "norm2_g", "w_in", "diff_lam", "diff_norm_g",
        "ml_conv_w", "ml_conv_b", "ml_gate_b", "ml_norm_g", "gqa_qnorm_g", "gqa_knorm_g",
        "hy_conv_w", "hy_conv_b", "hy_f_w1", "hy_f_b1", "hy_f_w2", "hy_f_b2", "hy_f_w3", "hy_f_freq", "hy_bias",
        "w_branch", "w_out", "moe_w_group", "moe_b_group", "moe_w_router", "moe_b_router",
        "moe_w_gate", "moe_w_up", "moe_w_down", "final_norm_g"]


def kernel(**inputs):
    import numpy as _np
    import concourse.bacc as _bacc
    from concourse import mybir as _mybir
    from concourse.bass_utils import run_bass_kernel_spmd as _run

    nc = _bacc.Bacc("TRN2", target_bir_lowering=False, num_devices=1)
    consts, ccols = shape_constants()
    arrays, args = {"constants_dram": consts}, {}
    for name in _INS:
        x = _np.ascontiguousarray(inputs[name])
        arrays[f"in_{name}_dram"] = x
        args[name] = nc.dram_tensor(f"in_{name}_dram", x.shape, _mybir.dt.from_np(x.dtype), kind="ExternalInput").ap()
    args["constants"] = nc.dram_tensor("constants_dram", consts.shape, _mybir.dt.from_np(consts.dtype),
                                       kind="ExternalInput").ap()
    shape = tuple(inputs["x"].shape)
    out = nc.dram_tensor("out_0_dram", shape, _mybir.dt.float32, kind="ExternalOutput").ap()
    backbone(nc, args, consts, ccols, out)
    r = _run(nc, [arrays], core_ids=[0])
    return r.results[0]["out_0_dram"]
```
